# Optimizing a Trainium2 kernel written in Bass

```python
import math, functools
import jax, jax.numpy as jnp
from jax import lax
import numpy as np
import math

D_MODEL = 1024
BATCH = 1
SEQ = 256
DEPTH = 2

D_FF = ((8 * D_MODEL // 3 + 127) // 128) * 128
FFN_HALF = 0.5
N_SUB = 3

ML_HEADS = 4
ML_QK = D_MODEL // 2
ML_V = D_MODEL
ML_DK = ML_QK // ML_HEADS
ML_DV = ML_V // ML_HEADS
ML_CHUNK = 64
ML_IN = 2 * ML_QK + 2 * ML_V + 2 * ML_HEADS

MB_EXPAND = 2
MB_DI = MB_EXPAND * D_MODEL
MB_HEADDIM = 64
MB_HEADS = MB_DI // MB_HEADDIM
MB_GROUPS = 4
MB_HPG = MB_HEADS // MB_GROUPS
MB_STATE = 128
MB_CONV = 4
MB_CHUNK = 128
MB_CONV_DIM = MB_DI + 2 * MB_GROUPS * MB_STATE
MB_IN = 2 * MB_DI + 2 * MB_GROUPS * MB_STATE + MB_HEADS

N_MLSTM_LAYERS = (DEPTH + 1) // 2
N_MAMBA_LAYERS = DEPTH // 2
EPS = 1e-6


def rms_norm(x, g):
    xf = x.astype(jnp.float32)
    y = xf * lax.rsqrt(jnp.mean(xf * xf, axis=-1, keepdims=True) + EPS)
    return (y * g.astype(jnp.float32)).astype(x.dtype)

def _to_chunks(t, L):
    B, S = t.shape[:2]
    return jnp.moveaxis(t.reshape(B, S // L, L, *t.shape[2:]), 1, 0)

def _mlstm_chunk(carry, xs):
    C, n, m = carry
    q, k, v, ig, lf = xs
    L = q.shape[2]
    causal = jnp.tril(jnp.ones((L, L), dtype=bool))
    b = jnp.cumsum(lf, axis=-1)
    log_d = jnp.where(causal, b[..., :, None] - b[..., None, :] + ig[..., None, :], -jnp.inf)
    m_inter = b + m[..., None]
    m_t = jnp.maximum(jnp.max(log_d, axis=-1), m_inter)
    s = jnp.einsum('bhtd,bhsd->bhts', q, k) * jnp.exp(log_d - m_t[..., None])
    inter = jnp.exp(m_inter - m_t)
    num = jnp.einsum('bhts,bhsv->bhtv', s, v) + inter[..., None] * jnp.einsum('bhtd,bhdv->bhtv', q, C)
    den = jnp.sum(s, axis=-1) + inter * jnp.einsum('bhtd,bhd->bht', q, n)
    h = num / jnp.maximum(jnp.abs(den), jnp.exp(-m_t))[..., None]
    b_last = b[..., -1]
    log_w = b_last[..., None] - b + ig
    m_new = jnp.maximum(b_last + m, jnp.max(log_w, axis=-1))
    w = jnp.exp(log_w - m_new[..., None])
    decay = jnp.exp(b_last + m - m_new)
    C_new = decay[..., None, None] * C + jnp.einsum('bhs,bhsd,bhsv->bhdv', w, k, v)
    n_new = decay[..., None] * n + jnp.einsum('bhs,bhsd->bhd', w, k)
    return (C_new, n_new, m_new), h

def mlstm_mixer(h, w_in, b_gate, norm_w, w_out):
    B, S, _ = h.shape
    proj = h @ w_in
    q, k, v, o, gates = jnp.split(proj, [ML_QK, 2 * ML_QK, 2 * ML_QK + ML_V, 2 * ML_QK + 2 * ML_V], axis=-1)
    f32 = jnp.float32
    q = q.reshape(B, S, ML_HEADS, ML_DK).astype(f32)
    k = k.reshape(B, S, ML_HEADS, ML_DK).astype(f32) * (ML_DK ** -0.5)
    v = v.reshape(B, S, ML_HEADS, ML_DV).astype(f32)
    gates = gates.astype(f32) + b_gate.astype(f32)
    ig, fg = jnp.split(gates, 2, axis=-1)
    lf = jax.nn.log_sigmoid(fg)
    xs = tuple(jnp.swapaxes(_to_chunks(t, ML_CHUNK), 2, 3) for t in (q, k, v, ig, lf))
    carry0 = (jnp.zeros((B, ML_HEADS, ML_DK, ML_DV), f32),
              jnp.zeros((B, ML_HEADS, ML_DK), f32),
              jnp.zeros((B, ML_HEADS), f32))
    _, hs = lax.scan(_mlstm_chunk, carry0, xs)
    hs = jnp.moveaxis(jnp.swapaxes(hs, 2, 3), 0, 1).reshape(B, S, ML_HEADS, ML_DV)
    hs = hs * lax.rsqrt(jnp.mean(hs * hs, axis=-1, keepdims=True) + EPS)
    hs = hs.reshape(B, S, ML_V) * norm_w.astype(f32) * jax.nn.sigmoid(o.astype(f32))
    return hs.astype(h.dtype) @ w_out

def _ssd_chunk(state, xs, A):
    x, dt, Bc, Cc = xs
    Q = x.shape[1]
    causal = jnp.tril(jnp.ones((Q, Q), dtype=bool))
    a = jnp.cumsum(dt * A, axis=1)
    seg = jnp.where(causal[None, :, :, None, None], a[:, :, None] - a[:, None, :], -jnp.inf)
    w = jnp.einsum('btgn,bsgn->btsg', Cc, Bc)[..., None] * jnp.exp(seg) * dt[:, None]
    y = (jnp.einsum('btsgh,bsghp->btghp', w, x)
         + jnp.exp(a)[..., None] * jnp.einsum('btgn,bghpn->btghp', Cc, state))
    a_last = a[:, -1]
    ws = jnp.exp(a_last[:, None] - a) * dt
    state_new = (jnp.exp(a_last)[..., None, None] * state
                 + jnp.einsum('bsgn,bsgh,bsghp->bghpn', Bc, ws, x))
    return state_new, y

def mamba2_mixer(h, w_in, conv_w, conv_b, dt_bias, A_log, D_skip, norm_w, w_out):
    B, S, _ = h.shape
    f32 = jnp.float32
    proj = h @ w_in
    z, xbc, dt = jnp.split(proj, [MB_DI, MB_DI + MB_CONV_DIM], axis=-1)
    xbc = lax.conv_general_dilated(xbc, conv_w[:, None, :].astype(xbc.dtype), window_strides=(1,),
                                   padding=[(MB_CONV - 1, 0)], dimension_numbers=('NWC', 'WIO', 'NWC'),
                                   feature_group_count=MB_CONV_DIM)
    xbc = jax.nn.silu((xbc + conv_b).astype(f32))
    xs, Bm, Cm = jnp.split(xbc, [MB_DI, MB_DI + MB_GROUPS * MB_STATE], axis=-1)
    xs = xs.reshape(B, S, MB_GROUPS, MB_HPG, MB_HEADDIM)
    Bm = Bm.reshape(B, S, MB_GROUPS, MB_STATE)
    Cm = Cm.reshape(B, S, MB_GROUPS, MB_STATE)
    dt = jax.nn.softplus(dt.astype(f32) + dt_bias.astype(f32)).reshape(B, S, MB_GROUPS, MB_HPG)
    A = -jnp.exp(A_log.astype(f32)).reshape(MB_GROUPS, MB_HPG)
    chunks = tuple(_to_chunks(t, MB_CHUNK) for t in (xs, dt, Bm, Cm))
    state0 = jnp.zeros((B, MB_GROUPS, MB_HPG, MB_HEADDIM, MB_STATE), f32)
    _, ys = lax.scan(functools.partial(_ssd_chunk, A=A), state0, chunks)
    y = jnp.moveaxis(ys, 0, 1).reshape(B, S, MB_GROUPS, MB_HPG, MB_HEADDIM)
    y = y + D_skip.astype(f32).reshape(MB_GROUPS, MB_HPG)[..., None] * xs
    y = y.reshape(B, S, MB_DI) * jax.nn.silu(z.astype(f32))
    y = y.reshape(B, S, MB_GROUPS, MB_DI // MB_GROUPS)
    y = y * lax.rsqrt(jnp.mean(y * y, axis=-1, keepdims=True) + EPS)
    y = y.reshape(B, S, MB_DI) * norm_w.astype(f32)
    return y.astype(h.dtype) @ w_out

def swiglu(h, w1, w3, w2):
    return (jax.nn.silu(h @ w1) * (h @ w3)) @ w2

def sublayer(x, fn, g_pre, g_post, shift, scale, gate, weight):
    hmod = rms_norm(x, g_pre) * (1 + scale[:, None, :]) + shift[:, None, :]
    y = rms_norm(fn(hmod), g_post)
    return x + weight * gate[:, None, :] * y

def first_inputs(seed: int = 0) -> dict:
    key = jax.random.key(seed)
    ks = jax.random.split(key, 24)
    D = D_MODEL
    nrm = lambda k, shape, fan_in: jax.random.normal(k, shape, jnp.float32) * (fan_in ** -0.5)
    u_dt = jax.random.uniform(ks[17], (N_MAMBA_LAYERS, MB_HEADS), jnp.float32)
    dt0 = jnp.exp(u_dt * (math.log(0.1) - math.log(1e-3)) + math.log(1e-3))
    ig_b = 0.5 * jax.random.normal(ks[12], (N_MLSTM_LAYERS, ML_HEADS), jnp.float32)
    fg_b = 3.0 + 3.0 * jax.random.uniform(ks[13], (N_MLSTM_LAYERS, ML_HEADS), jnp.float32)
    return {
        "x": jax.random.normal(ks[0], (BATCH, SEQ, D), jnp.float32),
        "c": jax.random.normal(ks[1], (BATCH, D), jnp.float32),
        "ada_w": 0.5 * nrm(ks[2], (DEPTH, D, 3 * N_SUB * D), D),
        "ada_b": 0.02 * jax.random.normal(ks[3], (DEPTH, 3 * N_SUB * D), jnp.float32),
        "norm_pre": 1.0 + 0.1 * jax.random.normal(ks[4], (DEPTH, N_SUB, D), jnp.float32),
        "norm_post": 1.0 + 0.1 * jax.random.normal(ks[5], (DEPTH, N_SUB, D), jnp.float32),
        "ffn_w1": nrm(ks[6], (DEPTH, 2, D, D_FF), D),
        "ffn_w3": nrm(ks[7], (DEPTH, 2, D, D_FF), D),
        "ffn_w2": nrm(ks[8], (DEPTH, 2, D_FF, D), D_FF),
        "ml_w_in": nrm(ks[9], (N_MLSTM_LAYERS, D, ML_IN), D),
        "ml_b_gate": jnp.concatenate([ig_b, fg_b], axis=-1),
        "ml_norm_w": 1.0 + 0.1 * jax.random.normal(ks[10], (N_MLSTM_LAYERS, ML_V), jnp.float32),
        "ml_w_out": nrm(ks[11], (N_MLSTM_LAYERS, ML_V, D), ML_V),
        "mb_w_in": nrm(ks[14], (N_MAMBA_LAYERS, D, MB_IN), D),
        "mb_conv_w": nrm(ks[15], (N_MAMBA_LAYERS, MB_CONV, MB_CONV_DIM), MB_CONV),
        "mb_conv_b": 0.02 * jax.random.normal(ks[16], (N_MAMBA_LAYERS, MB_CONV_DIM), jnp.float32),
        "mb_dt_bias": dt0 + jnp.log(-jnp.expm1(-dt0)),
        "mb_A_log": jnp.log(jax.random.uniform(ks[18], (N_MAMBA_LAYERS, MB_HEADS), jnp.float32, 1.0, 16.0)),
        "mb_D": 1.0 + 0.1 * jax.random.normal(ks[19], (N_MAMBA_LAYERS, MB_HEADS), jnp.float32),
        "mb_norm_w": 1.0 + 0.1 * jax.random.normal(ks[20], (N_MAMBA_LAYERS, MB_DI), jnp.float32),
        "mb_w_out": nrm(ks[21], (N_MAMBA_LAYERS, MB_DI, D), MB_DI),
    }

def first_block(x, c, ada_w, ada_b, norm_pre, norm_post, ffn_w1, ffn_w3, ffn_w2,
              ml_w_in, ml_b_gate, ml_norm_w, ml_w_out,
              mb_w_in, mb_conv_w, mb_conv_b, mb_dt_bias, mb_A_log, mb_D, mb_norm_w, mb_w_out):
    B = x.shape[0]
    c_act = jax.nn.silu(c)
    for i in range(DEPTH):
        mod = (c_act @ ada_w[i] + ada_b[i]).reshape(B, N_SUB, 3, D_MODEL)
        j = i // 2
        if i % 2 == 0:
            mixer = lambda h, j=j: mlstm_mixer(h, ml_w_in[j], ml_b_gate[j], ml_norm_w[j], ml_w_out[j])
        else:
            mixer = lambda h, j=j: mamba2_mixer(h, mb_w_in[j], mb_conv_w[j], mb_conv_b[j], mb_dt_bias[j],
                                                mb_A_log[j], mb_D[j], mb_norm_w[j], mb_w_out[j])
        fns = (lambda h, i=i: swiglu(h, ffn_w1[i, 0], ffn_w3[i, 0], ffn_w2[i, 0]),
               mixer,
               lambda h, i=i: swiglu(h, ffn_w1[i, 1], ffn_w3[i, 1], ffn_w2[i, 1]))
        weights = (FFN_HALF, 1.0, FFN_HALF)
        for s in range(N_SUB):
            x = sublayer(x, fns[s], norm_pre[i, s], norm_post[i, s],
                         mod[:, s, 0], mod[:, s, 1], mod[:, s, 2], weights[s])
    return x


DEPTH_2 = 1

N_HEADS = 8
HEAD_DIM = 128
ATTN_WIDTH = N_HEADS * HEAD_DIM
CONV_WIDTH = 1024
CONV_K = 3
MOBA_BLOCK = 256
MOBA_TOPK = 3
Q_CHUNK = 8
N_BUCKETS = 32
MAX_DISTANCE = 128
IN_WIDTHS = (ATTN_WIDTH, ATTN_WIDTH, ATTN_WIDTH, ATTN_WIDTH,
             CONV_WIDTH, CONV_WIDTH, CONV_WIDTH, CONV_WIDTH,
             D_MODEL, D_MODEL)
IN_COLS = sum(IN_WIDTHS)
IN_OFFSETS = tuple(int(o) for o in np.cumsum(IN_WIDTHS)[:-1])


def rmsnorm(x, g):
    x32 = x.astype(jnp.float32)
    y = x32 * lax.rsqrt(jnp.mean(x32 * x32, axis=-1, keepdims=True) + EPS)
    return (y * g.astype(jnp.float32)).astype(x.dtype)

def t5_bucket(dist):
    n = jnp.maximum(dist, 0)
    max_exact = N_BUCKETS // 2
    nf = jnp.maximum(n, 1).astype(jnp.float32)
    large = max_exact + (jnp.log(nf / max_exact) / math.log(MAX_DISTANCE / max_exact)
                         * (N_BUCKETS - max_exact)).astype(jnp.int32)
    large = jnp.minimum(large, N_BUCKETS - 1)
    return jnp.where(n < max_exact, n, large)

def moba_attention(q, k, v, rel_bias):
    bsz, n_h, seq, hd = q.shape
    s_pad = -(-seq // MOBA_BLOCK) * MOBA_BLOCK
    padw = ((0, 0), (0, 0), (0, s_pad - seq), (0, 0))
    q32 = jnp.pad(q.astype(jnp.float32), padw) * (hd ** -0.5)
    nb = s_pad // MOBA_BLOCK
    kb = jnp.pad(k.astype(jnp.float32), padw).reshape(bsz, n_h, nb, MOBA_BLOCK, hd)
    vb = jnp.pad(v.astype(jnp.float32), padw).reshape(bsz, n_h, nb, MOBA_BLOCK, hd)
    bias_hb = rel_bias.astype(jnp.float32).T
    n_sel = min(MOBA_TOPK, nb - 1)
    n_chunks = s_pad // Q_CHUNK
    q_ch = q32.reshape(bsz, n_h, n_chunks, Q_CHUNK, hd).transpose(2, 0, 1, 3, 4)
    starts = jnp.arange(n_chunks, dtype=jnp.int32) * Q_CHUNK

    if n_sel > 0:
        k_mean = kb.mean(axis=3)
        scores = jnp.einsum('bhsd,bhnd->bhsn', q32, k_mean)
        q_blk = jnp.arange(s_pad) // MOBA_BLOCK
        fully_past = jnp.arange(nb)[None, :] < q_blk[:, None]
        scores = jnp.where(fully_past, scores, -jnp.inf)
        _, sel = lax.top_k(scores, n_sel)
        sel = sel.astype(jnp.int32)
    else:
        sel = jnp.zeros((bsz, n_h, s_pad, 0), jnp.int32)
    sel_ch = sel.reshape(bsz, n_h, n_chunks, Q_CHUNK, n_sel).transpose(2, 0, 1, 3, 4)

    b_idx = jnp.arange(bsz)[:, None, None, None]
    h_idx = jnp.arange(n_h)[None, :, None, None]
    offs = jnp.arange(MOBA_BLOCK, dtype=jnp.int32)

    def chunk(args):
        qc, selc, c0 = args
        qpos = c0 + jnp.arange(Q_CHUNK, dtype=jnp.int32)
        own = c0 // MOBA_BLOCK
        k_own = kb[:, :, own]
        v_own = vb[:, :, own]
        dist_own = qpos[:, None] - (own * MOBA_BLOCK + offs)[None, :]
        lg_own = jnp.einsum('bhqd,bhkd->bhqk', qc, k_own) + bias_hb[:, t5_bucket(dist_own)]
        lg_own = jnp.where(dist_own >= 0, lg_own, -jnp.inf)
        k_sel = kb[b_idx, h_idx, selc]
        v_sel = vb[b_idx, h_idx, selc]
        dist_sel = qpos[:, None, None] - (selc[..., None] * MOBA_BLOCK + offs)
        lg_sel = (jnp.einsum('bhqd,bhqnkd->bhqnk', qc, k_sel)
                  + bias_hb[h_idx[..., None], t5_bucket(dist_sel)])
        lg_sel = jnp.where((selc < own)[..., None], lg_sel, -jnp.inf)
        logits = jnp.concatenate(
            [lg_sel.reshape(bsz, n_h, Q_CHUNK, n_sel * MOBA_BLOCK), lg_own], axis=-1)
        p = jax.nn.softmax(logits, axis=-1)
        p_sel = p[..., :n_sel * MOBA_BLOCK].reshape(bsz, n_h, Q_CHUNK, n_sel, MOBA_BLOCK)
        p_own = p[..., n_sel * MOBA_BLOCK:]
        return (jnp.einsum('bhqnk,bhqnkd->bhqd', p_sel, v_sel)
                + jnp.einsum('bhqk,bhkd->bhqd', p_own, v_own))

    out = lax.map(chunk, (q_ch, sel_ch, starts))
    out = out.transpose(1, 2, 0, 3, 4).reshape(bsz, n_h, s_pad, hd)[:, :, :seq]
    return out.astype(q.dtype)

def short_conv(cb, cc, cx, conv_w):
    u = cc * cx
    y = lax.conv_general_dilated(
        u, conv_w[:, None, :].astype(u.dtype), window_strides=(1,),
        padding=[(CONV_K - 1, 0)], dimension_numbers=('NWC', 'WIO', 'NWC'),
        feature_group_count=CONV_WIDTH)
    return cb * y

def split_heads(t):
    b, s, _ = t.shape
    return t.reshape(b, s, N_HEADS, HEAD_DIM).transpose(0, 2, 1, 3)

def hybrid_layer(x, c, norm_g, w_ada, b_ada, w_in, conv_w, w_o_attn, w_o_conv, w_out, rel_bias):
    bsz, seq, _ = x.shape
    mod = jax.nn.silu(c) @ w_ada + b_ada
    shift, scale, gate = jnp.split(mod, 3, axis=-1)
    h = rmsnorm(x, norm_g) * (1 + scale[:, None, :]) + shift[:, None, :]
    proj = h @ w_in
    q, k, v, g_attn, cb, cc, cx, g_conv, m_attn, m_conv = jnp.split(proj, IN_OFFSETS, axis=-1)
    attn = moba_attention(split_heads(q), split_heads(k), split_heads(v), rel_bias)
    attn = attn.transpose(0, 2, 1, 3).reshape(bsz, seq, ATTN_WIDTH)
    y_attn = (attn * jax.nn.silu(g_attn)) @ w_o_attn
    y_conv = (short_conv(cb, cc, cx, conv_w) * jax.nn.silu(g_conv)) @ w_o_conv
    merged = jax.nn.sigmoid(m_attn) * y_attn + jax.nn.sigmoid(m_conv) * y_conv
    return x + gate[:, None, :] * (merged @ w_out)

def second_inputs(seed: int = 0) -> dict:
    key = jax.random.key(seed)
    ks = jax.random.split(key, 13)
    nrm = jax.random.normal
    f32 = jnp.float32
    return {
        "x": nrm(ks[0], (BATCH, SEQ, D_MODEL), f32),
        "c": nrm(ks[1], (BATCH, D_MODEL), f32),
        "norm_g": 1.0 + 0.05 * nrm(ks[2], (DEPTH_2, D_MODEL), f32),
        "w_ada": 0.5 * D_MODEL ** -0.5 * nrm(ks[3], (DEPTH_2, D_MODEL, 3 * D_MODEL), f32),
        "b_ada": 0.1 * nrm(ks[4], (DEPTH_2, 3 * D_MODEL), f32),
        "w_in": D_MODEL ** -0.5 * nrm(ks[5], (DEPTH_2, D_MODEL, IN_COLS), f32),
        "conv_w": CONV_K ** -0.5 * nrm(ks[6], (DEPTH_2, CONV_K, CONV_WIDTH), f32),
        "w_o_attn": ATTN_WIDTH ** -0.5 * nrm(ks[7], (DEPTH_2, ATTN_WIDTH, D_MODEL), f32),
        "w_o_conv": CONV_WIDTH ** -0.5 * nrm(ks[8], (DEPTH_2, CONV_WIDTH, D_MODEL), f32),
        "w_out": D_MODEL ** -0.5 * nrm(ks[9], (DEPTH_2, D_MODEL, D_MODEL), f32),
        "rel_bias": 0.5 * nrm(ks[10], (N_BUCKETS, N_HEADS), f32),
        "final_g": 1.0 + 0.05 * nrm(ks[11], (D_MODEL,), f32),
    }

def second_block(x, c, norm_g, w_ada, b_ada, w_in, conv_w, w_o_attn, w_o_conv, w_out, rel_bias, final_g):
    for layer in range(DEPTH_2):
        x = hybrid_layer(x, c, norm_g[layer], w_ada[layer], b_ada[layer], w_in[layer],
                         conv_w[layer], w_o_attn[layer], w_o_conv[layer], w_out[layer], rel_bias)
    return rmsnorm(x, final_g)


def setup_inputs(seed=0):
    out = dict(first_inputs(seed))
    for name, value in second_inputs(seed + 1).items():
        if name != "x":
            out[name + "_2"] = value
    return out


def reference(
    x, c, ada_w, ada_b, norm_pre, norm_post, ffn_w1, ffn_w3, ffn_w2, ml_w_in, ml_b_gate,
    ml_norm_w, ml_w_out, mb_w_in, mb_conv_w, mb_conv_b, mb_dt_bias, mb_A_log, mb_D, mb_norm_w,
    mb_w_out, c_2, norm_g_2, w_ada_2, b_ada_2, w_in_2, conv_w_2, w_o_attn_2, w_o_conv_2,
    w_out_2, rel_bias_2, final_g_2,
):
    x = first_block(
        x, c, ada_w, ada_b, norm_pre, norm_post, ffn_w1, ffn_w3, ffn_w2, ml_w_in, ml_b_gate,
        ml_norm_w, ml_w_out, mb_w_in, mb_conv_w, mb_conv_b, mb_dt_bias, mb_A_log, mb_D,
        mb_norm_w, mb_w_out,
    )
    return second_block(
        x, c_2, norm_g_2, w_ada_2, b_ada_2, w_in_2, conv_w_2, w_o_attn_2, w_o_conv_2, w_out_2,
        rel_bias_2, final_g_2,
    )


_drawn_inputs = setup_inputs


def setup_inputs(seed=0):
    import zlib

    import numpy as np

    out = dict(_drawn_inputs(seed))
    spreads = {}
    factors = {'mb_conv_b': 8.0, 'mb_D': 2.84, 'norm_g_2': 4.108, 'rel_bias_2': 14.412}
    for name, (base, spread) in spreads.items():
        noise = np.random.default_rng([zlib.crc32(name.encode()), seed]).standard_normal(out[name].shape)
        drawn = base * np.exp(spread * noise) if base else spread * noise
        out[name] = __import__('jax').numpy.asarray(drawn.astype(out[name].dtype))
    for name, factor in factors.items():
        out[name] = (out[name] * factor).astype(out[name].dtype)
    return out
```

```python
import numpy as np
from contextlib import ExitStack

import concourse.bass as bass
from concourse import mybir

F32 = mybir.dt.float32
F32R = mybir.dt.float32r
BF16 = mybir.dt.bfloat16
ALU = mybir.AluOpType
ACT = mybir.ActivationFunctionType
AX = mybir.AxisListType.X

P = 128
D = 1024
SEQ = 256
T = SEQ // P
KT = D // P
F = 2816
FB = 256
NF = F // FB
UNIT = 2048
SLOTS = 3
EPS = 1e-6
NEG = -1e30

H_ML, DK, DV = 4, 128, 256
H_MB, HD, GROUPS, HPG, DI = 32, 64, 4, 8, 2048
CONV_F = 24
H_AT, DH = 8, 128
REL = 384

STAGES = 7

ROW_MOD = 0
ROW_C = ROW_MOD + 7 * 24
ROW_MBW = ROW_C + 16
ROW_HYW = ROW_MBW + 5 * CONV_F
ROWS = 384
assert ROW_HYW + 24 <= ROWS

ADA_GROUPS = {0: (1, 2), 2: (3,), 3: (4, 5), 5: (6,)}


class Count:

    def __init__(self, sem):
        self.sem, self.n, self.i, self.per = sem, 0, None, 0

    def on(self, ins, k=1):
        ins.then_inc(self.sem, k)
        self.n += k
        return ins

    def value(self):
        return self.n if self.i is None else self.i * self.per + self.n

    def enter(self, i, per):
        self.i, self.per, self.first = i, per, self.n

    def leave(self, steps):
        assert self.n - self.first == self.per, (self.n - self.first, self.per)
        self.n, self.i = self.first + self.per * steps, None


class Uses:

    def __init__(self, n):
        self.n, self.i, self.steps = [0] * n, None, 0

    def next(self, s):
        n = self.n[s] if self.i is None else self.i + self.n[s]
        self.n[s] += 1 if self.i is None else self.steps
        return n

    def enter(self, i, steps):
        self.i, self.steps = i, steps

    def leave(self):
        self.i = None


def build(nc, x_in, units, ada_units, rows, bcast, mlw, mlb, mbw, mbv, mbd, nw_ml, nw_mb, rel, onehot,
          negrow, out):
    scratch = nc.dram_tensor("bias_by_distance", (H_AT, REL), F32).ap()
    ctx = ExitStack()
    with ctx:
        def sb(name, shape, dt=F32):
            return ctx.enter_context(nc.sbuf_tensor(name, shape, dt))

        def sem(name):
            return ctx.enter_context(nc.semaphore(name))

        raw = sb("raw", [P, SLOTS, UNIT])
        whi = sb("whi", [P, SLOTS, UNIT], F32R)
        wlo = sb("wlo", [P, SLOTS, UNIT], F32R)
        xhi = sb("xhi", [P, 16, SEQ], F32R)
        xlo = sb("xlo", [P, 16, SEQ], F32R)
        hf = sb("hf", [P, KT, SEQ])
        x = sb("x", [P, T, D])
        gp = sb("gp", [P, 2, D])
        cols = sb("cols", [P, ROWS])
        cT = sb("cT", [P, 16])
        shT = sb("shT", [P, 7, KT])
        g1T = sb("g1T", [P, 7, KT])
        modc = sb("modc", [P, KT])
        ident = sb("ident", [P, P])
        ones = sb("ones", [P, SEQ])
        zero = sb("zero", [1, 512], BF16)
        negh = sb("negh", [P, 8])
        ssx = sb("ssx", [P, 8, 8])
        base = sb("base", [P, 8])
        mask = sb("mask", [P, SEQ])
        WORDS = 18432
        M = sb("M", [P, WORDS])
        ps = ctx.enter_context(nc.psum_tensor("ps", [P, 8, 512], F32))

        def m(off, *shape):
            n = int(np.prod(shape))
            assert off + n <= WORDS, off + n
            ap = M[:, off:off + n]
            return ap.rearrange("p (a b) -> p a b", b=shape[1]) if len(shape) == 2 else ap

        acc = m(0, 6144)
        araw = m(6144, 2, UNIT)
        brow = m(10240, 2, D)
        sil = m(12288, T, FB)
        g = m(12800, T, FB)
        qkT = m(0, 8, SEQ)
        vv = m(2048, T, D)
        og = m(4096, T, D)
        am = m(6144, T, D)
        E_ml = m(9216, 2, 384)
        gt = m(9984, 9, SEQ)
        colm = m(12544, T, 8)
        sm = m(12576, 8, 8)
        nwl = m(13312, D)
        mlw_sb = m(14336, KT, 36)
        mlb_sb = m(14624, 1)
        zs = m(0, T, DI)
        xcT = m(4096, CONV_F, SEQ)
        xs = m(10240, T, DI)
        cin = m(10240, 4, SEQ)
        cacc = m(11264, 4, SEQ)
        dtt = m(14336, 6, SEQ)
        colb = m(15872, 4, H_MB)
        nwm = m(16000, DI)
        xd = m(4096, T, 512)
        xj = m(5120, T, 512)
        mbw_sb = sb("mbw_sb", [P, KT, H_MB])
        mbd_sb = sb("mbd_sb", [P, H_MB])
        mbv_sb = sb("mbv_sb", [H_MB, 2])
        sg = sb("sg", [P, 2, 8])
        hfl = hf[:, :, :].rearrange("p a b -> p (a b)")
        E_mb = hfl[:, 0:768].rearrange("p (a b) -> p a b", b=384)
        W_mb = hfl[:, 768:1536].rearrange("p (a b) -> p a b", b=384)
        hT = m(0, 56, SEQ)
        vh = m(14336, T, D)
        bm = m(16384, H_AT, SEQ)
        bmr = m(4096, H_AT, SEQ)
        sgm = m(0, T, 2 * D)
        mg = m(6144, T, D)
        L_at = E_mb
        P_at = W_mb
        stat = sb("stat", [P, H_AT, 8])
        wdist = m(15200, REL)
        rel_sb = m(15600, H_AT)
        oneh_sb = m(17024, REL)
        negr_sb = m(17408, REL)
        vrow = m(14712, 3, P)
        jrev = m(8192, P)

        def xn_of(n):
            return m(6144, T, D) if n == 6 else m(16000, T, D)

        w_in = [sem(f"w_in{s}") for s in range(SLOTS)]
        w_hi = [sem(f"w_hi{s}") for s in range(SLOTS)]
        w_lo = [sem(f"w_lo{s}") for s in range(SLOTS)]
        w_used = [sem(f"w_used{s}") for s in range(SLOTS)]
        a_in = [sem(f"a_in{s}") for s in range(2)]
        a_used = [sem(f"a_used{s}") for s in range(2)]
        names = """x_in rows_in bias_in mlc_in mbc_in nwm_in scratch_in scratch_out bmr_in out_in brow_in
            const zero_acc cols_tr cols_ok c_ok wd_ps wd_ok  acc_act acc_dve acc_pool
            post_ss post_rstd pre_ss pre_rstd xn_ok tr_ok pre_hf pre_hi pre_lo
            mod_cols mod_gate mods_ok gate_read gp_ok
            gt_ps gt_hi gt_lo
            ml_gate ml_na ml_e ml_u ml_l ml_rows ml_em ml_ct ml_cols ml_sc ml_nm ml_arg ml_E ml_ST ml_nd
            ml_r ml_ss ml_rs ml_am ml_tr ml_hi ml_lo ml_row_free
            mb_gate mb_na mb_e mb_u mb_l mb_eA mb_rows mb_ct mb_cols mb_cv0 mb_conv mb_silu mb_xtr mb_xs
            mb_cb mb_ab mb_arg mb_E mb_W mb_y mb_xd mb_z mb_ss mb_rs mb_yn mb_tr mb_hi mb_lo
            hy_flip hy_bm hy_sc hy_L hy_P hy_Pn hy_pt hy_ptc hy_o hy_at hy_ga hy_alo  hy_cv hy_chi hy_clo
            hy_ya  hy_mg hy_mtr hy_mhi hy_mlo hy_fx hy_fs hy_fr hy_out hy_gs fg_in""".split()
        S = {k: sem(k) for k in names}
        y_done = [sem(f"y_done{t}") for t in range(T)]
        x_new = [sem(f"x_new{t}") for t in range(T)]
        s1_ok = [sem(f"s1_ok{t}") for t in range(T)]
        sil_ok = [sem(f"sil_ok{t}") for t in range(T)]
        g_ok = [sem(f"g_ok{t}") for t in range(T)]
        pj_ok = [sem(f"pj_ok{b}") for b in range(2)]
        pj_free = [sem(f"pj_free{b}") for b in range(2)]

        KIND = ["ffn", "ml", "ffn", "ffn", "mb", "ffn", "hy"][:STAGES]
        FFN_NO = {0: 0, 2: 1, 3: 2, 5: 3}
        PROJ_BEFORE = {1: 0, 4: 6, 6: 16}

        block = ctx.enter_context(nc.Block())

        LAST, used = {}, [0] * SLOTS
        for n_, kind_ in enumerate(KIND):
            if kind_ == "ffn":
                used = [u + NF for u in used]
                LAST[n_] = (2, used[2])
            else:
                if kind_ == "hy":
                    used_before_hy = list(used)
                blocks, outs = {"ml": (6, 4), "mb": (10, 8), "hy": (20, 12)}[kind_]
                used[0] += blocks
                used[1] += blocks
                for u in range(outs):
                    used[u % SLOTS] += 1
                LAST[n_] = ((outs - 1) % SLOTS, used[(outs - 1) % SLOTS])

        def wait_y(eng, n, t):
            if t == 0:
                eng.wait_ge(y_done[0], n + 1)
            else:
                eng.wait_ge(w_used[LAST[n][0]], LAST[n][1])

        MODS_BEFORE = {n_: 1 + sum(len(v) for k, v in ADA_GROUPS.items() if k < n_) for n_ in range(7)}
        ADA_PEEL = {1: 2, 2: 4}
        A_TOTAL = {}
        at = [6, 6]
        A_TOTAL[0] = tuple(at)
        for n_ in (0, 2, 3, 5):
            k = len(ADA_GROUPS[n_])
            at = [at[0] + (12 if k == 2 else 11), at[1] + (12 if k == 2 else 1)]
            for gr in ADA_GROUPS[n_]:
                A_TOTAL[gr] = tuple(at)

        @block.sync
        def _(sp):
            unit = [0]
            us = Uses(SLOTS)
            aunit = [0]
            ua = Uses(2)

            def load(s, index):
                n = us.next(s)
                if us.i is not None or n > 0:
                    sp.wait_ge(w_lo[s], n)
                sp.dma_start(raw[:, s, :], units[bass.ds(index, 1), :, :].rearrange("u p n -> p (u n)"))\
                  .then_inc(w_in[s], 16)

            def load_ada(s, index):
                n = ua.next(s)
                if ua.i is not None or n > 0:
                    sp.wait_ge(a_used[s], n)
                sp.dma_start(araw[:, s, :], ada_units[bass.ds(index, 1), :, :].rearrange("u p n -> p (u n)"))\
                  .then_inc(a_in[s], 16)

            def load_brow(k):
                if k:
                    sp.wait_ge(S["gp_ok"], k)
                sp.dma_start(brow[:, :, :], bass.AP(bcast.tensor, k * 2 * D, [[0, P], [1, 2 * D]]))\
                  .then_inc(S["brow_in"], 16)

            sp.dma_start(vrow[:, :, :], rows.rearrange("(a p) n -> p a n", p=P)).then_inc(S["rows_in"], 16)
            sp.dma_start(x[:, :, :], x_in.rearrange("(t p) d -> p t d", p=P)).then_inc(S["x_in"], 16)
            for a in range(2):
                load_ada(a, a)
            sp.dma_start(oneh_sb[0:32, :], onehot[:, :]).then_inc(S["bias_in"], 16)
            sp.dma_start(negr_sb[0:H_AT, :], negrow[:, :]).then_inc(S["bias_in"], 16)
            sp.dma_start(rel_sb[0:32, :], rel[:, :]).then_inc(S["bias_in"], 16)
            for a in range(2, 8):
                load_ada(a % 2, a)
            load(0, 0)
            load(1, 1)
            for a in range(8, 12):
                load_ada(a % 2, a)
            load_brow(0)
            unit[0], aunit[0] = 2, 12
            sp.wait_ge(S["wd_ok"], 1)
            sp.wait_ge(S["cols_ok"], 1)
            sp.dma_start(nwl, bass.AP(nw_ml.tensor, 0, [[0, P], [1, D]])).then_inc(S["mlc_in"], 16)
            sp.dma_start(mlw_sb[:, :, :], mlw).then_inc(S["mlc_in"], 16)
            sp.dma_start(mlb_sb[0:4, :], mlb[0:4, :]).then_inc(S["mlc_in"], 16)
            sp.dma_start(mlb_sb[32:36, :], mlb[4:8, :]).then_inc(S["mlc_in"], 16)
            sp.dma_start(mbw_sb[:, :, :], mbw).then_inc(S["mbc_in"], 16)
            sp.dma_start(mbv_sb[:, :], mbv).then_inc(S["mbc_in"], 16)
            sp.dma_start(mbd_sb[:, :], bass.AP(mbd.tensor, 0, [[0, P], [1, H_MB]])).then_inc(S["mbc_in"], 16)
            sp.dma_start(scratch[:, :], wdist[0:H_AT, :]).then_inc(S["scratch_out"], 16)

            for n, kind in enumerate(KIND):
                if kind == "ffn":
                    na = len(ADA_GROUPS[n])
                    if n:
                        for t in range(T):
                            sp.wait_ge(x_new[t], n)
                    load_brow(MODS_BEFORE[n])
                    load(0, unit[0])
                    load(1, unit[0] + 1)
                    for a in range(ADA_PEEL[na]):
                        load_ada(a % 2, aunit[0] + a)
                    unit[0] += 2
                    aunit[0] += ADA_PEEL[na]
                    with sp.Fori(0, NF - 1) as i:
                        us.enter(i, NF - 1)
                        ua.enter(i, NF - 1)
                        load(2, i * 3 + unit[0])
                        load_ada(0, i * na + aunit[0])
                        load(0, i * 3 + (unit[0] + 1))
                        load(1, i * 3 + (unit[0] + 2))
                        if na == 2:
                            load_ada(1, i * na + (aunit[0] + 1))
                        us.leave()
                        ua.leave()
                    unit[0] += 3 * (NF - 1)
                    aunit[0] += na * (NF - 1)
                    load(2, unit[0])
                    unit[0] += 1
                    if na == 2:
                        load_brow(MODS_BEFORE[n] + 1)
                else:
                    blocks, outs = {"ml": (6, 4), "mb": (10, 8), "hy": (20, 12)}[kind]
                    if kind == "mb":
                        sp.wait_ge(S["tr_ok"], 2 * n + 2)
                        sp.dma_start(nwm, bass.AP(nw_mb.tensor, 0, [[0, P], [1, DI]])).then_inc(S["nwm_in"], 16)
                    if kind == "hy":
                        for t in range(T):
                            sp.wait_ge(x_new[t], n)
                        sp.wait_ge(S["scratch_out"], 16)
                        sp.dma_start(bmr[:, :, 0:P], bass.AP(scratch.tensor, 0, [[1, P], [REL, H_AT], [1, P]]))\
                          .then_inc(S["bmr_in"], 16)
                        sp.dma_start(bmr[:, :, P:SEQ], bass.AP(scratch.tensor, P, [[1, P], [REL, H_AT], [1, P]]))\
                          .then_inc(S["bmr_in"], 16)
                    with sp.Fori(0, blocks) as i:
                        us.enter(i, blocks)
                        load(0, i * 2 + unit[0])
                        load(1, i * 2 + (unit[0] + 1))
                        us.leave()
                    unit[0] += 2 * blocks
                    for u in range(2, outs):
                        load(u % SLOTS, unit[0])
                        unit[0] += 1
                    if kind != "hy":
                        load(0, unit[0])
                        load(1, unit[0] + 1)
                        unit[0] += 2
                    else:
                        sp.dma_start(gp[:, 1, :], bass.AP(bcast.tensor, 13 * D, [[0, P], [1, D]])).then_inc(S["fg_in"], 16)
            if STAGES == 7:
                for t in range(T):
                    sp.wait_ge(S["hy_out"], t + 1)
                    sp.dma_start(out[t * P:(t + 1) * P, :], vh[:, t, :]).then_inc(S["out_in"], 16)
            else:
                sp.wait_ge(S["mlc_in"], 64)
                sp.wait_ge(S["mbc_in"], 48)
                sp.wait_ge(S["scratch_out"], 16)
                for s in range(SLOTS):
                    if s < 2: sp.wait_ge(w_lo[s], us.n[s])
                for t in range(T):
                    sp.wait_ge(x_new[t], STAGES)
                    sp.dma_start(out[t * P:(t + 1) * P, :], x[:, t, :]).then_inc(S["out_in"], 16)
            sp.wait_ge(S["out_in"], 16 * T)

        @block.gpsimd
        def _(pool):
            c = Count(S["acc_pool"])

            def step(ins):
                c.on(ins)
                pool.wait_ge(c.sem, c.n)

            pool.memset(zero[:, :], 0.0).then_inc(S["const"], 1)
            pool.memset(ones[:, :], 1.0).then_inc(S["const"], 1)
            pool.memset(negh[:, :], -0.5).then_inc(S["const"], 1)
            step(pool.memset(ident[:, :], 0.0))
            pool.affine_select(out=ident[:, :], in_=ident[:, :], compare_op=ALU.not_equal, fill=1.0, base=0,
                               pattern=[[-1, P]], channel_multiplier=1).then_inc(S["const"], 1)
            pool.memset(acc, 0.0).then_inc(S["zero_acc"], 1)
            step(pool.memset(mask[:, :], 0.0))
            pool.affine_select(out=mask[:, 0:P], in_=mask[:, 0:P], compare_op=ALU.is_ge, fill=NEG, base=0,
                               pattern=[[1, P]], channel_multiplier=-1).then_inc(S["const"], 1)

            taken = {}

            def inv_rms(src, dst, count, ready):
                w = src.shape[1]
                step(pool.tensor_scalar(base[:, 0:w], src, 1.0 / count, EPS, ALU.mult, ALU.add))
                pool.tensor_tensor(dst, base[:, 0:w], negh[:, 0:w], ALU.pow).then_inc(ready, 1)
                taken[ready.name] = taken.get(ready.name, 0) + 1
                pool.wait_ge(ready, taken[ready.name])

            for n, kind in enumerate(KIND):
                for t in range(T):
                    pool.wait_ge(S["pre_ss"], 2 * n + t + 1)
                    inv_rms(ssx[:, n, t:t + 1], ssx[:, n, 2 + t:3 + t], D, S["pre_rstd"])
                if kind == "ffn":
                    k = MODS_BEFORE[n]
                    pool.wait_ge(S["mod_gate"], k)
                    pool.memset(acc, 0.0).then_inc(S["zero_acc"], 1)
                if kind == "ml":
                    for k in range(2):
                        pool.wait_ge(pj_free[1], PROJ_BEFORE[n] + 5 + k)
                        pool.wait_ge(S["mlc_in"], 64)
                        o_ = og[:, :, 512 * k:512 * (k + 1)]
                        for t in range(T):
                            pool.tensor_tensor(o_[:, t, :], o_[:, t, :], nwl[:, 512 * k:512 * (k + 1)], ALU.mult)\
                                .then_inc(S["ml_row_free"], 1)
                    pool.wait_ge(S["ml_ss"], 8)
                    inv_rms(sm[:, 3, :], sm[:, 4, :], DV, S["ml_rs"])
                if kind == "mb":
                    for gr in range(GROUPS):
                        pool.wait_ge(S["mb_xs"], GROUPS)
                        if gr:
                            pool.wait_ge(S["mb_z"], 4 * gr)
                        for t in range(T):
                            pool.tensor_tensor(
                                xd[:, t, :].rearrange("p (h d) -> p h d", d=HD),
                                xs[:, t, gr * 512:(gr + 1) * 512].rearrange("p (h d) -> p h d", d=HD),
                                mbd_sb[:, gr * HPG:(gr + 1) * HPG].unsqueeze(2).to_broadcast([P, HPG, HD]),
                                ALU.mult).then_inc(S["mb_xd"], 1)
                        pool.wait_ge(S["mb_ss"], 2 * gr + 2)
                        inv_rms(sg[:, 0, 2 * gr:2 * gr + 2], sg[:, 1, 2 * gr:2 * gr + 2], 512, S["mb_rs"])
                if kind == "hy":
                    pool.wait_ge(S["bmr_in"], 32)
                    step(pool.memset(jrev, 0.0))
                    pool.affine_select(out=jrev, in_=jrev, compare_op=ALU.not_equal, fill=1.0, base=1 - P,
                                       pattern=[[1, P]], channel_multiplier=1).then_inc(S["hy_gs"], 1)
                    for t in range(T):
                        pool.wait_ge(S["hy_fs"], t + 1)
                        inv_rms(ssx[:, n, 4 + t:5 + t], ssx[:, n, 6 + t:7 + t], D, S["hy_fr"])
                else:
                    for t in range(T):
                        pool.wait_ge(S["post_ss"], 2 * n + t + 1)
                        inv_rms(ssx[:, n, 4 + t:5 + t], ssx[:, n, 6 + t:7 + t], D, S["post_rstd"])

        @block.scalar
        def _(act):
            c = Count(S["acc_act"])
            us = Uses(SLOTS)

            def step(ins):
                c.on(ins)
                act.wait_ge(c.sem, c.n)

            def hi(s):
                n = us.next(s)
                act.wait_ge(w_in[s], 16 * n + 16)
                if us.i is not None or n > 0:
                    act.wait_ge(w_used[s], n)
                act.activation(whi[:, s, :], raw[:, s, :], ACT.Copy).then_inc(w_hi[s], 1)

            def project(blocks, evacs, pb):
                with act.Fori(0, blocks) as i:
                    us.enter(i, blocks)
                    hi(0)
                    act.wait_ge(pj_ok[0], i + (pb + 1))
                    evacs(0, i)
                    n1 = i + us.n[1]
                    hi(1)
                    evacs(1, i)
                    us.leave()

            def out_units(outs, more):
                for u in range(2, outs):
                    hi(u % SLOTS)
                if more:
                    hi(0)
                    hi(1)

            act.wait_ge(S["cols_ok"], 1)
            act.activation(cT[:, :], cols[:, ROW_C:ROW_C + 16], ACT.Silu).then_inc(S["c_ok"], 1)
            hi(0)
            hi(1)

            for n, kind in enumerate(KIND):
                for t in range(T):
                    if n == 0:
                        act.wait_ge(S["x_in"], 16)
                    else:
                        act.wait_ge(x_new[t], n)
                    act.activation(hfl[:, t * D:(t + 1) * D], x[:, t, :], ACT.Square,
                                   accum_out=ssx[:, n, t:t + 1]).then_inc(S["pre_ss"], 1)
                for half in range(2):
                    act.wait_ge(S["pre_hf"], 2 * n + half + 1)
                    act.activation(xhi[:, 4 * half:4 * half + 4, :], hf[:, 4 * half:4 * half + 4, :], ACT.Copy)\
                       .then_inc(S["pre_hi"], 1)
                if kind == "ffn":
                    f = FFN_NO[n]

                    def silu(t, done):
                        act.wait_ge(g_ok[t], done)
                        act.activation(sil[:, t, :], ps[:, 4 + t, 0:FB], ACT.Silu).then_inc(sil_ok[t], 1)

                    hi(0)
                    act.wait_ge(s1_ok[0], NF * f + 1)
                    silu(0, NF * f)
                    hi(1)
                    silu(1, NF * f)
                    with act.Fori(0, NF - 1) as i:
                        us.enter(i, NF - 1)
                        hi(2)
                        act.wait_ge(S["gt_ps"], i + (NF * f + 1))
                        act.activation(xhi[:, 8:10, :], ps[:, 6, :], ACT.Copy).then_inc(S["gt_hi"], 1)
                        hi(0)
                        act.wait_ge(s1_ok[0], i + (NF * f + 2))
                        silu(0, i + (NF * f + 1))
                        hi(1)
                        silu(1, i + (NF * f + 1))
                        us.leave()
                    act.wait_ge(w_used[2], us.n[2])
                    act.wait_ge(S["gt_ps"], NF * f + NF)
                    act.activation(xhi[:, 8:10, :], ps[:, 6, :], ACT.Copy).then_inc(S["gt_hi"], 1)
                    hi(2)
                if kind == "ml":
                    act.wait_ge(S["gp_ok"], MODS_BEFORE[n])
                    act.wait_ge(S["ml_na"], 1)
                    act.activation(gt[0:4, 3, :], gt[0:4, 2, :], ACT.Exp).then_inc(S["ml_e"], 1)
                    act.wait_ge(S["ml_u"], 1)
                    act.activation(gt[0:4, 5, :], gt[0:4, 4, :], ACT.Ln).then_inc(S["ml_l"], 1)
                    act.wait_ge(S["ml_rows"], 1)
                    act.activation(gt[0:4, 3, :], gt[0:4, 2, :], ACT.Exp, scale=-1.0).then_inc(S["ml_em"], 1)

                    def ev_qk(b, i):
                        act.activation(qkT[:, bass.ds(i * 4 + 2 * b, 2), :],
                                       ps[:, 4 + b, :].rearrange("p (a b) -> p a b", b=SEQ), ACT.Copy)\
                           .then_inc(pj_free[b], 1)

                    def ev_v(b, i):
                        act.activation(vv[:, b, bass.ds(i * 512, 512)], ps[:, 4 + b, :], ACT.Copy)\
                           .then_inc(pj_free[b], 1)

                    def ev_o(b, i):
                        act.activation(og[:, b, bass.ds(i * 512, 512)], ps[:, 4 + b, :], ACT.Sigmoid)\
                           .then_inc(pj_free[b], 1)

                    pb = PROJ_BEFORE[n]
                    project(2, ev_qk, pb)
                    project(2, ev_v, pb + 2)
                    project(2, ev_o, pb + 4)
                    for h in range(H_ML):
                        act.wait_ge(S["ml_arg"], h + 1)
                        act.activation(E_ml[:, h % 2, :], E_ml[:, h % 2, :], ACT.Exp).then_inc(S["ml_E"], 1)
                    act.wait_ge(S["ml_nd"], H_ML)
                    act.wait_ge(S["ml_r"], 1)
                    for t in range(T):
                        for h in range(H_ML):
                            act.activation(hfl[:, (4 * t + h) * DV:(4 * t + h + 1) * DV],
                                           ps[:, 2 * t + h // 2, (h % 2) * DV:(h % 2 + 1) * DV], ACT.Square,
                                           scale=sm[:, 2, 4 * t + h:4 * t + h + 1],
                                           accum_out=sm[:, 3, 4 * t + h:4 * t + h + 1]).then_inc(S["ml_ss"], 1)
                    for q in range(2):
                        act.wait_ge(S["ml_tr"], q + 1)
                        act.activation(xhi[:, 4 * q:4 * q + 4, :], ps[:, 4 + 2 * q:6 + 2 * q, :], ACT.Copy)\
                           .then_inc(S["ml_hi"], 1)
                    out_units(4, True)
                if kind == "mb":
                    act.wait_ge(S["gp_ok"], MODS_BEFORE[n])
                    act.wait_ge(S["mb_na"], 1)
                    act.activation(dtt[0:H_MB, 2, :], dtt[0:H_MB, 1, :], ACT.Exp).then_inc(S["mb_e"], 1)
                    act.wait_ge(S["mbc_in"], 48)
                    act.activation(sg[0:H_MB, 0, 0:1], mbv_sb[:, 1:2], ACT.Exp).then_inc(S["mb_eA"], 1)
                    act.wait_ge(S["mb_u"], 1)
                    act.activation(dtt[0:H_MB, 4, :], dtt[0:H_MB, 3, :], ACT.Ln).then_inc(S["mb_l"], 1)

                    def ev_z(b, i):
                        act.activation(zs[:, b, bass.ds(i * 512, 512)], ps[:, 4 + b, :], ACT.Silu)\
                           .then_inc(pj_free[b], 1)

                    def ev_x(b, i):
                        act.wait_ge(S["mb_conv"], i * 2)
                        act.wait_ge(S["mb_silu"], i * 2)
                        for k in range(2):
                            q = 2 * b + k
                            act.activation(cacc[:, q, :], ps[:, 4 + b, k * SEQ:(k + 1) * SEQ], ACT.Identity,
                                           scale=cols[:, bass.ds(i * 4 + (ROW_MBW + 3 * CONV_F + q), 1)],
                                           bias=cols[:, bass.ds(i * 4 + (ROW_MBW + 4 * CONV_F + q), 1)])\
                               .then_inc(S["mb_cv0"], 1)
                        act.activation(cin[:, 2 * b:2 * b + 2, :],
                                       ps[:, 4 + b, :].rearrange("p (a b) -> p a b", b=SEQ), ACT.Copy)\
                           .then_inc(pj_free[b], 1)
                        if b:
                            for bb in range(2):
                                act.wait_ge(S["mb_conv"], i * 2 + (bb + 1))
                                act.activation(xcT[:, bass.ds(i * 4 + 2 * bb, 2), :], cacc[:, 2 * bb:2 * bb + 2, :],
                                               ACT.Silu).then_inc(S["mb_silu"], 1)

                    pb = PROJ_BEFORE[n]
                    project(4, ev_z, pb)
                    project(6, ev_x, pb + 4)
                    for k in range(GROUPS):
                        act.wait_ge(S["mb_xtr"], k + 1)
                        act.activation(xs[:, k % 2, (k // 2) * D:(k // 2 + 1) * D], ps[:, 2 * (k % 2):2 * (k % 2) + 2, :],
                                       ACT.Copy).then_inc(S["mb_xs"], 1)
                    for h in range(H_MB):
                        act.wait_ge(S["mb_arg"], h + 1)
                        act.activation(E_mb[:, h % 2, :], E_mb[:, h % 2, :], ACT.Exp).then_inc(S["mb_E"], 1)
                        if h % HPG == 4 and h > HPG:
                            gr = h // HPG - 1
                            for t in range(T):
                                act.wait_ge(S["mb_z"], 4 * gr + 2 * t + 2)
                                act.activation(xj[:, t, :], zs[:, t, gr * 512:(gr + 1) * 512], ACT.Square,
                                               accum_out=sg[:, 0, 2 * gr + t:2 * gr + t + 1]).then_inc(S["mb_ss"], 1)
                    for t in range(T):
                        gr = GROUPS - 1
                        act.wait_ge(S["mb_z"], 4 * gr + 2 * t + 2)
                        act.activation(xj[:, t, :], zs[:, t, gr * 512:(gr + 1) * 512], ACT.Square,
                                       accum_out=sg[:, 0, 2 * gr + t:2 * gr + t + 1]).then_inc(S["mb_ss"], 1)
                    for q in range(4):
                        act.wait_ge(S["mb_tr"], q + 1)
                        act.activation(xhi[:, 4 * q:4 * q + 4, :], ps[:, 2 * q:2 * q + 2, :], ACT.Copy)\
                           .then_inc(S["mb_hi"], 1)
                    out_units(8, True)
                if kind == "hy":
                    for k in range(4):
                        act.wait_ge(S["hy_flip"], k + 1)
                        act.activation(bm[:, 2 * k:2 * k + 2, :], ps[:, 4 + k % 2, :]
                                       .rearrange("p (a b) -> p a b", b=SEQ), ACT.Copy).then_inc(S["hy_bm"], 1)

                    def ev_h(b, i):
                        act.activation(hT[:, bass.ds(i * 4 + 2 * b, 2), :],
                                       ps[:, 4 + b, :].rearrange("p (a b) -> p a b", b=SEQ), ACT.Copy)\
                           .then_inc(pj_free[b], 1)

                    def ev_hs(off):
                        def ev(b, i):
                            act.activation(hT[:, bass.ds(i * 4 + (off + 2 * b), 2), :],
                                           ps[:, 4 + b, :].rearrange("p (a b) -> p a b", b=SEQ), ACT.Silu)\
                               .then_inc(pj_free[b], 1)
                        return ev

                    def ev_hc(b, i):
                        act.activation(hT[:, bass.ds(i * 4 + (24 + 2 * b), 2), :],
                                       ps[:, 4 + b, :].rearrange("p (a b) -> p a b", b=SEQ), ACT.Copy)\
                           .then_inc(pj_free[b], 1)

                    def ev_vh(b, i):
                        act.activation(vh[:, b, bass.ds(i * 512, 512)], ps[:, 4 + b, :], ACT.Copy)\
                           .then_inc(pj_free[b], 1)

                    def ev_m(b, i):
                        act.activation(sgm[:, b, bass.ds(i * 512, 512)], ps[:, 4 + b, :], ACT.Sigmoid)\
                           .then_inc(pj_free[b], 1)

                    pb = PROJ_BEFORE[n]
                    project(4, ev_h, pb)
                    project(2, ev_hs(16), pb + 4)
                    project(6, ev_hc, pb + 6)
                    project(2, ev_hs(48), pb + 12)
                    project(2, ev_vh, pb + 14)

                    def softmax(h):
                        act.wait_ge(S["hy_L"], h + 1)
                        for t in range(T):
                            sl = slice(0, P) if t == 0 else slice(P, 384)
                            act.activation(P_at[:, h % 2, sl], L_at[:, h % 2, sl], ACT.Exp,
                                           bias=stat[:, h, 2 + t:3 + t], accum_out=stat[:, h, 4 + t:5 + t])\
                               .then_inc(S["hy_P"], 1)

                    softmax(0)
                    for h in range(H_AT):
                        if h + 1 < H_AT:
                            softmax(h + 1)
                        act.wait_ge(S["hy_pt"], h + 1)
                        act.activation(L_at[:, h % 2, :], ps[:, 6, 0:384], ACT.Copy).then_inc(S["hy_ptc"], 1)
                    act.wait_ge(S["hy_at"], H_AT)
                    act.activation(xhi[:, 8:16, :], hT[:, 16:24, :], ACT.Copy).then_inc(S["hy_ga"], 1)
                    project(4, ev_m, pb + 16)
                    act.wait_ge(S["hy_cv"], 4)
                    act.activation(xhi[:, 0:8, :], hT[:, 40:48, :], ACT.Copy).then_inc(S["hy_chi"], 1)
                    for u in range(2, 8):
                        hi(u % SLOTS)
                    for q in range(2):
                        act.wait_ge(S["hy_mtr"], q + 1)
                        act.activation(xhi[:, 8 + 4 * q:12 + 4 * q, :], ps[:, 4 + 2 * q:6 + 2 * q, :], ACT.Copy)\
                           .then_inc(S["hy_mhi"], 1)
                    for u in range(8, 12):
                        hi(u % SLOTS)
                    for t in range(T):
                        act.wait_ge(S["hy_fx"], t + 1)
                        act.activation(hfl[:, t * D:(t + 1) * D], x[:, t, :], ACT.Square,
                                       accum_out=ssx[:, n, 4 + t:5 + t]).then_inc(S["hy_fs"], 1)
                else:
                    for t in range(T):
                        wait_y(act, n, t)
                        act.activation(hfl[:, t * D:(t + 1) * D], ps[:, 2 * t:2 * t + 2, :], ACT.Square,
                                       accum_out=ssx[:, n, 4 + t:5 + t]).then_inc(S["post_ss"], 1)

        @block.tensor
        def _(pe):
            us = Uses(SLOTS)

            def mm(out, lhsT, rhs, start=False, stop=False):
                return pe.matmul(out, lhsT, rhs, start=start, stop=stop, skip_group_check=True)

            def three(out, ahi, alo, bhi, blo, start=False, stop=False):
                mm(out, ahi, bhi, start=start)
                mm(out, ahi, blo)
                return mm(out, alo, bhi, stop=stop)

            def ready(s):
                pe.wait_ge(w_lo[s], us.next(s) + 1)

            def by_token(s, t, last):
                for kk in range(4):
                    k = 4 * s + kk
                    w = slice(kk * 512, kk * 512 + 512)
                    r = three(ps[:, 4 + t, :], xhi[:, k, t * P:(t + 1) * P], xlo[:, k, t * P:(t + 1) * P],
                              whi[:, s, w], wlo[:, s, w], start=(k == 0), stop=(k == 7))
                return r

            def by_feature(s, q):
                for kk in range(4):
                    k = 4 * s + kk
                    w = slice(kk * 512 + q * P, kk * 512 + q * P + P)
                    r = three(ps[:, 4 + q // 2, (q % 2) * SEQ:(q % 2 + 1) * SEQ], whi[:, s, w], wlo[:, s, w],
                              xhi[:, k, :], xlo[:, k, :], start=(k == 0 and q % 2 == 0), stop=(k == 7))
                return r

            def project(blocks, token, pb):
                with pe.Fori(0, blocks) as i:
                    us.enter(i, blocks)
                    ready(0)
                    if token:
                        pe.wait_ge(pj_free[0], i + pb)
                        by_token(0, 0, False)
                        pe.wait_ge(pj_free[1], i + pb)
                        by_token(0, 1, False).then_inc(w_used[0], 1)
                        ready(1)
                        by_token(1, 0, True).then_inc(pj_ok[0], 1)
                        by_token(1, 1, True).then_inc(w_used[1], 1)
                    else:
                        for b in range(2):
                            pe.wait_ge(pj_free[b], i + pb)
                            by_feature(0, 2 * b)
                            r = by_feature(0, 2 * b + 1)
                        r.then_inc(w_used[0], 1)
                        ready(1)
                        by_feature(1, 0)
                        by_feature(1, 1).then_inc(pj_ok[0], 1)
                        by_feature(1, 2)
                        by_feature(1, 3).then_inc(w_used[1], 1)
                    us.leave()

            def down(s, k, start=False, stop=False, done0=None):
                ready(s)
                for t in range(T):
                    for kk in range(2):
                        for n in range(2):
                            w = slice(kk * D + n * 512, kk * D + n * 512 + 512)
                            r = three(ps[:, 2 * t + n, :], xhi[:, k + kk, t * P:(t + 1) * P],
                                      xlo[:, k + kk, t * P:(t + 1) * P], whi[:, s, w], wlo[:, s, w],
                                      start=start and kk == 0, stop=stop and kk == 1)
                    if t == 0 and done0 is not None:
                        r.then_inc(done0, 1)
                r.then_inc(w_used[s], 1)

            def modulation(k, a):
                for s in range(2):
                    pe.wait_ge(a_used[s], A_TOTAL[k][s])
                if k:
                    pe.wait_ge(S["mods_ok"], k)
                for q in range(16):
                    r = mm(ps[:, 7, q:q + 1], acc[:, a + q * P:a + (q + 1) * P], ones[:, 0:1], start=True, stop=True)
                r.then_inc(S["mod_cols"], 1)
                if k:
                    pe.wait_ge(S["gate_read"], k)
                for q in range(2):
                    r = mm(ps[:, 4 + q, :], ones[:, 0:P], acc[:, a + 2 * D + q * 512:a + 2 * D + (q + 1) * 512],
                           start=True, stop=True)
                r.then_inc(S["mod_gate"], 1)

            pe.wait_ge(S["const"], 5)
            pe.wait_ge(S["rows_in"], 16)
            for a in range(3):
                r = pe.transpose(ps[:, 6, a * P:(a + 1) * P], vrow[:, a, :], ident[:, :])
            r.then_inc(S["cols_tr"], 1)
            pe.wait_ge(S["bias_in"], 48)
            mm(ps[0:H_AT, 5, 0:REL], rel_sb[0:32, :], oneh_sb[0:32, :], start=True, stop=True).then_inc(S["wd_ps"], 1)
            pe.wait_ge(S["wd_ok"], 1)
            modulation(0, 0)

            for n, kind in enumerate(KIND):
                pe.wait_ge(S["xn_ok"], 2 * n + 2)
                xn = xn_of(n)
                for k in range(KT):
                    for t in range(T):
                        r = pe.transpose(ps[:, k // 2, (k % 2) * SEQ + t * P:(k % 2) * SEQ + (t + 1) * P],
                                         xn[:, t, k * P:(k + 1) * P], ident[:, :])
                    if k % 4 == 3:
                        r.then_inc(S["tr_ok"], 1)
                if kind == "hy":
                    pe.wait_ge(S["gate_read"], MODS_BEFORE[n])
                    pe.wait_ge(S["hy_gs"], 1)
                    for k in range(4):
                        if k >= 2:
                            pe.wait_ge(S["hy_bm"], k - 1)
                        mm(ps[:, 4 + k % 2, :], jrev, bmr[:, 2 * k:2 * k + 2, :], start=True, stop=True)\
                            .then_inc(S["hy_flip"], 1)
                    pe.wait_ge(S["hy_bm"], 4)
                pe.wait_ge(S["gate_read"], MODS_BEFORE[n])
                pe.wait_ge(S["pre_lo"], 2 * n + 1)
                if kind == "ffn":
                    f = FFN_NO[n]
                    b = NF * f

                    def turn(i):
                        for t in range(T):
                            pe.wait_ge(g_ok[t], i + (b + 1))
                        pe.wait_ge(S["gt_lo"], i + b)
                        for kk in range(2):
                            for t in range(T):
                                r = pe.transpose(ps[:, 6, kk * SEQ + t * P:kk * SEQ + (t + 1) * P],
                                                 g[:, t, kk * P:(kk + 1) * P], ident[:, :])
                        r.then_inc(S["gt_ps"], 1)

                    ready(0)
                    by_token(0, 0, False)
                    by_token(0, 1, False).then_inc(w_used[0], 1)
                    ready(1)
                    pe.wait_ge(S["pre_lo"], 2 * n + 2)
                    by_token(1, 0, True).then_inc(s1_ok[0], 1)
                    by_token(1, 1, True).then_inc(w_used[1], 1)
                    for q in range(4):
                        mm(ps[:, q, :], zero[0:1, 0:P], zero[0:1, :], start=True)
                    with pe.Fori(0, NF - 1) as i:
                        us.enter(i, NF - 1)
                        ready(0)
                        for t in range(T):
                            pe.wait_ge(g_ok[t], i + (b + 1))
                            r = by_token(0, t, False)
                        r.then_inc(w_used[0], 1)
                        turn(i)
                        ready(1)
                        by_token(1, 0, True).then_inc(s1_ok[0], 1)
                        by_token(1, 1, True).then_inc(w_used[1], 1)
                        pe.wait_ge(S["gt_lo"], i + (b + 1))
                        down(2, 8)
                        us.leave()
                    turn(NF - 1)
                    for q, k in enumerate(ADA_GROUPS[n][:1]):
                        modulation(k, 0)
                    pe.wait_ge(S["gt_lo"], b + NF)
                    down(2, 8, stop=True, done0=y_done[0])
                    for k in ADA_GROUPS[n][1:]:
                        modulation(k, 3 * D)
                if kind == "ml":
                    pe.wait_ge(S["mlc_in"], 64)
                    pe.wait_ge(S["pre_lo"], 2 * n + 2)
                    pe.wait_ge(S["mods_ok"], MODS_BEFORE[n])
                    for k in range(KT):
                        r = mm(ps[0:36, 7, 0:SEQ], mlw_sb[:, k, :], hf[:, k, :], start=(k == 0), stop=(k == 7))
                    r.then_inc(S["ml_gate"], 1)
                    pb = PROJ_BEFORE[n]
                    project(2, False, pb)
                    pe.wait_ge(S["ml_rows"], 2)
                    pe.wait_ge(S["ml_em"], 1)
                    for j, row in enumerate((8, 3)):
                        for t in range(T):
                            r = pe.transpose(ps[:, 7, 256 + (t * 2 + j) * 4:256 + (t * 2 + j) * 4 + 4],
                                             gt[0:4, row, t * P:(t + 1) * P], ident[0:4, 0:4])
                    r.then_inc(S["ml_ct"], 1)
                    project(4, True, pb + 2)

                    def scores(h):
                        if h >= 2:
                            pe.wait_ge(S["ml_ST"], h - 1)
                        else:
                            pe.wait_ge(pj_free[h], pb + 6)
                        b = 4 + h % 2
                        mm(ps[:, b, 0:SEQ], qkT[:, 4 + h, 0:P], qkT[:, h, :], start=True, stop=True)
                        mm(ps[:, b, SEQ:384], qkT[:, 4 + h, P:SEQ], qkT[:, h, P:SEQ], start=True, stop=True)\
                            .then_inc(S["ml_sc"], 1)

                    def minus_max(h):
                        pe.wait_ge(S["ml_cols"], 1)
                        if h >= 2:
                            pe.wait_ge(S["ml_arg"], h - 1)
                        mm(ps[:, 6 + h % 2, 0:SEQ], ident[0:4, h:h + 1].to_broadcast([4, P]), gt[0:4, 2, :],
                           start=True, stop=True).then_inc(S["ml_nm"], 1)

                    pe.wait_ge(pj_free[1], pb + 6)
                    scores(0)
                    minus_max(0)
                    scores(1)
                    minus_max(1)
                    for h in range(H_ML):
                        pe.wait_ge(S["ml_ST"], h + 1)
                        e0, e1, e2 = (E_ml[:, h % 2, k * P:(k + 1) * P] for k in range(3))
                        v0, v1 = (vv[:, t, h * DV:(h + 1) * DV] for t in range(2))
                        o0, o1 = (ps[:, 2 * t + h // 2, (h % 2) * DV:(h % 2 + 1) * DV] for t in range(2))
                        d0, d1 = (ps[:, 7, 300 + 4 * t + h:301 + 4 * t + h] for t in range(2))
                        mm(o0, e0, v0, start=True, stop=True)
                        mm(o1, e1, v0, start=True)
                        mm(o1, e2, v1, stop=True)
                        mm(d0, e0, ones[:, 0:1], start=True, stop=True)
                        mm(d1, e1, ones[:, 0:1], start=True)
                        mm(d1, e2, ones[:, 0:1], stop=True).then_inc(S["ml_nd"], 1)
                        if h + 2 < H_ML:
                            scores(h + 2)
                            minus_max(h + 2)
                    pe.wait_ge(S["ml_am"], 8)
                    for k in range(KT):
                        for t in range(T):
                            r = pe.transpose(ps[:, 4 + k // 2, (k % 2) * SEQ + t * P:(k % 2) * SEQ + (t + 1) * P],
                                             am[:, t, k * P:(k + 1) * P], ident[:, :])
                        if k % 4 == 3:
                            r.then_inc(S["ml_tr"], 1)
                    for u in range(4):
                        pe.wait_ge(S["ml_lo"], u // 2 + 1)
                        down(u % SLOTS, 2 * u, start=(u == 0), stop=(u == 3), done0=y_done[0] if u == 3 else None)
                if kind == "mb":
                    pe.wait_ge(S["mbc_in"], 48)
                    pe.wait_ge(S["pre_lo"], 2 * n + 2)
                    pe.wait_ge(S["mods_ok"], MODS_BEFORE[n])
                    for k in range(KT):
                        r = mm(ps[0:H_MB, 7, 0:SEQ], mbw_sb[:, k, :], hf[:, k, :], start=(k == 0), stop=(k == 7))
                    r.then_inc(S["mb_gate"], 1)
                    pb = PROJ_BEFORE[n]
                    project(4, True, pb)
                    pe.wait_ge(S["mb_rows"], 1)
                    for j, row in enumerate((5, 3)):
                        for t in range(T):
                            r = pe.transpose(ps[:, 7, 256 + (2 * j + t) * 32:256 + (2 * j + t + 1) * 32],
                                             dtt[0:H_MB, row, t * P:(t + 1) * P], ident[0:H_MB, 0:H_MB])
                    r.then_inc(S["mb_ct"], 1)
                    project(6, False, pb + 4)
                    pe.wait_ge(S["mb_silu"], 12)
                    for k in range(GROUPS):
                        if k >= 2:
                            pe.wait_ge(S["mb_xs"], k - 1)
                        for q in range(8):
                            r = pe.transpose(ps[:, 2 * (k % 2) + q // 4, (q % 4) * P:(q % 4 + 1) * P],
                                             xcT[:, 8 * (k // 2) + q, (k % 2) * P:(k % 2 + 1) * P], ident[:, :])
                        r.then_inc(S["mb_xtr"], 1)

                    def cb(gr):
                        if gr >= 2:
                            pe.wait_ge(S["mb_W"], HPG * (gr - 1))
                        bT, cT_ = xcT[:, 16 + gr, :], xcT[:, 20 + gr, :]
                        mm(ps[:, 6 + gr % 2, 0:SEQ], bT[:, 0:P], cT_, start=True, stop=True)
                        mm(ps[:, 6 + gr % 2, SEQ:384], bT[:, P:SEQ], cT_[:, P:SEQ], start=True, stop=True)\
                            .then_inc(S["mb_cb"], 1)

                    def decay(h):
                        if h >= 2:
                            pe.wait_ge(S["mb_arg"], h - 1)
                        mm(ps[:, 4 + h % 2, 0:SEQ], ident[0:H_MB, h:h + 1].to_broadcast([H_MB, P]),
                           dtt[0:H_MB, 5, :], start=True, stop=True).then_inc(S["mb_ab"], 1)

                    for b in range(2):
                        pe.wait_ge(pj_free[b], pb + 10)
                    pe.wait_ge(S["mb_cols"], 1)
                    decay(0)
                    cb(0)
                    decay(1)
                    pe.wait_ge(S["mb_xs"], GROUPS)
                    for h in range(H_MB):
                        gr, hh = h // HPG, h % HPG
                        if hh == 0 and gr >= 2:
                            pe.wait_ge(S["mb_z"], 4 * (gr - 1))
                        if hh == 6 and gr + 1 < GROUPS:
                            cb(gr + 1)
                        pe.wait_ge(S["mb_W"], h + 1)
                        w0, w1, w2_ = (W_mb[:, h % 2, k * P:(k + 1) * P] for k in range(3))
                        o0, o1 = (ps[:, 2 * (gr % 2) + t, hh * HD:(hh + 1) * HD] for t in range(2))
                        x0, x1 = (xs[:, t, h * HD:(h + 1) * HD] for t in range(2))
                        mm(o0, w0, x0, start=True, stop=True)
                        mm(o1, w1, x0, start=True)
                        mm(o1, w2_, x1, stop=True).then_inc(S["mb_y"], 1)
                        if h + 2 < H_MB:
                            decay(h + 2)
                    pe.wait_ge(S["mb_yn"], 2 * GROUPS)
                    for k in range(16):
                        for t in range(T):
                            r = pe.transpose(ps[:, k // 2, (k % 2) * SEQ + t * P:(k % 2) * SEQ + (t + 1) * P],
                                             zs[:, t, k * P:(k + 1) * P], ident[:, :])
                        if k % 4 == 3:
                            r.then_inc(S["mb_tr"], 1)
                    for u in range(8):
                        pe.wait_ge(S["mb_lo"], max(u // 2 + 1, 2))
                        down(u % SLOTS, 2 * u, start=(u == 0), stop=(u == 7), done0=y_done[0] if u == 7 else None)
                if kind == "hy":
                    pe.wait_ge(S["pre_lo"], 2 * n + 2)
                    pb = PROJ_BEFORE[n]
                    project(14, False, pb)
                    project(2, True, pb + 14)
                    for b in range(2):
                        pe.wait_ge(pj_free[b], pb + 16)

                    def logits(h):
                        if h >= 2:
                            pe.wait_ge(S["hy_L"], h - 1)
                        q, k, b = hT[:, h, :], hT[:, 8 + h, :], 4 + h % 2
                        mm(ps[:, b, 0:P], q[:, 0:P], k[:, 0:P], start=True, stop=True)
                        mm(ps[:, b, P:384], q[:, P:SEQ], k, start=True, stop=True).then_inc(S["hy_sc"], 1)

                    logits(0)
                    logits(1)
                    for h in range(H_AT):
                        pe.wait_ge(S["hy_Pn"], h + 1)
                        if h:
                            pe.wait_ge(S["hy_ptc"], h)
                        for dst, src in ((0, 0), (1, 1), (2, 2)):
                            r = pe.transpose(ps[:, 6, dst * P:(dst + 1) * P], P_at[:, h % 2, src * P:(src + 1) * P],
                                             ident[:, :])
                        r.then_inc(S["hy_pt"], 1)
                        if h + 2 < H_AT:
                            logits(h + 2)
                        pe.wait_ge(S["hy_ptc"], h + 1)
                        if h >= 4:
                            pe.wait_ge(S["hy_at"], h - 3)
                        o = ps[:, h % 4, 0:SEQ]
                        mm(o, vh[:, 0, h * DH:(h + 1) * DH], L_at[:, h % 2, 0:SEQ], start=True)
                        mm(o[:, P:SEQ], vh[:, 1, h * DH:(h + 1) * DH], L_at[:, h % 2, SEQ:384], stop=True)\
                            .then_inc(S["hy_o"], 1)
                    pe.wait_ge(S["hy_L"], H_AT)
                    project(4, True, pb + 16)
                    pe.wait_ge(S["hy_alo"], 1)
                    for u in range(4):
                        down(u % SLOTS, 8 + 2 * u, start=(u == 0), stop=(u == 3))
                    pe.wait_ge(S["hy_clo"], 1)
                    pe.wait_ge(S["hy_ya"], 1)
                    for u in range(4, 8):
                        down(u % SLOTS, 2 * (u - 4), start=(u == 4), stop=(u == 7))
                    pe.wait_ge(S["hy_mg"], T)
                    for k in range(KT):
                        for t in range(T):
                            r = pe.transpose(ps[:, 4 + k // 2, (k % 2) * SEQ + t * P:(k % 2) * SEQ + (t + 1) * P],
                                             mg[:, t, k * P:(k + 1) * P], ident[:, :])
                        if k % 4 == 3:
                            r.then_inc(S["hy_mtr"], 1)
                    for u in range(8, 12):
                        pe.wait_ge(S["hy_mlo"], (u - 8) // 2 + 1)
                        down(u % SLOTS, 8 + 2 * (u - 8), start=(u == 8), stop=(u == 11),
                             done0=y_done[0] if u == 11 else None)

        @block.vector
        def _(dve):
            c = Count(S["acc_dve"])
            us = Uses(SLOTS)
            ua = Uses(2)

            def step(ins):
                c.on(ins)
                dve.wait_ge(c.sem, c.value())

            def mark(ins):
                c.on(ins)

            def lo(s):
                n = us.next(s)
                dve.wait_ge(w_hi[s], n + 1)
                dve.tensor_tensor(wlo[:, s, :], raw[:, s, :], whi[:, s, :].bitcast(F32), ALU.subtract)\
                   .then_inc(w_lo[s], 1)

            def ada(s, a, k0, after):
                n = ua.next(s)
                dve.wait_ge(a_in[s], 16 * n + 16)
                if after is not None:
                    dve.wait_ge(a_used[after[0]], after[1])
                sums = acc[:, bass.ds((a // 4) * D, D)]
                for kk in range(2):
                    r = dve.scalar_tensor_tensor(out=sums, in0=araw[:, s, kk * D:(kk + 1) * D],
                                                 scalar=cT[:, bass.ds((a % 4) * 2 + (k0 + kk), 1)], in1=sums,
                                                 op0=ALU.mult, op1=ALU.add)
                    if kk == 0:
                        step(r)
                r.then_inc(a_used[s], 1)

            def project(blocks, body=None, per=0):
                with dve.Fori(0, blocks) as i:
                    us.enter(i, blocks)
                    c.enter(i, per)
                    lo(0)
                    if body:
                        body(0, i)
                    lo(1)
                    if body:
                        body(1, i)
                    c.leave(blocks)
                    us.leave()

            def out_units(outs, more):
                for u in range(2, outs):
                    lo(u % SLOTS)
                if more:
                    lo(0)
                    lo(1)

            def mod_columns(k):
                r = ROW_MOD + 24 * k
                dve.wait_ge(S["mod_cols"], k + 1)
                mark(dve.tensor_tensor(shT[:, k, :], ps[:, 7, 0:8], cols[:, r:r + 8], ALU.add))
                step(dve.tensor_tensor(modc[:, :], ps[:, 7, 8:16], cols[:, r + 8:r + 16], ALU.add))
                dve.scalar_tensor_tensor(out=g1T[:, k, :], in0=modc[:, :], scalar=1.0, in1=cols[:, r + 16:r + 24],
                                         op0=ALU.add, op1=ALU.mult).then_inc(S["mods_ok"], 1)

            def mod_gate(k):
                dve.wait_ge(S["mod_gate"], k + 1)
                dve.wait_ge(S["brow_in"], 16 * k + 16)
                dve.tensor_tensor(gp[:, k % 2, :], ps[:, 4:6, :].rearrange("p a b -> p (a b)"), brow[:, 0, :], ALU.add)\
                   .then_inc(S["gate_read"], 1)
                dve.wait_ge(S["gate_read"], k + 1)
                if k < 6:
                    dve.scalar_tensor_tensor(out=gp[:, k % 2, :], in0=gp[:, k % 2, :],
                                             scalar=1.0 if k in (1, 4) else 0.5, in1=brow[:, 1, :],
                                             op0=ALU.mult, op1=ALU.mult).then_inc(S["gp_ok"], 1)
                else:
                    dve.tensor_copy(gp[:, k % 2, 0:1], gp[:, k % 2, 0:1]).then_inc(S["gp_ok"], 1)

            def log1p(e, u, ln, z, u_ok, ln_ok):
                dve.tensor_scalar(u, e, 1.0, None, ALU.add).then_inc(u_ok, 1)
                dve.wait_ge(u_ok, 1)
                step(dve.tensor_scalar(z, u, -1.0, 0.0, ALU.add, ALU.is_equal))
                dve.wait_ge(ln_ok, 1)
                step(dve.scalar_tensor_tensor(out=u, in0=u, scalar=-1.0, in1=z, op0=ALU.add, op1=ALU.add))
                step(dve.reciprocal(u, u))
                step(dve.tensor_tensor(u, u, e, ALU.mult))
                mark(dve.tensor_tensor(ln, ln, u, ALU.mult))
                step(dve.tensor_tensor(z, z, e, ALU.mult))
                step(dve.tensor_tensor(ln, ln, z, ALU.add))

            dve.wait_ge(S["cols_tr"], 1)
            dve.tensor_copy(cols[:, :], ps[:, 6, 0:ROWS]).then_inc(S["cols_ok"], 1)
            dve.wait_ge(S["wd_ps"], 1)
            dve.tensor_tensor(wdist[0:H_AT, :], ps[0:H_AT, 5, 0:REL], negr_sb[0:H_AT, :], ALU.add).then_inc(S["wd_ok"], 1)
            dve.wait_ge(S["c_ok"], 1)
            dve.wait_ge(S["zero_acc"], 1)
            last = None
            for a in range(12):
                ada(a % 2, a, 0, last)
                last = (a % 2, ua.n[a % 2])
                if a == 7:
                    lo(0)
                    lo(1)
            mod_columns(0)
            mod_gate(0)

            for n, kind in enumerate(KIND):
                xn = xn_of(n)
                if n == 0:
                    dve.wait_ge(S["x_in"], 16)
                for t in range(T):
                    dve.wait_ge(S["pre_rstd"], 2 * n + t + 1)
                    dve.tensor_scalar(xn[:, t, :], x[:, t, :], ssx[:, n, 2 + t:3 + t], None, ALU.mult)\
                       .then_inc(S["xn_ok"], 1)
                dve.wait_ge(S["mods_ok"], n + 1)
                for half in range(2):
                    dve.wait_ge(S["tr_ok"], 2 * n + half + 1)
                    for k in range(4 * half, 4 * half + 4):
                        r = dve.tensor_scalar(hf[:, k, :], ps[:, k // 2, (k % 2) * SEQ:(k % 2 + 1) * SEQ],
                                              g1T[:, n, k:k + 1], shT[:, n, k:k + 1], ALU.mult, ALU.add)
                    r.then_inc(S["pre_hf"], 1)
                for half in range(2):
                    dve.wait_ge(S["pre_hi"], 2 * n + half + 1)
                    s_ = slice(4 * half, 4 * half + 4)
                    dve.tensor_tensor(xlo[:, s_, :], hf[:, s_, :], xhi[:, s_, :].bitcast(F32), ALU.subtract)\
                       .then_inc(S["pre_lo"], 1)
                if n in (1, 4):
                    mod_columns(n + 1)
                    mod_gate(n + 1)
                if kind == "ffn":
                    f = FFN_NO[n]
                    b = NF * f
                    na = len(ADA_GROUPS[n])
                    k0 = 8 if ADA_GROUPS[n] == (6,) else 0

                    def gate_up(t, i):
                        dve.wait_ge(sil_ok[t], i + 1)
                        if t == 0:
                            dve.wait_ge(S["gt_ps"], i)
                        dve.tensor_tensor(g[:, t, :], sil[:, t, :], ps[:, 4 + t, FB:2 * FB], ALU.mult)\
                           .then_inc(g_ok[t], 1)

                    lo(0)
                    gate_up(0, b)
                    lo(1)
                    gate_up(1, b)
                    dve.wait_ge(S["zero_acc"], f + 2)
                    last = None
                    for a in range(ADA_PEEL[na]):
                        ada(a % 2, a, k0, last)
                        last = (a % 2, ua.n[a % 2])
                    dve.wait_ge(a_used[last[0]], last[1])
                    with dve.Fori(0, NF - 1) as i:
                        us.enter(i, NF - 1)
                        ua.enter(i, NF - 1)
                        c.enter(i, na)
                        lo(2)
                        before = (1, i + ua.n[1]) if na == 2 else (0, i + ua.n[0])
                        ada(0, i * na + ADA_PEEL[na], k0, before)
                        dve.wait_ge(S["gt_hi"], i + (b + 1))
                        dve.tensor_tensor(xlo[:, 8:10, :], ps[:, 6, :].rearrange("p (a b) -> p a b", b=SEQ),
                                          xhi[:, 8:10, :].bitcast(F32), ALU.subtract).then_inc(S["gt_lo"], 1)
                        lo(0)
                        gate_up(0, i + (b + 1))
                        gate_up(1, i + (b + 1))
                        lo(1)
                        if na == 2:
                            ada(1, i * na + (ADA_PEEL[na] + 1), k0, (0, i + (ua.n[0] - (NF - 1) + 1)))
                        c.leave(NF - 1)
                        ua.leave()
                        us.leave()
                    dve.wait_ge(S["gt_hi"], b + NF)
                    dve.tensor_tensor(xlo[:, 8:10, :], ps[:, 6, :].rearrange("p (a b) -> p a b", b=SEQ),
                                      xhi[:, 8:10, :].bitcast(F32), ALU.subtract).then_inc(S["gt_lo"], 1)
                    lo(2)
                    mod_columns(ADA_GROUPS[n][0])
                    mod_gate(ADA_GROUPS[n][0])
                if kind == "ml":
                    G = lambda j: gt[0:4, j, :]
                    dve.wait_ge(S["ml_gate"], 1)
                    dve.wait_ge(S["mlc_in"], 64)
                    step(dve.tensor_scalar(G(1), ps[32:36, 7, 0:SEQ], mlb_sb[32:36, :], None, ALU.add))
                    mark(dve.tensor_scalar(G(0), ps[0:4, 7, 0:SEQ], mlb_sb[0:4, :], None, ALU.add))
                    dve.scalar_tensor_tensor(out=G(2), in0=G(1), scalar=-1.0, in1=G(1), op0=ALU.mult, op1=ALU.min)\
                       .then_inc(S["ml_na"], 1)
                    dve.wait_ge(S["ml_e"], 1)
                    log1p(G(3), G(4), G(5), G(6), S["ml_u"], S["ml_l"])
                    step(dve.scalar_tensor_tensor(out=G(6), in0=G(1), scalar=0.0, in1=G(5), op0=ALU.min, op1=ALU.subtract))
                    step(dve.tensor_tensor_scan(G(7), ones[0:4, :], G(6), 0.0, ALU.mult, ALU.add))
                    step(dve.tensor_tensor(G(8), G(0), G(7), ALU.subtract))
                    step(dve.tensor_tensor_scan(G(4), G(8), G(8), 0.0, ALU.max, ALU.max))
                    dve.tensor_tensor(G(2), G(4), G(7), ALU.add).then_inc(S["ml_rows"], 1)
                    dve.wait_ge(S["ml_em"], 1)
                    dve.tensor_scalar(G(2), G(4), -1.0, None, ALU.mult).then_inc(S["ml_rows"], 1)
                    project(2)
                    dve.wait_ge(S["ml_ct"], 1)
                    dve.tensor_copy(colm[:, :, :], ps[:, 7, 256:272].rearrange("p (a b) -> p a b", b=8))\
                       .then_inc(S["ml_cols"], 1)
                    project(4)
                    dve.wait_ge(S["ml_cols"], 1)

                    def exponent(h):
                        dve.wait_ge(S["ml_nm"], h + 1)
                        if h >= 2:
                            dve.wait_ge(S["ml_nd"], h - 1)
                        e, q = E_ml[:, h % 2, :], ps[:, 6 + h % 2, 0:SEQ]
                        dve.scalar_tensor_tensor(out=e[:, 0:SEQ], in0=q, scalar=colm[:, 0, h:h + 1], in1=mask[:, :],
                                                 op0=ALU.add, op1=ALU.min)
                        dve.scalar_tensor_tensor(out=e[:, SEQ:384], in0=q[:, P:SEQ], scalar=colm[:, 1, h:h + 1],
                                                 in1=mask[:, 0:P], op0=ALU.add, op1=ALU.min).then_inc(S["ml_arg"], 1)

                    dve.wait_ge(S["const"], 5)
                    exponent(0)
                    for h in range(H_ML):
                        if h + 1 < H_ML:
                            exponent(h + 1)
                        dve.wait_ge(S["ml_E"], h + 1)
                        dve.wait_ge(S["ml_sc"], h + 1)
                        dve.scalar_tensor_tensor(out=E_ml[:, h % 2, :], in0=E_ml[:, h % 2, :], scalar=DK ** -0.5,
                                                 in1=ps[:, 4 + h % 2, 0:384], op0=ALU.mult, op1=ALU.mult)\
                           .then_inc(S["ml_ST"], 1)
                    dve.wait_ge(S["ml_nd"], H_ML)
                    step(dve.tensor_copy(sm[:, 0, :], ps[:, 7, 300:308]))
                    step(dve.scalar_tensor_tensor(out=sm[:, 1, :], in0=sm[:, 0, :], scalar=-1.0, in1=sm[:, 0, :],
                                                  op0=ALU.mult, op1=ALU.max))
                    step(dve.tensor_tensor(sm[:, 1, :].rearrange("p (a b) -> p a b", b=4),
                                           sm[:, 1, :].rearrange("p (a b) -> p a b", b=4), colm[:, :, 4:8], ALU.max))
                    dve.reciprocal(sm[:, 2, :], sm[:, 1, :]).then_inc(S["ml_r"], 1)
                    dve.wait_ge(S["ml_r"], 1)
                    dve.wait_ge(S["ml_rs"], 1)
                    step(dve.tensor_tensor(sm[:, 5, :], sm[:, 2, :], sm[:, 4, :], ALU.mult))
                    dve.wait_ge(S["ml_row_free"], 4)
                    for t in range(T):
                        for h in range(H_ML):
                            v_ = slice(h * DV, (h + 1) * DV)
                            dve.scalar_tensor_tensor(out=am[:, t, v_], in0=ps[:, 2 * t + h // 2, (h % 2) * DV:(h % 2 + 1) * DV],
                                                     scalar=sm[:, 5, 4 * t + h:4 * t + h + 1], in1=og[:, t, v_],
                                                     op0=ALU.mult, op1=ALU.mult).then_inc(S["ml_am"], 1)
                    for q in range(2):
                        dve.wait_ge(S["ml_hi"], q + 1)
                        dve.tensor_tensor(xlo[:, 4 * q:4 * q + 4, :], ps[:, 4 + 2 * q:6 + 2 * q, :].rearrange(
                            "p a (c b) -> p (a c) b", b=SEQ), xhi[:, 4 * q:4 * q + 4, :].bitcast(F32), ALU.subtract)\
                           .then_inc(S["ml_lo"], 1)
                    out_units(4, True)
                if kind == "mb":
                    R = lambda j: dtt[0:H_MB, j, :]
                    dve.wait_ge(S["mb_gate"], 1)
                    dve.wait_ge(S["mbc_in"], 48)
                    step(dve.tensor_scalar(R(0), ps[0:H_MB, 7, 0:SEQ], mbv_sb[:, 0:1], None, ALU.add))
                    dve.scalar_tensor_tensor(out=R(1), in0=R(0), scalar=-1.0, in1=R(0), op0=ALU.mult, op1=ALU.min)\
                       .then_inc(S["mb_na"], 1)
                    dve.wait_ge(S["mb_e"], 1)
                    log1p(R(2), R(3), R(4), R(5), S["mb_u"], S["mb_l"])
                    step(dve.scalar_tensor_tensor(out=R(3), in0=R(0), scalar=0.0, in1=R(4), op0=ALU.max, op1=ALU.add))
                    dve.wait_ge(S["mb_eA"], 1)
                    step(dve.tensor_scalar(R(1), R(3), sg[0:H_MB, 0, 0:1], -1.0, ALU.mult, ALU.mult))
                    dve.tensor_tensor_scan(R(5), ones[0:H_MB, :], R(1), 0.0, ALU.mult, ALU.add).then_inc(S["mb_rows"], 1)
                    project(4)
                    dve.wait_ge(S["mb_ct"], 1)
                    mark(dve.tensor_scalar(colb[:, 0:2, :], ps[:, 7, 256:320].rearrange("p (a b) -> p a b", b=H_MB),
                                           -1.0, None, ALU.mult))
                    dve.tensor_copy(colb[:, 2:4, :], ps[:, 7, 320:384].rearrange("p (a b) -> p a b", b=H_MB))\
                       .then_inc(S["mb_cols"], 1)

                    def convolve(b, i):
                        dve.wait_ge(pj_free[b], i + (PROJ_BEFORE[4] + 5))
                        for j in range(3):
                            sh = 3 - j
                            for q in (2 * b, 2 * b + 1):
                                r = dve.scalar_tensor_tensor(
                                    out=cacc[:, q, sh:SEQ], in0=cin[:, q, 0:SEQ - sh],
                                    scalar=cols[:, bass.ds(i * 4 + (ROW_MBW + j * CONV_F + q), 1)],
                                    in1=cacc[:, q, sh:SEQ], op0=ALU.mult, op1=ALU.add)
                                if j < 2:
                                    if q % 2:
                                        step(r)
                                    else:
                                        mark(r)
                                elif q % 2 == 0:
                                    mark(r)
                        r.then_inc(S["mb_conv"], 1)

                    project(6, convolve, 10)

                    def exponent(h):
                        dve.wait_ge(S["mb_ab"], h + 1)
                        e, q = E_mb[:, h % 2, :], ps[:, 4 + h % 2, 0:SEQ]
                        dve.scalar_tensor_tensor(out=e[:, 0:SEQ], in0=q, scalar=colb[:, 0, h:h + 1], in1=mask[:, :],
                                                 op0=ALU.add, op1=ALU.min)
                        dve.scalar_tensor_tensor(out=e[:, SEQ:384], in0=q[:, P:SEQ], scalar=colb[:, 1, h:h + 1],
                                                 in1=mask[:, 0:P], op0=ALU.add, op1=ALU.min).then_inc(S["mb_arg"], 1)

                    def finish(gr):
                        dve.wait_ge(S["mb_y"], HPG * (gr + 1))
                        s_ = slice(gr * 512, (gr + 1) * 512)
                        for t in range(T):
                            dve.wait_ge(S["mb_xd"], 2 * gr + t + 1)
                            dve.tensor_tensor(xd[:, t, :], ps[:, 2 * (gr % 2) + t, :], xd[:, t, :], ALU.add)\
                               .then_inc(S["mb_z"], 1)
                            dve.wait_ge(S["mb_z"], 4 * gr + 2 * t + 1)
                            dve.tensor_tensor(zs[:, t, s_], xd[:, t, :], zs[:, t, s_], ALU.mult).then_inc(S["mb_z"], 1)

                    def normed(gr):
                        dve.wait_ge(S["mb_rs"], gr + 1)
                        dve.wait_ge(S["nwm_in"], 16)
                        s_ = slice(gr * 512, (gr + 1) * 512)
                        for t in range(T):
                            dve.scalar_tensor_tensor(out=zs[:, t, s_], in0=zs[:, t, s_],
                                                     scalar=sg[:, 1, 2 * gr + t:2 * gr + t + 1], in1=nwm[:, s_],
                                                     op0=ALU.mult, op1=ALU.mult).then_inc(S["mb_yn"], 1)

                    dve.wait_ge(S["mb_cols"], 1)
                    exponent(0)
                    for h in range(H_MB):
                        if h + 1 < H_MB:
                            exponent(h + 1)
                        dve.wait_ge(S["mb_E"], h + 1)
                        dve.wait_ge(S["mb_cb"], h // HPG + 1)
                        if h >= 2:
                            dve.wait_ge(S["mb_y"], h - 1)
                        e, w, q = E_mb[:, h % 2, :], W_mb[:, h % 2, :], ps[:, 6 + (h // HPG) % 2, :]
                        dve.scalar_tensor_tensor(out=w[:, 0:SEQ], in0=e[:, 0:SEQ], scalar=colb[:, 2, h:h + 1],
                                                 in1=q[:, 0:SEQ], op0=ALU.mult, op1=ALU.mult)
                        dve.scalar_tensor_tensor(out=w[:, SEQ:384], in0=e[:, SEQ:384], scalar=colb[:, 3, h:h + 1],
                                                 in1=q[:, SEQ:384], op0=ALU.mult, op1=ALU.mult).then_inc(S["mb_W"], 1)
                        if h % HPG == 1 and h > HPG:
                            finish(h // HPG - 1)
                        if h % HPG == 6 and h > HPG:
                            normed(h // HPG - 1)
                    finish(GROUPS - 1)
                    normed(GROUPS - 1)
                    for q in range(4):
                        dve.wait_ge(S["mb_hi"], q + 1)
                        dve.tensor_tensor(xlo[:, 4 * q:4 * q + 4, :], ps[:, 2 * q:2 * q + 2, :].rearrange(
                            "p a (c b) -> p (a c) b", b=SEQ), xhi[:, 4 * q:4 * q + 4, :].bitcast(F32), ALU.subtract)\
                           .then_inc(S["mb_lo"], 1)
                    out_units(8, True)
                if kind == "hy":
                    project(16)

                    def logits(h):
                        dve.wait_ge(S["hy_sc"], h + 1)
                        if h >= 2:
                            dve.wait_ge(S["hy_o"], h - 1)
                        L, q, st = L_at[:, h % 2, :], ps[:, 4 + h % 2, :], stat[:, h, :]
                        mark(dve.scalar_tensor_tensor(out=L[:, 0:P], in0=q[:, 0:P], scalar=DH ** -0.5,
                                                      in1=bm[:, h, P:SEQ], op0=ALU.mult, op1=ALU.add))
                        step(dve.scalar_tensor_tensor(out=L[:, P:384], in0=q[:, P:384], scalar=DH ** -0.5,
                                                      in1=bm[:, h, :], op0=ALU.mult, op1=ALU.add))
                        mark(dve.tensor_reduce(st[:, 0:1], L[:, 0:P], AX, ALU.max))
                        step(dve.tensor_reduce(st[:, 1:2], L[:, P:384], AX, ALU.max))
                        dve.tensor_scalar(st[:, 2:4], st[:, 0:2], -1.0, None, ALU.mult).then_inc(S["hy_L"], 1)

                    def weigh(h):
                        dve.wait_ge(S["hy_o"], h + 1)
                        dve.tensor_tensor(hT[:, 16 + h, :], ps[:, h % 4, 0:SEQ], hT[:, 16 + h, :],
                                          ALU.mult).then_inc(S["hy_at"], 1)

                    dve.wait_ge(S["hy_bm"], 4)
                    logits(0)
                    for h in range(H_AT):
                        if h + 1 < H_AT:
                            logits(h + 1)
                        dve.wait_ge(S["hy_P"], 2 * h + 2)
                        pr, st = P_at[:, h % 2, :], stat[:, h, :]
                        step(dve.reciprocal(st[:, 6:8], st[:, 4:6]))
                        mark(dve.tensor_scalar(pr[:, 0:P], pr[:, 0:P], st[:, 6:7], None, ALU.mult))
                        dve.tensor_scalar(pr[:, P:384], pr[:, P:384], st[:, 7:8], None, ALU.mult).then_inc(S["hy_Pn"], 1)
                        if h:
                            weigh(h - 1)
                    weigh(H_AT - 1)
                    dve.wait_ge(S["hy_ga"], 1)
                    dve.tensor_tensor(xlo[:, 8:16, :], hT[:, 16:24, :], xhi[:, 8:16, :].bitcast(F32), ALU.subtract)\
                       .then_inc(S["hy_alo"], 1)

                    def short_conv(b, i):
                        if b == 0:
                            return
                        tile = lambda o: hT[:, bass.ds(i * 2 + o, 2), :]
                        u, y = tile(32), tile(40)
                        step(dve.tensor_tensor(u, u, y, ALU.mult))
                        for j in (2, 1, 0):
                            sh = 2 - j
                            for q in range(2):
                                w_ = cols[:, bass.ds(i * 2 + (ROW_HYW + j * 8 + q), 1)]
                                yq = hT[:, bass.ds(i * 2 + (40 + q), 1), sh:SEQ].rearrange("p a b -> p (a b)")
                                uq = hT[:, bass.ds(i * 2 + (32 + q), 1), 0:SEQ - sh].rearrange("p a b -> p (a b)")
                                if j == 2:
                                    r = dve.tensor_scalar(yq, uq, w_, None, ALU.mult)
                                else:
                                    r = dve.scalar_tensor_tensor(out=yq, in0=uq, scalar=w_, in1=yq,
                                                                 op0=ALU.mult, op1=ALU.add)
                                (step if q else mark)(r)
                        step(dve.tensor_tensor(y, y, tile(24), ALU.mult))
                        dve.tensor_tensor(y, y, tile(48), ALU.mult).then_inc(S["hy_cv"], 1)

                    project(4, short_conv, 8)
                    dve.wait_ge(S["hy_chi"], 1)
                    dve.tensor_tensor(xlo[:, 0:8, :], hT[:, 40:48, :], xhi[:, 0:8, :].bitcast(F32), ALU.subtract)\
                       .then_inc(S["hy_clo"], 1)
                    for u in range(2, 4):
                        lo(u % SLOTS)
                    tot = used_before_hy
                    lo(4 % SLOTS)
                    dve.wait_ge(w_used[3 % SLOTS], tot[0] + 20 + 2)
                    for t in range(T):
                        r = dve.tensor_tensor(mg[:, t, :], ps[:, 2 * t:2 * t + 2, :].rearrange("p a b -> p (a b)"),
                                              sgm[:, t, 0:D], ALU.mult)
                        if t == 0:
                            mark(r)
                    r.then_inc(S["hy_ya"], 1)
                    dve.wait_ge(S["hy_ya"], 1)
                    for u in range(5, 8):
                        lo(u % SLOTS)
                    dve.wait_ge(w_used[7 % SLOTS], tot[1] + 20 + 3)
                    for t in range(T):
                        step(dve.tensor_tensor(sgm[:, t, D:2 * D], ps[:, 2 * t:2 * t + 2, :]
                                               .rearrange("p a b -> p (a b)"), sgm[:, t, D:2 * D], ALU.mult))
                        dve.tensor_tensor(mg[:, t, :], mg[:, t, :], sgm[:, t, D:2 * D], ALU.add).then_inc(S["hy_mg"], 1)
                    for q in range(2):
                        dve.wait_ge(S["hy_mhi"], q + 1)
                        dve.tensor_tensor(xlo[:, 8 + 4 * q:12 + 4 * q, :], ps[:, 4 + 2 * q:6 + 2 * q, :].rearrange(
                            "p a (c b) -> p (a c) b", b=SEQ), xhi[:, 8 + 4 * q:12 + 4 * q, :].bitcast(F32), ALU.subtract)\
                           .then_inc(S["hy_mlo"], 1)
                    for u in range(8, 12):
                        lo(u % SLOTS)
                    yb = vh
                    for t in range(T):
                        wait_y(dve, n, t)
                        step(dve.tensor_tensor(yb[:, t, :], ps[:, 2 * t:2 * t + 2, :].rearrange("p a b -> p (a b)"),
                                               gp[:, n % 2, :], ALU.mult))
                        dve.tensor_tensor(x[:, t, :], x[:, t, :], yb[:, t, :], ALU.add).then_inc(S["hy_fx"], 1)
                    dve.wait_ge(S["fg_in"], 16)
                    for t in range(T):
                        dve.wait_ge(S["hy_fr"], t + 1)
                        dve.scalar_tensor_tensor(out=yb[:, t, :], in0=x[:, t, :], scalar=ssx[:, n, 6 + t:7 + t],
                                                 in1=gp[:, 1, :], op0=ALU.mult, op1=ALU.mult).then_inc(S["hy_out"], 1)
                else:
                    yb = m(16000, T, D)
                    for t in range(T):
                        dve.wait_ge(S["post_rstd"], 2 * n + t + 1)
                        step(dve.scalar_tensor_tensor(out=yb[:, t, :], in0=ps[:, 2 * t:2 * t + 2, :]
                                                      .rearrange("p a b -> p (a b)"), scalar=ssx[:, n, 6 + t:7 + t],
                                                      in1=gp[:, n % 2, :], op0=ALU.mult, op1=ALU.mult))
                        dve.tensor_tensor(x[:, t, :], x[:, t, :], yb[:, t, :], ALU.add).then_inc(x_new[t], 1)


def _halves(w):
    k, n = w.shape
    return w.reshape(2, 4, P, n // 512, 512).transpose(3, 0, 2, 1, 4).reshape(-1, P, UNIT)


def _pairs(w):
    return w.reshape(-1, 2, P, D).transpose(0, 2, 1, 3).reshape(-1, P, UNIT)


def _ffn_units(w1, w3, w2):
    up = np.concatenate([w1.reshape(D, NF, 1, FB), w3.reshape(D, NF, 1, FB)], 2).reshape(D, NF * 512)
    up, dn = _halves(up).reshape(NF, 2, P, UNIT), _pairs(w2)
    return up, dn


def _stream(stages):
    out = [stages[0][1]]
    for j, (kind, _, rest) in enumerate(stages):
        nxt = stages[j + 1][1] if j + 1 < len(stages) else None
        if kind == "ffn":
            up, dn = rest
            out.append(up[1])
            for i in range(NF - 1):
                out.append(dn[i:i + 1])
                out.append(up[i + 2] if i + 2 < NF else nxt)
            out.append(dn[NF - 1:NF])
        else:
            out.append(rest)
            if nxt is not None:
                out.append(nxt)
    return np.concatenate(out)


def kernel(**inputs):
    import concourse.bacc as _bacc
    from concourse.bass_utils import run_bass_kernel_spmd as _run

    a = {k: np.asarray(v) for k, v in inputs.items()}
    f32 = np.float32
    stages = []
    for layer in range(2):
        ffn = [_ffn_units(a["ffn_w1"][layer, s], a["ffn_w3"][layer, s], a["ffn_w2"][layer, s]) for s in range(2)]
        if layer == 0:
            w = a["ml_w_in"][0]
            mix = np.concatenate([_halves(w[:, :3072]), _pairs(a["ml_w_out"][0])])
        else:
            w = a["mb_w_in"][0]
            mix = np.concatenate([_halves(w[:, :5120]), _pairs(a["mb_w_out"][0])])
        stages += [("ffn", ffn[0][0][0], ffn[0]), ("mix", mix[:2], mix[2:]), ("ffn", ffn[1][0][0], ffn[1])]
    w = a["w_in_2"][0]
    order = [w[:, 0:2048], w[:, 3072:8192], w[:, 2048:3072], w[:, 8192:10240]]
    hy = np.concatenate([_halves(v) for v in order] + [_pairs(a[k][0]) for k in ("w_o_attn_2", "w_o_conv_2", "w_out_2")])
    stages.append(("mix", hy[:2], hy[2:]))
    units = _stream(stages)

    def ada(w, n):
        return w.reshape(4, 2, P, 3 * n, D).transpose(3, 0, 2, 1, 4).reshape(-1, P, UNIT)

    ada_units = np.concatenate([ada(a["ada_w"][0], 3), ada(a["ada_w"][1], 3), ada(a["w_ada_2"][0], 1)])
    adab = np.concatenate([a["ada_b"].reshape(6, 3, D), a["b_ada_2"].reshape(1, 3, D)])
    pre = np.concatenate([a["norm_pre"].reshape(6, 1, D), a["norm_g_2"].reshape(1, 1, D)])
    rows = np.concatenate([
        np.concatenate([adab[:, 0:2], pre], 1).reshape(-1, P),
        a["c"].reshape(-1, P), a["c_2"].reshape(-1, P),
        a["mb_conv_w"].reshape(-1, P), a["mb_conv_b"].reshape(-1, P), a["conv_w_2"].reshape(-1, P)])
    rows = np.concatenate([rows, np.zeros((ROWS - rows.shape[0], P), f32)])
    post = np.concatenate([a["norm_post"].reshape(6, D), a["final_g_2"].reshape(1, D)])
    bcast = np.stack([adab[:, 2], post], 1).reshape(1, -1)
    mlw = np.zeros((D, 36), f32)
    mlw[:, 0:4], mlw[:, 32:36] = a["ml_w_in"][0][:, 3072:3076], a["ml_w_in"][0][:, 3076:3080]
    mlw = mlw.reshape(KT, P, 36).transpose(1, 0, 2)
    mbw = a["mb_w_in"][0][:, 5120:].reshape(KT, P, H_MB).transpose(1, 0, 2)
    dist = 255 - np.arange(REL)
    big = 16 + (np.log(np.maximum(dist, 1).astype(f32) / f32(16)) / f32(np.log(8.0)) * f32(16)).astype(np.int32)
    bucket = np.where(dist < 16, np.maximum(dist, 0), np.minimum(big, 31))
    onehot = ((bucket[None, :] == np.arange(32)[:, None]) & (dist >= 0)[None, :]).astype(f32)
    negrow = np.broadcast_to(np.where(dist >= 0, 0.0, NEG).astype(f32), (H_AT, REL))
    arrays = dict(
        x_in=a["x"].reshape(SEQ, D), units=units, ada_units=ada_units, rows=rows, bcast=bcast, mlw=mlw,
        mlb=a["ml_b_gate"].reshape(8, 1), mbw=mbw, mbv=np.stack([a["mb_dt_bias"][0], a["mb_A_log"][0]], 1),
        mbd=a["mb_D"].reshape(1, H_MB), nw_ml=a["ml_norm_w"].reshape(1, D), nw_mb=a["mb_norm_w"].reshape(1, DI),
        rel=a["rel_bias_2"], onehot=onehot, negrow=negrow)
    arrays = {k: np.ascontiguousarray(v) for k, v in arrays.items()}
    nc = _bacc.Bacc("TRN2", target_bir_lowering=False, num_devices=1)
    args = [nc.dram_tensor(k, v.shape, mybir.dt.from_np(v.dtype), kind="ExternalInput").ap() for k, v in arrays.items()]
    out = nc.dram_tensor("out", (SEQ, D), F32, kind="ExternalOutput").ap()
    build(nc, *args, out)
    r = _run(nc, [arrays], core_ids=[0])
    return r.results[0]["out"].reshape(1, SEQ, D)
```

```python
import numpy as np
from contextlib import ExitStack

import concourse.bass as bass
from concourse import mybir

F32 = mybir.dt.float32
F32R = mybir.dt.float32r
BF16 = mybir.dt.bfloat16
ALU = mybir.AluOpType
ACT = mybir.ActivationFunctionType
AX = mybir.AxisListType.X

P = 128
D = 1024
SEQ = 256
T = SEQ // P
KT = D // P
F = 2816
FB = 256
NF = F // FB
UNIT = 2048
SLOTS = 3
EPS = 1e-6
NEG = -1e30

H_ML, DK, DV = 4, 128, 256
H_MB, HD, GROUPS, HPG, DI = 32, 64, 4, 8, 2048
CONV_F = 24
H_AT, DH = 8, 128
REL = 384

STAGES = 7

ROW_MOD = 0
ROW_C = ROW_MOD + 7 * 24
ROW_MBW = ROW_C + 16
ROW_HYW = ROW_MBW + 5 * CONV_F
ROWS = 384
assert ROW_HYW + 24 <= ROWS

ADA_PLAN = {0: (8, 2, 4), 2: (36, 0, 2), 3: (48, 4, NF - 1), 5: (72, 0, 2)}
ADA_ML = 24


class Count:

    def __init__(self, sem):
        self.sem, self.n, self.i, self.per = sem, 0, None, 0

    def on(self, ins, k=1):
        ins.then_inc(self.sem, k)
        self.n += k
        return ins

    def value(self):
        return self.n if self.i is None else self.i * self.per + self.n

    def enter(self, i, per):
        self.i, self.per, self.first = i, per, self.n

    def leave(self, steps):
        assert self.n - self.first == self.per, (self.n - self.first, self.per)
        self.n, self.i = self.first + self.per * steps, None


class Uses:

    def __init__(self, n):
        self.n, self.i, self.steps = [0] * n, None, 0

    def next(self, s):
        n = self.n[s] if self.i is None else self.i + self.n[s]
        self.n[s] += 1 if self.i is None else self.steps
        return n

    def enter(self, i, steps):
        self.i, self.steps = i, steps

    def leave(self):
        self.i = None


def build(nc, x_in, units, ada_units, rows, bcast, mlw, mlb, mbw, mbv, mbd, nw_ml, nw_mb, rel, onehot,
          negrow, out):
    scratch = nc.dram_tensor("bias_by_distance", (H_AT, REL), F32).ap()
    ctx = ExitStack()
    with ctx:
        def sb(name, shape, dt=F32):
            return ctx.enter_context(nc.sbuf_tensor(name, shape, dt))

        def sem(name):
            return ctx.enter_context(nc.semaphore(name))

        raw = sb("raw", [P, SLOTS, UNIT])
        whi = sb("whi", [P, SLOTS, UNIT], F32R)
        wlo = sb("wlo", [P, SLOTS, UNIT], F32R)
        xhi = sb("xhi", [P, 16, SEQ], F32R)
        xlo = sb("xlo", [P, 16, SEQ], F32R)
        hf = sb("hf", [P, KT, SEQ])
        x = sb("x", [P, T, D])
        gp = sb("gp", [P, 2, D])
        cols = sb("cols", [P, ROWS])
        cT = sb("cT", [P, 16])
        shT = sb("shT", [P, 7, KT])
        g1T = sb("g1T", [P, 7, KT])
        modc = sb("modc", [P, KT])
        ident = sb("ident", [P, P])
        ones = sb("ones", [P, SEQ])
        zero = sb("zero", [1, 512], BF16)
        negh = sb("negh", [P, 8])
        ssx = sb("ssx", [P, 8, 8])
        base = sb("base", [P, 8])
        mask = sb("mask", [P, SEQ])
        WORDS = 18432
        M = sb("M", [P, WORDS])
        ps = ctx.enter_context(nc.psum_tensor("ps", [P, 8, 512], F32))

        def m(off, *shape):
            n = int(np.prod(shape))
            assert off + n <= WORDS, off + n
            ap = M[:, off:off + n]
            return ap.rearrange("p (a b) -> p a b", b=shape[1]) if len(shape) == 2 else ap

        acc = m(0, 6144)
        araw = m(6144, 2, UNIT)
        brow = m(10240, 2, D)
        sil = m(12288, T, FB)
        g = m(12800, T, FB)
        qkT = m(0, 8, SEQ)
        vv = m(2048, T, D)
        og = m(4096, T, D)
        am = m(0, T, D)
        acc2 = m(6144, 3072)
        araw2 = [m(16000, UNIT), hf[:, :, :].rearrange("p a b -> p (a b)")]
        brow2 = m(4096, 2, D)
        ml_junk = m(9216, 8, DV)
        E_ml = m(9216, H_ML, 384)
        gt = m(10752, 9, SEQ)
        colm = m(13056, T, 8)
        sm = m(13072, 8, 8)
        nwl = m(13312, D)
        mlw_sb = m(14336, KT, 36)
        mlb_sb = m(14624, 1)
        zs = m(0, T, DI)
        xcT = m(4096, CONV_F, SEQ)
        xs = m(10240, T, DI)
        cin = m(10240, 4, SEQ)
        cacc = m(11264, 4, SEQ)
        dtt = m(14336, 6, SEQ)
        colb = m(15872, 4, H_MB)
        nwm = m(16000, DI)
        xd = m(4096, T, 512)
        xj = m(5120, T, 512)
        mbw_sb = sb("mbw_sb", [P, KT, H_MB])
        mbd_sb = sb("mbd_sb", [P, H_MB])
        mbv_sb = sb("mbv_sb", [H_MB, 2])
        sg = sb("sg", [P, 2, 8])
        hfl = hf[:, :, :].rearrange("p a b -> p (a b)")
        E_mb = hfl[:, 0:1536].rearrange("p (a b) -> p a b", b=768)
        W_mb = m(6144, 2, 768)
        hT = m(0, 56, SEQ)
        vh = m(14336, T, D)
        bm = m(16384, H_AT, SEQ)
        bmr = m(4096, H_AT, SEQ)
        sgm = m(0, T, 2 * D)
        mg = m(6144, T, D)
        L_at = hfl[:, 0:768].rearrange("p (a b) -> p a b", b=384)
        P_at = hfl[:, 768:1536].rearrange("p (a b) -> p a b", b=384)
        stat = sb("stat", [P, H_AT, 8])
        wdist = m(15200, REL)
        rel_sb = m(15600, H_AT)
        oneh_sb = m(17024, REL)
        negr_sb = m(17408, REL)
        vrow = m(14712, 3, P)
        jrev = m(8192, P)

        def yb_of(n):
            return m(2048, T, D) if n == 1 else m(16000, T, D)

        def xn_of(n):
            return m(6144, T, D) if n == 6 else m(16000, T, D)

        w_in = [sem(f"w_in{s}") for s in range(SLOTS)]
        w_hi = [sem(f"w_hi{s}") for s in range(SLOTS)]
        w_lo = [sem(f"w_lo{s}") for s in range(SLOTS)]
        w_used = [sem(f"w_used{s}") for s in range(SLOTS)]
        a_in = [sem(f"a_in{s}") for s in range(2)]
        a_used = [sem(f"a_used{s}") for s in range(2)]
        names = """x_in rows_in bias_in mlc_in mbc_in nwm_in scratch_in scratch_out bmr_in out_in brow_in brow2_in zero_acc2
            const zero_acc cols_tr cols_ok c_ok wd_ps wd_ok  acc_act acc_dve acc_pool
            post_ss post_rstd pre_ss pre_rstd xn_ok tr_ok pre_hf pre_hi pre_lo
            mod_cols mod_gate mods_ok gate_read gp_ok
            gt_ps gt_hi gt_lo
            ml_gate ml_na ml_e ml_u ml_l ml_rows ml_em ml_ct ml_cols ml_sc ml_nm ml_arg ml_E ml_ST ml_nd
            ml_r ml_ss ml_rs ml_am ml_tr ml_hi ml_lo ml_gw ml_og ml_den
            mb_gate mb_na mb_e mb_u mb_l mb_eA mb_rows mb_ct mb_cols mb_cv0 mb_conv mb_silu mb_xtr mb_xs
            mb_cb mb_ab mb_arg mb_E mb_W mb_y mb_xd mb_z mb_zs mb_add mb_ss mb_rs mb_yn mb_tr mb_hi mb_lo
            hy_flip hy_bm hy_sc hy_L hy_P hy_Pn hy_pt hy_ptc hy_o hy_at hy_ga hy_alo  hy_cv hy_chi hy_clo
            hy_ya  hy_mg hy_mtr hy_mhi hy_mlo hy_fx hy_fs hy_fr hy_out hy_gs fg_in""".split()
        S = {k: sem(k) for k in names}
        y_done = [sem(f"y_done{t}") for t in range(T)]
        x_new = [sem(f"x_new{t}") for t in range(T)]
        s1_ok = [sem(f"s1_ok{t}") for t in range(T)]
        sil_ok = [sem(f"sil_ok{t}") for t in range(T)]
        g_ok = [sem(f"g_ok{t}") for t in range(T)]
        pj_ok = [sem(f"pj_ok{b}") for b in range(2)]
        pj_free = [sem(f"pj_free{b}") for b in range(2)]

        KIND = ["ffn", "ml", "ffn", "ffn", "mb", "ffn", "hy"][:STAGES]
        FFN_NO = {0: 0, 2: 1, 3: 2, 5: 3}
        PROJ_BEFORE = {1: 0, 4: 6, 6: 16}

        block = ctx.enter_context(nc.Block())

        CREDIT = [0, 0, 1]
        ONE = 1

        LAST, used = {}, [0] * SLOTS
        for n_, kind_ in enumerate(KIND):
            if kind_ == "ffn":
                used = [u + NF for u in used]
                LAST[n_] = (2, used[2] + CREDIT[2])
            else:
                if kind_ == "hy":
                    used_before_hy = list(used)
                blocks, outs = {"ml": (6, 4), "mb": (10, 8), "hy": (20, 12)}[kind_]
                used[0] += blocks
                used[1] += blocks
                for u in range(outs):
                    used[u % SLOTS] += 1
                s_ = (outs - 1) % SLOTS
                LAST[n_] = (s_, used[s_] + CREDIT[s_])

        def wait_y(eng, n, t):
            if t == 0:
                eng.wait_ge(y_done[0], n + 1)
            else:
                eng.wait_ge(w_used[LAST[n][0]], LAST[n][1])

        GATES_BEFORE = [0, 2, 3, 4, 6, 6, 7]

        def ada_steps(n):
            two = ADA_PLAN[n][2]
            return [(f_, k_, p_) for f_, k_, p_ in ((0, two, 2), (two, NF - 1 - two, 1)) if k_]

        A_TOTAL = {"start": (4, 4)}
        at = [4, 4]
        for n_ in (0, 1, 2, 3, 5):
            if n_ == 1:
                at = [at[0] + 8, at[1] + 4]
            else:
                _, before_, two = ADA_PLAN[n_]
                at = [at[0] + before_ // 2 + NF - 1, at[1] + before_ // 2 + two]
            A_TOTAL[n_] = tuple(at)

        @block.sync
        def _(sp):
            unit = [0]
            us = Uses(SLOTS)
            aunit = [0]
            ua = Uses(2)

            def load(s, index):
                n = us.next(s)
                if us.i is not None or n > 0:
                    sp.wait_ge(w_lo[s], n + CREDIT[s])
                sp.dma_start(raw[:, s, :], units[bass.ds(index, 1), :, :].rearrange("u p n -> p (u n)"))\
                  .then_inc(w_in[s], 16)

            def load_ada(s, index, place=(araw[:, 0, :], araw[:, 1, :])):
                n = ua.next(s)
                if ua.i is not None or n > 0:
                    sp.wait_ge(a_used[s], n)
                sp.dma_start(place[s], ada_units[bass.ds(index, 1), :, :].rearrange("u p n -> p (u n)"))\
                  .then_inc(a_in[s], 16)

            def load_brow(k):
                if k:
                    sp.wait_ge(S["gp_ok"], k)
                sp.dma_start(brow[:, :, :], bass.AP(bcast.tensor, k * 2 * D, [[0, P], [1, 2 * D]]))\
                  .then_inc(S["brow_in"], 16)

            sp.dma_start(vrow[:, :, :], rows.rearrange("(a p) n -> p a n", p=P)).then_inc(S["rows_in"], 16)
            sp.dma_start(x[:, :, :], x_in.rearrange("(t p) d -> p t d", p=P)).then_inc(S["x_in"], 16)
            for a in range(2):
                load_ada(a, a)
            sp.dma_start(oneh_sb[0:32, :], onehot[:, :]).then_inc(S["bias_in"], 16)
            sp.dma_start(negr_sb[0:H_AT, :], negrow[:, :]).then_inc(S["bias_in"], 16)
            sp.dma_start(rel_sb[0:32, :], rel[:, :]).then_inc(S["bias_in"], 16)
            for a in range(2, 8):
                load_ada(a % 2, a)
            load(0, 0)
            load(1, 1)
            for a in range(8, 10):
                load_ada(a % 2, a)
            unit[0], aunit[0] = 2, 10
            sp.wait_ge(S["wd_ok"], 1)
            sp.wait_ge(S["cols_ok"], 1)
            sp.dma_start(nwl, bass.AP(nw_ml.tensor, 0, [[0, P], [1, D]])).then_inc(S["mlc_in"], 16)
            sp.dma_start(mlw_sb[:, :, :], mlw).then_inc(S["mlc_in"], 16)
            sp.dma_start(mlb_sb[0:4, :], mlb[0:4, :]).then_inc(S["mlc_in"], 16)
            sp.dma_start(mlb_sb[32:36, :], mlb[4:8, :]).then_inc(S["mlc_in"], 16)
            sp.dma_start(mbw_sb[:, :, :], mbw).then_inc(S["mbc_in"], 16)
            sp.dma_start(mbv_sb[:, :], mbv).then_inc(S["mbc_in"], 16)
            sp.dma_start(mbd_sb[:, :], bass.AP(mbd.tensor, 0, [[0, P], [1, H_MB]])).then_inc(S["mbc_in"], 16)
            sp.dma_start(scratch[:, :], wdist[0:H_AT, :]).then_inc(S["scratch_out"], 16)

            for n, kind in enumerate(KIND):
                if kind == "ffn":
                    if KIND[n - 1] != "ffn" and n:
                        for t in range(T):
                            sp.wait_ge(x_new[t], n)
                    if n == 2:
                        sp.wait_ge(S["mod_gate"], 3)
                    load(0, unit[0])
                    load(1, unit[0] + 1)
                    load_brow(GATES_BEFORE[n])
                    unit[0] += 2
                    if n:
                        for a in range(ADA_PLAN[n][1]):
                            load_ada(a % 2, aunit[0])
                            aunit[0] += 1
                    for _, steps, per in ada_steps(n):
                        with sp.Fori(0, steps) as i:
                            us.enter(i, steps)
                            ua.enter(i, steps)
                            load(2, i * 3 + unit[0])
                            load_ada(0, i * per + aunit[0])
                            load(0, i * 3 + (unit[0] + 1))
                            load(1, i * 3 + (unit[0] + 2))
                            if per == 2:
                                load_ada(1, i * per + (aunit[0] + 1))
                            us.leave()
                            ua.leave()
                        unit[0] += 3 * steps
                        aunit[0] += per * steps
                    load(2, unit[0])
                    unit[0] += 1
                    if n in (0, 3):
                        load_brow(GATES_BEFORE[n] + 1)
                else:
                    blocks, outs = {"ml": (6, 4), "mb": (10, 8), "hy": (20, 12)}[kind]
                    if kind == "mb":
                        sp.wait_ge(S["tr_ok"], 2 * n + 2)
                        sp.dma_start(nwm, bass.AP(nw_mb.tensor, 0, [[0, P], [1, DI]])).then_inc(S["nwm_in"], 16)
                    if kind == "hy":
                        for t in range(T):
                            sp.wait_ge(x_new[t], n)
                        sp.wait_ge(S["scratch_out"], 16)
                        sp.dma_start(bmr[:, :, 0:P], bass.AP(scratch.tensor, 0, [[1, P], [REL, H_AT], [1, P]]))\
                          .then_inc(S["bmr_in"], 16)
                        sp.dma_start(bmr[:, :, P:SEQ], bass.AP(scratch.tensor, P, [[1, P], [REL, H_AT], [1, P]]))\
                          .then_inc(S["bmr_in"], 16)
                    if kind == "ml":
                        sp.wait_ge(S["tr_ok"], 2 * n + 2)
                        sp.wait_ge(S["pre_lo"], 2 * n + 2)
                        sp.wait_ge(S["ml_gate"], 1)
                    for steps, per in ((4, 1), (2, 2)) if kind == "ml" else ((blocks, 0),):
                        with sp.Fori(0, steps) as i:
                            us.enter(i, steps)
                            ua.enter(i, steps)
                            load(0, i * 2 + unit[0])
                            if per:
                                load_ada(0, i * per + aunit[0], araw2)
                            load(1, i * 2 + (unit[0] + 1))
                            if per == 2:
                                load_ada(1, i * per + (aunit[0] + 1), araw2)
                            us.leave()
                            ua.leave()
                        unit[0] += 2 * steps
                        aunit[0] += per * steps
                    for u in range(2, outs):
                        load(u % SLOTS, unit[0])
                        unit[0] += 1
                        if kind == "ml":
                            for s in range(2):
                                load_ada(s, aunit[0], araw2)
                                aunit[0] += 1
                    if kind == "ml":
                        sp.wait_ge(S["ml_tr"], 2)
                        sp.dma_start(brow2[:, :, :], bass.AP(bcast.tensor, 2 * 2 * D, [[0, P], [1, 2 * D]]))\
                          .then_inc(S["brow2_in"], 16)
                    if kind != "hy":
                        load(0, unit[0])
                        load(1, unit[0] + 1)
                        unit[0] += 2
                    else:
                        sp.dma_start(gp[:, 1, :], bass.AP(bcast.tensor, 13 * D, [[0, P], [1, D]])).then_inc(S["fg_in"], 16)
            if STAGES == 7:
                for t in range(T):
                    sp.wait_ge(S["hy_out"], t + 1)
                    sp.dma_start(out[t * P:(t + 1) * P, :], vh[:, t, :]).then_inc(S["out_in"], 16)
            else:
                sp.wait_ge(S["mlc_in"], 64)
                sp.wait_ge(S["mbc_in"], 48)
                sp.wait_ge(S["scratch_out"], 16)
                for s in range(SLOTS):
                    if s < 2: sp.wait_ge(w_lo[s], us.n[s])
                for t in range(T):
                    sp.wait_ge(x_new[t], STAGES)
                    sp.dma_start(out[t * P:(t + 1) * P, :], x[:, t, :]).then_inc(S["out_in"], 16)
            sp.wait_ge(S["out_in"], 16 * T)

        @block.gpsimd
        def _(pool):
            c = Count(S["acc_pool"])

            def step(ins):
                c.on(ins)
                pool.wait_ge(c.sem, c.n)

            pool.memset(zero[:, :], 0.0).then_inc(S["const"], 1)
            pool.memset(ones[:, :], 1.0).then_inc(S["const"], 1)
            pool.memset(negh[:, :], -0.5).then_inc(S["const"], 1)
            step(pool.memset(ident[:, :], 0.0))
            pool.affine_select(out=ident[:, :], in_=ident[:, :], compare_op=ALU.not_equal, fill=1.0, base=0,
                               pattern=[[-1, P]], channel_multiplier=1).then_inc(S["const"], 1)
            pool.memset(acc, 0.0).then_inc(S["zero_acc"], 1)
            step(pool.memset(mask[:, :], 0.0))
            pool.affine_select(out=mask[:, 0:P], in_=mask[:, 0:P], compare_op=ALU.is_ge, fill=NEG, base=0,
                               pattern=[[1, P]], channel_multiplier=-1).then_inc(S["const"], 1)

            taken = {}

            def inv_rms(src, dst, count, ready):
                w = src.shape[1]
                step(pool.tensor_scalar(base[:, 0:w], src, 1.0 / count, EPS, ALU.mult, ALU.add))
                pool.tensor_tensor(dst, base[:, 0:w], negh[:, 0:w], ALU.pow).then_inc(ready, 1)
                taken[ready.name] = taken.get(ready.name, 0) + 1
                pool.wait_ge(ready, taken[ready.name])

            for n, kind in enumerate(KIND):
                for t in range(T):
                    pool.wait_ge(S["pre_ss"], 2 * n + t + 1)
                    inv_rms(ssx[:, n, t:t + 1], ssx[:, n, 2 + t:3 + t], D, S["pre_rstd"])
                if n == 2:
                    pool.wait_ge(S["gp_ok"], 3)
                if n in (2, 3, 5):
                    pool.wait_ge(S["mod_gate"], GATES_BEFORE[n])
                    pool.memset({2: acc, 3: acc[:, 3 * D:6 * D], 5: acc[:, 0:3 * D]}[n], 0.0).then_inc(S["zero_acc"], 1)
                if n == 1:
                    for s in range(2):
                        pool.wait_ge(a_used[s], A_TOTAL[0][s])
                    pool.memset(acc2, 0.0).then_inc(S["zero_acc2"], 1)
                if kind == "ml":
                    pool.wait_ge(S["mlc_in"], 64)
                    pool.wait_ge(S["ml_og"], 1)
                    pool.tensor_tensor(og[:, 0, :], og[:, 0, :], nwl, ALU.mult).then_inc(S["ml_gw"], 1)
                    pool.wait_ge(S["ml_ss"], 8)
                    inv_rms(sm[:, 3, :], sm[:, 4, :], DV, S["ml_rs"])
                if kind == "mb":
                    for gr in range(GROUPS):
                        pool.wait_ge(S["mb_xs"], GROUPS)
                        if gr:
                            pool.wait_ge(S["mb_z"], 2 * gr)
                        for t in range(T):
                            pool.tensor_tensor(
                                xd[:, t, :].rearrange("p (h d) -> p h d", d=HD),
                                xs[:, t, gr * 512:(gr + 1) * 512].rearrange("p (h d) -> p h d", d=HD),
                                mbd_sb[:, gr * HPG:(gr + 1) * HPG].unsqueeze(2).to_broadcast([P, HPG, HD]),
                                ALU.mult).then_inc(S["mb_xd"], 1)
                        pool.wait_ge(S["mb_ss"], 2 * gr + 2)
                        inv_rms(sg[:, 0, 2 * gr:2 * gr + 2], sg[:, 1, 2 * gr:2 * gr + 2], 512, S["mb_rs"])
                if kind == "hy":
                    pool.wait_ge(S["bmr_in"], 32)
                    step(pool.memset(jrev, 0.0))
                    pool.affine_select(out=jrev, in_=jrev, compare_op=ALU.not_equal, fill=1.0, base=1 - P,
                                       pattern=[[1, P]], channel_multiplier=1).then_inc(S["hy_gs"], 1)
                    for t in range(T):
                        pool.wait_ge(S["hy_fs"], t + 1)
                        inv_rms(ssx[:, n, 4 + t:5 + t], ssx[:, n, 6 + t:7 + t], D, S["hy_fr"])
                else:
                    for t in range(T):
                        pool.wait_ge(S["post_ss"], 2 * n + t + 1)
                        inv_rms(ssx[:, n, 4 + t:5 + t], ssx[:, n, 6 + t:7 + t], D, S["post_rstd"])

        @block.scalar
        def _(act):
            c = Count(S["acc_act"])
            us = Uses(SLOTS)

            for q in pj_free + [S["mb_silu"]]:
                act.sem_inc(q, ONE)

            def hi(s):
                n = us.next(s)
                act.wait_ge(w_in[s], 16 * n + 16)
                if us.i is not None or n > 0:
                    act.wait_ge(w_used[s], n + CREDIT[s])
                act.activation(whi[:, s, :], raw[:, s, :], ACT.Copy).then_inc(w_hi[s], 1)

            def project(blocks, evacs, pb):
                with act.Fori(0, blocks) as i:
                    us.enter(i, blocks)
                    hi(0)
                    act.wait_ge(pj_ok[0], i + (pb + 1))
                    evacs(0, i)
                    n1 = i + us.n[1]
                    hi(1)
                    evacs(1, i)
                    us.leave()

            def after_piece(p, pb, evac):
                blk, part = divmod(p, 4)
                if part == 1:
                    hi(0)
                if part == 2:
                    act.wait_ge(pj_ok[0], pb + blk + 1)
                    evac(0, blk)
                if part == 3:
                    hi(1)
                    evac(1, blk)

            def out_units(outs, more):
                for u in range(2, outs):
                    hi(u % SLOTS)
                if more:
                    hi(0)
                    hi(1)

            act.wait_ge(S["cols_ok"], 1)
            act.activation(cT[:, :], cols[:, ROW_C:ROW_C + 16], ACT.Silu).then_inc(S["c_ok"], 1)

            for n, kind in enumerate(KIND):
                for t in range(T):
                    if n == 0:
                        act.wait_ge(S["x_in"], 16)
                    else:
                        act.wait_ge(x_new[t], n)
                    act.activation(hfl[:, t * D:(t + 1) * D], x[:, t, :], ACT.Square,
                                   accum_out=ssx[:, n, t:t + 1]).then_inc(S["pre_ss"], 1)
                for half in range(2):
                    act.wait_ge(S["pre_hf"], 2 * n + half + 1)
                    act.activation(xhi[:, 4 * half:4 * half + 4, :], hf[:, 4 * half:4 * half + 4, :], ACT.Copy)\
                       .then_inc(S["pre_hi"], 1)
                if n == 0:
                    hi(0)
                    hi(1)
                if kind == "ffn":
                    f = FFN_NO[n]

                    def silu(t, done):
                        if not (isinstance(done, int) and done == 0):
                            act.wait_ge(g_ok[t], done)
                        act.activation(sil[:, t, :], ps[:, 4 + t, 0:FB], ACT.Silu).then_inc(sil_ok[t], 1)

                    hi(0)
                    act.wait_ge(s1_ok[0], NF * f + 1)
                    silu(0, NF * f)
                    hi(1)
                    silu(1, NF * f)
                    with act.Fori(0, NF - 1) as i:
                        us.enter(i, NF - 1)
                        hi(2)
                        act.wait_ge(S["gt_ps"], i + (NF * f + 1))
                        act.activation(xhi[:, 8:10, :], ps[:, 6, :], ACT.Copy).then_inc(S["gt_hi"], 1)
                        hi(0)
                        act.wait_ge(s1_ok[0], i + (NF * f + 2))
                        silu(0, i + (NF * f + 1))
                        hi(1)
                        silu(1, i + (NF * f + 1))
                        us.leave()
                    act.wait_ge(w_used[2], us.n[2] + CREDIT[2])
                    act.wait_ge(S["gt_ps"], NF * f + NF)
                    act.activation(xhi[:, 8:10, :], ps[:, 6, :], ACT.Copy).then_inc(S["gt_hi"], 1)
                    hi(2)
                if kind == "ml":
                    act.wait_ge(S["gp_ok"], GATES_BEFORE[n])
                    act.wait_ge(S["ml_na"], 1)
                    act.activation(gt[0:4, 3, :], gt[0:4, 2, :], ACT.Exp).then_inc(S["ml_e"], 1)
                    act.wait_ge(S["ml_u"], 1)
                    act.activation(gt[0:4, 5, :], gt[0:4, 4, :], ACT.Ln).then_inc(S["ml_l"], 1)
                    act.wait_ge(S["ml_rows"], 1)
                    act.activation(gt[0:4, 3, :], gt[0:4, 2, :], ACT.Exp, scale=-1.0).then_inc(S["ml_em"], 1)

                    def ev_qk(b, i):
                        act.activation(qkT[:, bass.ds(i * 4 + 2 * b, 2), :],
                                       ps[:, 4 + b, :].rearrange("p (a b) -> p a b", b=SEQ), ACT.Copy)\
                           .then_inc(pj_free[b], 1)

                    def ev_v(b, i):
                        act.activation(vv[:, b, bass.ds(i * 512, 512)], ps[:, 4 + b, :], ACT.Copy)\
                           .then_inc(pj_free[b], 1)

                    def ev_o(b, i):
                        act.activation(og[:, b, i * 512:(i + 1) * 512], ps[:, 4 + b, :], ACT.Copy)\
                           .then_inc(pj_free[b], 1)

                    pb = PROJ_BEFORE[n]
                    project(2, ev_qk, pb)
                    project(2, ev_v, pb + 2)
                    act.wait_ge(S["ml_arg"], H_ML)
                    act.activation(E_ml[:, :, :], E_ml[:, :, :], ACT.Exp).then_inc(S["ml_E"], 1)
                    for p in range(8):
                        after_piece(p, pb + 4, ev_o)
                    act.wait_ge(pj_free[1], pb + 6 + ONE)
                    for t in range(T):
                        act.activation(og[:, t, :], og[:, t, :], ACT.Sigmoid).then_inc(S["ml_og"], 1)
                    act.wait_ge(S["ml_nd"], H_ML)
                    act.wait_ge(S["ml_r"], 1)
                    for t in range(T):
                        for h in range(H_ML):
                            act.activation(ml_junk[:, 4 * t + h, :],
                                           ps[:, 2 * t + h // 2, (h % 2) * DV:(h % 2 + 1) * DV], ACT.Square,
                                           scale=sm[:, 2, 4 * t + h:4 * t + h + 1],
                                           accum_out=sm[:, 3, 4 * t + h:4 * t + h + 1]).then_inc(S["ml_ss"], 1)
                    for q in range(2):
                        act.wait_ge(S["ml_tr"], q + 1)
                        act.activation(xhi[:, 4 * q:4 * q + 4, :], ps[:, 4 + 2 * q:6 + 2 * q, :], ACT.Copy)\
                           .then_inc(S["ml_hi"], 1)
                    out_units(4, True)
                if kind == "mb":
                    act.wait_ge(S["gp_ok"], GATES_BEFORE[n])
                    act.wait_ge(S["mb_na"], 1)
                    act.activation(dtt[0:H_MB, 2, :], dtt[0:H_MB, 1, :], ACT.Exp).then_inc(S["mb_e"], 1)
                    act.wait_ge(S["mbc_in"], 48)
                    act.activation(sg[0:H_MB, 0, 0:1], mbv_sb[:, 1:2], ACT.Exp).then_inc(S["mb_eA"], 1)
                    act.wait_ge(S["mb_u"], 1)
                    act.activation(dtt[0:H_MB, 4, :], dtt[0:H_MB, 3, :], ACT.Ln).then_inc(S["mb_l"], 1)

                    def ev_z(b, i):
                        act.activation(zs[:, b, i * 512:(i + 1) * 512], ps[:, 4 + b, :], ACT.Copy)\
                           .then_inc(pj_free[b], 1)

                    def ev_x(b, i):
                        act.wait_ge(S["mb_conv"], i * 2 + ONE)
                        act.wait_ge(S["mb_silu"], i * 2 + ONE)
                        for k in range(2):
                            q = 2 * b + k
                            act.activation(cacc[:, q, :], ps[:, 4 + b, k * SEQ:(k + 1) * SEQ], ACT.Identity,
                                           scale=cols[:, bass.ds(i * 4 + (ROW_MBW + 3 * CONV_F + q), 1)],
                                           bias=cols[:, bass.ds(i * 4 + (ROW_MBW + 4 * CONV_F + q), 1)])\
                               .then_inc(S["mb_cv0"], 1)
                        act.activation(cin[:, 2 * b:2 * b + 2, :],
                                       ps[:, 4 + b, :].rearrange("p (a b) -> p a b", b=SEQ), ACT.Copy)\
                           .then_inc(pj_free[b], 1)
                        if b:
                            for bb in range(2):
                                act.wait_ge(S["mb_conv"], i * 2 + (bb + 1 + ONE))
                                act.activation(xcT[:, bass.ds(i * 4 + 2 * bb, 2), :], cacc[:, 2 * bb:2 * bb + 2, :],
                                               ACT.Silu).then_inc(S["mb_silu"], 1)

                    pb = PROJ_BEFORE[n]
                    project(6, ev_x, pb)
                    for k in range(GROUPS):
                        act.wait_ge(S["mb_xtr"], k + 1)
                        act.activation(xs[:, k % 2, (k // 2) * D:(k // 2 + 1) * D], ps[:, 2 * (k % 2):2 * (k % 2) + 2, :],
                                       ACT.Copy).then_inc(S["mb_xs"], 1)

                    def decays(p):
                        act.wait_ge(S["mb_arg"], p + 1)
                        act.activation(E_mb[:, p % 2, :], E_mb[:, p % 2, :], ACT.Exp).then_inc(S["mb_E"], 1)

                    def silu_z(gr):
                        s_ = slice(gr * 512, (gr + 1) * 512)
                        act.wait_ge(pj_free[1], pb + 6 + gr + 1 + ONE)
                        act.activation(zs[:, :, s_], zs[:, :, s_], ACT.Silu).then_inc(S["mb_zs"], 1)

                    def squares(gr):
                        for t in range(T):
                            act.wait_ge(S["mb_z"], 2 * gr + t + 1)
                            act.activation(xj[:, t, :], zs[:, t, gr * 512:(gr + 1) * 512], ACT.Square,
                                           accum_out=sg[:, 0, 2 * gr + t:2 * gr + t + 1]).then_inc(S["mb_ss"], 1)

                    decays(0)
                    for p in range(16):
                        gr = p // 4
                        if p + 1 < 16:
                            decays(p + 1)
                        if p:
                            after_piece(p - 1, pb + 6, ev_z)
                        if p % 4 == 0 and gr:
                            silu_z(gr - 1)
                        if p % 4 == 2 and gr:
                            squares(gr - 1)
                    after_piece(15, pb + 6, ev_z)
                    silu_z(GROUPS - 1)
                    squares(GROUPS - 1)
                    for q in range(4):
                        act.wait_ge(S["mb_tr"], q + 1)
                        act.activation(xhi[:, 4 * q:4 * q + 4, :], ps[:, 2 * q:2 * q + 2, :], ACT.Copy)\
                           .then_inc(S["mb_hi"], 1)
                    out_units(8, True)
                if kind == "hy":
                    for k in range(4):
                        act.wait_ge(S["hy_flip"], k + 1)
                        act.activation(bm[:, 2 * k:2 * k + 2, :], ps[:, 4 + k % 2, :]
                                       .rearrange("p (a b) -> p a b", b=SEQ), ACT.Copy).then_inc(S["hy_bm"], 1)

                    def ev_h(first, func):
                        def ev(b, i):
                            act.activation(hT[:, bass.ds(i * 4 + (first + 2 * b), 2), :],
                                           ps[:, 4 + b, :].rearrange("p (a b) -> p a b", b=SEQ), func)\
                               .then_inc(pj_free[b], 1)
                        return ev

                    def ev_vh(b, i):
                        act.activation(vh[:, b, bass.ds(i * 512, 512)], ps[:, 4 + b, :], ACT.Copy)\
                           .then_inc(pj_free[b], 1)

                    def ev_m(b, i):
                        act.activation(sgm[:, b, bass.ds(i * 512, 512)], ps[:, 4 + b, :], ACT.Sigmoid)\
                           .then_inc(pj_free[b], 1)

                    pb = PROJ_BEFORE[n]
                    project(4, ev_h(0, ACT.Copy), pb)
                    project(2, ev_vh, pb + 4)
                    project(2, ev_h(16, ACT.Silu), pb + 6)

                    def softmax(h):
                        act.wait_ge(S["hy_L"], h + 1)
                        for t in range(T):
                            sl = slice(0, P) if t == 0 else slice(P, 384)
                            act.activation(P_at[:, h % 2, sl], L_at[:, h % 2, sl], ACT.Exp,
                                           bias=stat[:, h, 2 + t:3 + t], accum_out=stat[:, h, 4 + t:5 + t])\
                               .then_inc(S["hy_P"], 1)

                    softmax(0)
                    for h in range(H_AT):
                        if h + 1 < H_AT:
                            softmax(h + 1)
                        if h:
                            after_piece(2 * h - 2, pb + 8, ev_h(24, ACT.Copy))
                        act.wait_ge(S["hy_pt"], h + 1)
                        act.activation(L_at[:, h % 2, :], ps[:, 3, 0:384], ACT.Copy).then_inc(S["hy_ptc"], 1)
                        if h:
                            after_piece(2 * h - 1, pb + 8, ev_h(24, ACT.Copy))
                    after_piece(14, pb + 8, ev_h(24, ACT.Copy))
                    after_piece(15, pb + 8, ev_h(24, ACT.Copy))
                    act.wait_ge(S["hy_at"], H_AT)
                    act.activation(xhi[:, 8:16, :], hT[:, 16:24, :], ACT.Copy).then_inc(S["hy_ga"], 1)
                    project(2, ev_h(40, ACT.Copy), pb + 12)
                    project(2, ev_h(48, ACT.Silu), pb + 14)
                    project(4, ev_m, pb + 16)
                    act.wait_ge(S["hy_cv"], 4)
                    act.activation(xhi[:, 0:8, :], hT[:, 40:48, :], ACT.Copy).then_inc(S["hy_chi"], 1)
                    for u in range(2, 8):
                        hi(u % SLOTS)
                    for q in range(2):
                        act.wait_ge(S["hy_mtr"], q + 1)
                        act.activation(xhi[:, 8 + 4 * q:12 + 4 * q, :], ps[:, 4 + 2 * q:6 + 2 * q, :], ACT.Copy)\
                           .then_inc(S["hy_mhi"], 1)
                    for u in range(8, 12):
                        hi(u % SLOTS)
                    for t in range(T):
                        act.wait_ge(S["hy_fx"], t + 1)
                        act.activation(hfl[:, t * D:(t + 1) * D], x[:, t, :], ACT.Square,
                                       accum_out=ssx[:, n, 4 + t:5 + t]).then_inc(S["hy_fs"], 1)
                else:
                    if n == 1:
                        act.wait_ge(a_used[1], A_TOTAL[1][1])
                    for t in range(T):
                        wait_y(act, n, t)
                        act.activation(hfl[:, t * D:(t + 1) * D], ps[:, 2 * t:2 * t + 2, :], ACT.Square,
                                       accum_out=ssx[:, n, 4 + t:5 + t]).then_inc(S["post_ss"], 1)

        @block.tensor
        def _(pe):
            us = Uses(SLOTS)
            pe.sem_inc(w_used[2], CREDIT[2])

            def mm(out, lhsT, rhs, start=False, stop=False):
                return pe.matmul(out, lhsT, rhs, start=start, stop=stop, skip_group_check=True)

            def three(out, ahi, alo, bhi, blo, start=False, stop=False):
                mm(out, ahi, bhi, start=start)
                mm(out, ahi, blo)
                return mm(out, alo, bhi, stop=stop)

            def ready(s):
                pe.wait_ge(w_lo[s], us.next(s) + (1 + CREDIT[s]))

            def by_token(s, t, last):
                for kk in range(4):
                    k = 4 * s + kk
                    w = slice(kk * 512, kk * 512 + 512)
                    r = three(ps[:, 4 + t, :], xhi[:, k, t * P:(t + 1) * P], xlo[:, k, t * P:(t + 1) * P],
                              whi[:, s, w], wlo[:, s, w], start=(k == 0), stop=(k == 7))
                return r

            def by_feature(s, q):
                for kk in range(4):
                    k = 4 * s + kk
                    w = slice(kk * 512 + q * P, kk * 512 + q * P + P)
                    r = three(ps[:, 4 + q // 2, (q % 2) * SEQ:(q % 2 + 1) * SEQ], whi[:, s, w], wlo[:, s, w],
                              xhi[:, k, :], xlo[:, k, :], start=(k == 0 and q % 2 == 0), stop=(k == 7))
                return r

            def project(blocks, token, pb):
                with pe.Fori(0, blocks) as i:
                    us.enter(i, blocks)
                    ready(0)
                    if token:
                        pe.wait_ge(pj_free[0], i + (pb + ONE))
                        by_token(0, 0, False)
                        pe.wait_ge(pj_free[1], i + (pb + ONE))
                        by_token(0, 1, False).then_inc(w_used[0], 1)
                        ready(1)
                        by_token(1, 0, True).then_inc(pj_ok[0], 1)
                        by_token(1, 1, True).then_inc(w_used[1], 1)
                    else:
                        for b in range(2):
                            pe.wait_ge(pj_free[b], i + (pb + ONE))
                            by_feature(0, 2 * b)
                            r = by_feature(0, 2 * b + 1)
                        r.then_inc(w_used[0], 1)
                        ready(1)
                        by_feature(1, 0)
                        by_feature(1, 1).then_inc(pj_ok[0], 1)
                        by_feature(1, 2)
                        by_feature(1, 3).then_inc(w_used[1], 1)
                    us.leave()

            def token_piece(p, pb):
                blk, part = divmod(p, 4)
                s, t = divmod(part, 2)
                if t == 0:
                    ready(s)
                if s == 0:
                    pe.wait_ge(pj_free[t], pb + blk + ONE)
                r = by_token(s, t, False)
                if part:
                    r.then_inc((None, w_used[0], pj_ok[0], w_used[1])[part], 1)

            def feature_piece(p, pb):
                blk, part = divmod(p, 4)
                s, b = divmod(part, 2)
                if b == 0:
                    ready(s)
                if s == 0:
                    pe.wait_ge(pj_free[b], pb + blk + ONE)
                by_feature(s, 2 * b)
                r = by_feature(s, 2 * b + 1)
                if part:
                    r.then_inc((None, w_used[0], pj_ok[0], w_used[1])[part], 1)

            def down(s, k, start=False, stop=False, done0=None):
                ready(s)
                for t in range(T):
                    for kk in range(2):
                        for n in range(2):
                            w = slice(kk * D + n * 512, kk * D + n * 512 + 512)
                            r = three(ps[:, 2 * t + n, :], xhi[:, k + kk, t * P:(t + 1) * P],
                                      xlo[:, k + kk, t * P:(t + 1) * P], whi[:, s, w], wlo[:, s, w],
                                      start=start and kk == 0, stop=stop and kk == 1)
                    if t == 0 and done0 is not None:
                        r.then_inc(done0, 1)
                r.then_inc(w_used[s], 1)

            def mod_sums(k):
                return acc2 if k == 2 else acc[:, 3 * D * (k % 2):3 * D * (k % 2) + 3 * D]

            def shift_scale(k, when):
                for s in range(2):
                    pe.wait_ge(a_used[s], A_TOTAL[when][s])
                if k:
                    pe.wait_ge(S["mods_ok"], k)
                for q in range(16):
                    r = mm(ps[:, 7, q:q + 1], mod_sums(k)[:, q * P:(q + 1) * P], ones[:, 0:1], start=True, stop=True)
                r.then_inc(S["mod_cols"], 1)

            def gate(k, when):
                for s in range(2):
                    pe.wait_ge(a_used[s], A_TOTAL[when][s])
                if k:
                    pe.wait_ge(S["gate_read"], k)
                for q in range(2):
                    r = mm(ps[:, 4 + q, :], ones[:, 0:P], mod_sums(k)[:, 2 * D + q * 512:2 * D + (q + 1) * 512],
                           start=True, stop=True)
                r.then_inc(S["mod_gate"], 1)

            pe.wait_ge(S["const"], 5)
            pe.wait_ge(S["rows_in"], 16)
            for a in range(3):
                r = pe.transpose(ps[:, 6, a * P:(a + 1) * P], vrow[:, a, :], ident[:, :])
            r.then_inc(S["cols_tr"], 1)
            pe.wait_ge(S["bias_in"], 48)
            mm(ps[0:H_AT, 5, 0:REL], rel_sb[0:32, :], oneh_sb[0:32, :], start=True, stop=True).then_inc(S["wd_ps"], 1)
            pe.wait_ge(S["wd_ok"], 1)

            for n, kind in enumerate(KIND):
                pe.wait_ge(S["xn_ok"], 2 * n + 2)
                xn = xn_of(n)
                for k in range(KT):
                    for t in range(T):
                        r = pe.transpose(ps[:, k // 2, (k % 2) * SEQ + t * P:(k % 2) * SEQ + (t + 1) * P],
                                         xn[:, t, k * P:(k + 1) * P], ident[:, :])
                    if k % 4 == 3:
                        r.then_inc(S["tr_ok"], 1)
                if n == 0:
                    shift_scale(0, "start")
                if kind == "hy":
                    pe.wait_ge(S["gate_read"], GATES_BEFORE[n])
                    pe.wait_ge(S["hy_gs"], 1)
                    for k in range(4):
                        if k >= 2:
                            pe.wait_ge(S["hy_bm"], k - 1)
                        mm(ps[:, 4 + k % 2, :], jrev, bmr[:, 2 * k:2 * k + 2, :], start=True, stop=True)\
                            .then_inc(S["hy_flip"], 1)
                    pe.wait_ge(S["hy_bm"], 4)
                if n:
                    pe.wait_ge(S["gate_read"], GATES_BEFORE[n])
                pe.wait_ge(S["pre_lo"], 2 * n + 1)
                if kind == "ffn":
                    f = FFN_NO[n]
                    b = NF * f

                    def turn(i):
                        for t in range(T):
                            pe.wait_ge(g_ok[t], i + (b + 1))
                        pe.wait_ge(S["gt_lo"], i + (b + ONE))
                        for kk in range(2):
                            for t in range(T):
                                r = pe.transpose(ps[:, 6, kk * SEQ + t * P:kk * SEQ + (t + 1) * P],
                                                 g[:, t, kk * P:(kk + 1) * P], ident[:, :])
                        r.then_inc(S["gt_ps"], 1)

                    ready(0)
                    by_token(0, 0, False)
                    by_token(0, 1, False).then_inc(w_used[0], 1)
                    ready(1)
                    pe.wait_ge(S["pre_lo"], 2 * n + 2)
                    by_token(1, 0, True).then_inc(s1_ok[0], 1)
                    by_token(1, 1, True).then_inc(w_used[1], 1)
                    for q in range(4):
                        mm(ps[:, q, :], zero[0:1, 0:P], zero[0:1, :], start=True)
                    for first, steps, _ in ada_steps(n):
                        with pe.Fori(0, steps) as i:
                            us.enter(i, steps)
                            ready(0)
                            for t in range(T):
                                pe.wait_ge(g_ok[t], i + (b + first + 1))
                                r = by_token(0, t, False)
                            r.then_inc(w_used[0], 1)
                            turn(i + first)
                            ready(1)
                            by_token(1, 0, True).then_inc(s1_ok[0], 1)
                            by_token(1, 1, True).then_inc(w_used[1], 1)
                            pe.wait_ge(S["gt_lo"], i + (b + first + 1 + ONE))
                            down(2, 8)
                            us.leave()
                    turn(NF - 1)
                    if n == 0:
                        gate(0, 0)
                        shift_scale(1, 0)
                    else:
                        k = {2: 3, 3: 4, 5: 6}[n]
                        shift_scale(k, n)
                        gate(k, n)
                    pe.wait_ge(S["gt_lo"], b + NF + ONE)
                    down(2, 8, stop=True, done0=y_done[0])
                    if n == 0:
                        gate(1, 0)
                    if n == 3:
                        shift_scale(5, n)
                        gate(5, n)
                if kind == "ml":
                    pe.wait_ge(S["mlc_in"], 64)
                    pe.wait_ge(S["pre_lo"], 2 * n + 2)
                    pe.wait_ge(S["mods_ok"], GATES_BEFORE[n])
                    for k in range(KT):
                        r = mm(ps[0:36, 7, 0:SEQ], mlw_sb[:, k, :], hf[:, k, :], start=(k == 0), stop=(k == 7))
                    r.then_inc(S["ml_gate"], 1)
                    pb = PROJ_BEFORE[n]
                    project(2, False, pb)
                    pe.wait_ge(S["ml_rows"], 2)
                    pe.wait_ge(S["ml_em"], 1)
                    for j, row in enumerate((8, 3)):
                        for t in range(T):
                            r = pe.transpose(ps[:, 7, 256 + (t * 2 + j) * 4:256 + (t * 2 + j) * 4 + 4],
                                             gt[0:4, row, t * P:(t + 1) * P], ident[0:4, 0:4])
                    r.then_inc(S["ml_ct"], 1)
                    project(2, True, pb + 2)
                    pe.wait_ge(S["ml_cols"], 1)
                    for h in range(H_ML):
                        mm(ps[:, h, 0:SEQ], ident[0:4, h:h + 1].to_broadcast([4, P]), gt[0:4, 2, :],
                           start=True, stop=True).then_inc(S["ml_nm"], 1)

                    def scores(h):
                        if h >= 2:
                            pe.wait_ge(S["ml_den"], h - 1)
                        b = 6 + h % 2
                        mm(ps[:, b, 0:SEQ], qkT[:, 4 + h, 0:P], qkT[:, h, :], start=True, stop=True)
                        mm(ps[:, b, SEQ:384], qkT[:, 4 + h, P:SEQ], qkT[:, h, P:SEQ], start=True, stop=True)\
                            .then_inc(S["ml_sc"], 1)

                    scores(0)
                    scores(1)
                    pe.wait_ge(S["ml_arg"], H_ML)
                    token_piece(0, pb + 4)
                    for h in range(H_ML):
                        token_piece(2 * h + 1, pb + 4)
                        pe.wait_ge(S["ml_ST"], h + 1)
                        e0, e1, e2 = (E_ml[:, h, k * P:(k + 1) * P] for k in range(3))
                        v0, v1 = (vv[:, t, h * DV:(h + 1) * DV] for t in range(2))
                        o0, o1 = (ps[:, 2 * t + h // 2, (h % 2) * DV:(h % 2 + 1) * DV] for t in range(2))
                        d0, d1 = (ps[:, 6 + h % 2, 384 + t:385 + t] for t in range(2))
                        mm(o0, e0, v0, start=True, stop=True)
                        mm(o1, e1, v0, start=True)
                        mm(o1, e2, v1, stop=True)
                        mm(d0, e0, ones[:, 0:1], start=True, stop=True)
                        mm(d1, e1, ones[:, 0:1], start=True)
                        mm(d1, e2, ones[:, 0:1], stop=True).then_inc(S["ml_nd"], 1)
                        if h < 3:
                            token_piece(2 * h + 2, pb + 4)
                        if h + 2 < H_ML:
                            scores(h + 2)
                    pe.wait_ge(S["ml_am"], 8)
                    for k in range(KT):
                        for t in range(T):
                            r = pe.transpose(ps[:, 4 + k // 2, (k % 2) * SEQ + t * P:(k % 2) * SEQ + (t + 1) * P],
                                             am[:, t, k * P:(k + 1) * P], ident[:, :])
                        if k % 4 == 3:
                            r.then_inc(S["ml_tr"], 1)
                    for u in range(4):
                        pe.wait_ge(S["ml_lo"], u // 2 + 1)
                        down(u % SLOTS, 2 * u, start=(u == 0), stop=(u == 3), done0=y_done[0] if u == 3 else None)
                    shift_scale(2, 1)
                    gate(2, 1)
                if kind == "mb":
                    pe.wait_ge(S["mbc_in"], 48)
                    pe.wait_ge(S["pre_lo"], 2 * n + 2)
                    pe.wait_ge(S["mods_ok"], GATES_BEFORE[n])
                    for k in range(KT):
                        r = mm(ps[0:H_MB, 7, 0:SEQ], mbw_sb[:, k, :], hf[:, k, :], start=(k == 0), stop=(k == 7))
                    r.then_inc(S["mb_gate"], 1)
                    pb = PROJ_BEFORE[n]
                    project(6, False, pb)
                    pe.wait_ge(S["mb_rows"], 1)
                    for j, row in enumerate((5, 3)):
                        for t in range(T):
                            r = pe.transpose(ps[:, 7, 256 + (2 * j + t) * 32:256 + (2 * j + t + 1) * 32],
                                             dtt[0:H_MB, row, t * P:(t + 1) * P], ident[0:H_MB, 0:H_MB])
                    r.then_inc(S["mb_ct"], 1)
                    pe.wait_ge(S["mb_silu"], 12 + ONE)
                    for k in range(GROUPS):
                        if k >= 2:
                            pe.wait_ge(S["mb_xs"], k - 1)
                        for q in range(8):
                            r = pe.transpose(ps[:, 2 * (k % 2) + q // 4, (q % 4) * P:(q % 4 + 1) * P],
                                             xcT[:, 8 * (k // 2) + q, (k % 2) * P:(k % 2 + 1) * P], ident[:, :])
                        r.then_inc(S["mb_xtr"], 1)

                    def cb(gr):
                        if gr >= 2:
                            pe.wait_ge(S["mb_W"], 4 * (gr - 1))
                        bT, cT_ = xcT[:, 16 + gr, :], xcT[:, 20 + gr, :]
                        mm(ps[:, 2 + gr % 2, 0:SEQ], bT[:, 0:P], cT_, start=True, stop=True)
                        mm(ps[:, 2 + gr % 2, SEQ:384], bT[:, P:SEQ], cT_[:, P:SEQ], start=True, stop=True)\
                            .then_inc(S["mb_cb"], 1)

                    def decay(p):
                        if p >= 2:
                            pe.wait_ge(S["mb_arg"], p - 1)
                        for j in range(2):
                            h = 2 * p + j
                            r = mm(ps[:, 6 + p % 2, j * SEQ:(j + 1) * SEQ],
                                   ident[0:H_MB, h:h + 1].to_broadcast([H_MB, P]), dtt[0:H_MB, 5, :],
                                   start=True, stop=True)
                        r.then_inc(S["mb_ab"], 1)

                    pe.wait_ge(S["mb_cols"], 1)
                    decay(0)
                    decay(1)
                    pe.wait_ge(S["mb_xs"], GROUPS)
                    cb(0)
                    for p in range(16):
                        gr = p // 4
                        if p % 4 == 2 and gr + 1 < GROUPS:
                            cb(gr + 1)
                        pe.wait_ge(S["mb_W"], p + 1)
                        if p % 4 == 0 and gr:
                            pe.wait_ge(S["mb_add"], 2 * gr)
                        for j in range(2):
                            h = 2 * p + j
                            hh = h % HPG
                            w0, w1, w2_ = (W_mb[:, p % 2, j * 384 + k * P:j * 384 + (k + 1) * P] for k in range(3))
                            o0, o1 = (ps[:, t, hh * HD:(hh + 1) * HD] for t in range(2))
                            x0, x1 = (xs[:, t, h * HD:(h + 1) * HD] for t in range(2))
                            mm(o0, w0, x0, start=True, stop=True)
                            mm(o1, w1, x0, start=True)
                            r = mm(o1, w2_, x1, stop=True)
                        r.then_inc(S["mb_y"], 1)
                        if p + 2 < 16:
                            decay(p + 2)
                        token_piece(p, pb + 6)
                    pe.wait_ge(S["mb_yn"], 2 * GROUPS)
                    for k in range(16):
                        for t in range(T):
                            r = pe.transpose(ps[:, k // 2, (k % 2) * SEQ + t * P:(k % 2) * SEQ + (t + 1) * P],
                                             zs[:, t, k * P:(k + 1) * P], ident[:, :])
                        if k % 4 == 3:
                            r.then_inc(S["mb_tr"], 1)
                    for u in range(8):
                        pe.wait_ge(S["mb_lo"], max(u // 2 + 1, 2))
                        down(u % SLOTS, 2 * u, start=(u == 0), stop=(u == 7), done0=y_done[0] if u == 7 else None)
                if kind == "hy":
                    pe.wait_ge(S["pre_lo"], 2 * n + 2)
                    pb = PROJ_BEFORE[n]
                    project(4, False, pb)
                    project(2, True, pb + 4)
                    project(2, False, pb + 6)

                    def logits(h):
                        if h >= 2:
                            pe.wait_ge(S["hy_L"], h - 1)
                        q, k, b = hT[:, h, :], hT[:, 8 + h, :], 6 + h % 2
                        mm(ps[:, b, 0:P], q[:, 0:P], k[:, 0:P], start=True, stop=True)
                        mm(ps[:, b, P:384], q[:, P:SEQ], k, start=True, stop=True).then_inc(S["hy_sc"], 1)

                    logits(0)
                    logits(1)
                    for h in range(H_AT):
                        pe.wait_ge(S["hy_Pn"], h + 1)
                        if h:
                            pe.wait_ge(S["hy_ptc"], h)
                        for dst, src in ((0, 0), (1, 1), (2, 2)):
                            r = pe.transpose(ps[:, 3, dst * P:(dst + 1) * P], P_at[:, h % 2, src * P:(src + 1) * P],
                                             ident[:, :])
                        r.then_inc(S["hy_pt"], 1)
                        if h + 2 < H_AT:
                            logits(h + 2)
                        feature_piece(2 * h, pb + 8)
                        pe.wait_ge(S["hy_ptc"], h + 1)
                        if h >= 3:
                            pe.wait_ge(S["hy_at"], h - 2)
                        o = ps[:, h % 3, 0:SEQ]
                        mm(o, vh[:, 0, h * DH:(h + 1) * DH], L_at[:, h % 2, 0:SEQ], start=True)
                        mm(o[:, P:SEQ], vh[:, 1, h * DH:(h + 1) * DH], L_at[:, h % 2, SEQ:384], stop=True)\
                            .then_inc(S["hy_o"], 1)
                        feature_piece(2 * h + 1, pb + 8)
                    project(4, False, pb + 12)
                    project(4, True, pb + 16)
                    pe.wait_ge(S["hy_alo"], 1)
                    for u in range(4):
                        down(u % SLOTS, 8 + 2 * u, start=(u == 0), stop=(u == 3))
                    pe.wait_ge(S["hy_clo"], 1)
                    pe.wait_ge(S["hy_ya"], 1)
                    for u in range(4, 8):
                        down(u % SLOTS, 2 * (u - 4), start=(u == 4), stop=(u == 7))
                    pe.wait_ge(S["hy_mg"], T)
                    for k in range(KT):
                        for t in range(T):
                            r = pe.transpose(ps[:, 4 + k // 2, (k % 2) * SEQ + t * P:(k % 2) * SEQ + (t + 1) * P],
                                             mg[:, t, k * P:(k + 1) * P], ident[:, :])
                        if k % 4 == 3:
                            r.then_inc(S["hy_mtr"], 1)
                    for u in range(8, 12):
                        pe.wait_ge(S["hy_mlo"], (u - 8) // 2 + 1)
                        down(u % SLOTS, 8 + 2 * (u - 8), start=(u == 8), stop=(u == 11),
                             done0=y_done[0] if u == 11 else None)

        @block.vector
        def _(dve):
            c = Count(S["acc_dve"])
            us = Uses(SLOTS)
            ua = Uses(2)
            for q in (w_lo[2], S["gt_lo"], S["mb_conv"]):
                dve.sem_inc(q, ONE)

            def step(ins):
                c.on(ins)
                dve.wait_ge(c.sem, c.value())

            def mark(ins):
                c.on(ins)

            def lo(s):
                n = us.next(s)
                dve.wait_ge(w_hi[s], n + 1)
                dve.tensor_tensor(wlo[:, s, :], raw[:, s, :], whi[:, s, :].bitcast(F32), ALU.subtract)\
                   .then_inc(w_lo[s], 1)

            def ada(s, a, k0, after, total=acc, place=(araw[:, 0, :], araw[:, 1, :])):
                n = ua.next(s)
                dve.wait_ge(a_in[s], 16 * n + 16)
                if after is not None:
                    dve.wait_ge(a_used[after[0]], after[1])
                sums = total[:, bass.ds((a // 4) * D, D)]
                for kk in range(2):
                    r = dve.scalar_tensor_tensor(out=sums, in0=place[s][:, kk * D:(kk + 1) * D],
                                                 scalar=cT[:, bass.ds((a % 4) * 2 + (k0 + kk), 1)], in1=sums,
                                                 op0=ALU.mult, op1=ALU.add)
                    if kk == 0:
                        step(r)
                r.then_inc(a_used[s], 1)

            def project(blocks, body=None, per=0):
                with dve.Fori(0, blocks) as i:
                    us.enter(i, blocks)
                    ua.enter(i, blocks)
                    c.enter(i, per)
                    lo(0)
                    if body:
                        body(0, i)
                    lo(1)
                    if body:
                        body(1, i)
                    c.leave(blocks)
                    us.leave()
                    ua.leave()

            def after_piece(p):
                if p % 4 in (1, 3):
                    lo((0, 1)[p % 4 == 3])

            def out_units(outs, more):
                for u in range(2, outs):
                    lo(u % SLOTS)
                if more:
                    lo(0)
                    lo(1)

            def mod_columns(k):
                r = ROW_MOD + 24 * k
                dve.wait_ge(S["mod_cols"], k + 1)
                mark(dve.tensor_tensor(shT[:, k, :], ps[:, 7, 0:8], cols[:, r:r + 8], ALU.add))
                step(dve.tensor_tensor(modc[:, :], ps[:, 7, 8:16], cols[:, r + 8:r + 16], ALU.add))
                dve.scalar_tensor_tensor(out=g1T[:, k, :], in0=modc[:, :], scalar=1.0, in1=cols[:, r + 16:r + 24],
                                         op0=ALU.add, op1=ALU.mult).then_inc(S["mods_ok"], 1)

            def mod_gate(k):
                dve.wait_ge(S["mod_gate"], k + 1)
                bw = brow2 if k == 2 else brow
                if k == 2:
                    dve.wait_ge(S["brow2_in"], 16)
                else:
                    dve.wait_ge(S["brow_in"], 16 * (k + 1 - (k > 2)))
                dve.tensor_tensor(gp[:, k % 2, :], ps[:, 4:6, :].rearrange("p a b -> p (a b)"), bw[:, 0, :], ALU.add)\
                   .then_inc(S["gate_read"], 1)
                dve.wait_ge(S["gate_read"], k + 1)
                if k < 6:
                    dve.scalar_tensor_tensor(out=gp[:, k % 2, :], in0=gp[:, k % 2, :],
                                             scalar=1.0 if k in (1, 4) else 0.5, in1=bw[:, 1, :],
                                             op0=ALU.mult, op1=ALU.mult).then_inc(S["gp_ok"], 1)
                else:
                    dve.tensor_copy(gp[:, k % 2, 0:1], gp[:, k % 2, 0:1]).then_inc(S["gp_ok"], 1)

            def log1p(e, u, ln, z, u_ok, ln_ok):
                dve.tensor_scalar(u, e, 1.0, None, ALU.add).then_inc(u_ok, 1)
                dve.wait_ge(u_ok, 1)
                step(dve.tensor_scalar(z, u, -1.0, 0.0, ALU.add, ALU.is_equal))
                dve.wait_ge(ln_ok, 1)
                step(dve.scalar_tensor_tensor(out=u, in0=u, scalar=-1.0, in1=z, op0=ALU.add, op1=ALU.add))
                step(dve.reciprocal(u, u))
                step(dve.tensor_tensor(u, u, e, ALU.mult))
                mark(dve.tensor_tensor(ln, ln, u, ALU.mult))
                step(dve.tensor_tensor(z, z, e, ALU.mult))
                step(dve.tensor_tensor(ln, ln, z, ALU.add))

            dve.wait_ge(S["cols_tr"], 1)
            dve.tensor_copy(cols[:, :], ps[:, 6, 0:ROWS]).then_inc(S["cols_ok"], 1)
            dve.wait_ge(S["wd_ps"], 1)
            dve.tensor_tensor(wdist[0:H_AT, :], ps[0:H_AT, 5, 0:REL], negr_sb[0:H_AT, :], ALU.add).then_inc(S["wd_ok"], 1)
            dve.wait_ge(S["c_ok"], 1)
            dve.wait_ge(S["zero_acc"], 1)
            last = [None]

            def ada_one(s, *args, **kw):
                ada(s, *args[:2], last[0], *args[2:], **kw)
                last[0] = (s, ua.n[s])

            def normed_x(n):
                if n == 0:
                    dve.wait_ge(S["x_in"], 16)
                for t in range(T):
                    dve.wait_ge(S["pre_rstd"], 2 * n + t + 1)
                    dve.tensor_scalar(xn_of(n)[:, t, :], x[:, t, :], ssx[:, n, 2 + t:3 + t], None, ALU.mult)\
                       .then_inc(S["xn_ok"], 1)

            ada_one(0, 0, 0)
            normed_x(0)
            for a in range(1, 8):
                ada_one(a % 2, a, 0)
            mod_columns(0)

            for n, kind in enumerate(KIND):
                if n == 3:
                    ada_one(0, 0, 0)
                if n:
                    normed_x(n)
                if n == 3:
                    ada_one(1, 1, 0)
                dve.wait_ge(S["mods_ok"], n + 1)
                for half in range(2):
                    dve.wait_ge(S["tr_ok"], 2 * n + half + 1)
                    for k in range(4 * half, 4 * half + 4):
                        r = dve.tensor_scalar(hf[:, k, :], ps[:, k // 2, (k % 2) * SEQ:(k % 2 + 1) * SEQ],
                                              g1T[:, n, k:k + 1], shT[:, n, k:k + 1], ALU.mult, ALU.add)
                    r.then_inc(S["pre_hf"], 1)
                for half in range(2):
                    dve.wait_ge(S["pre_hi"], 2 * n + half + 1)
                    s_ = slice(4 * half, 4 * half + 4)
                    dve.tensor_tensor(xlo[:, s_, :], hf[:, s_, :], xhi[:, s_, :].bitcast(F32), ALU.subtract)\
                       .then_inc(S["pre_lo"], 1)
                if n == 0:
                    lo(0)
                    lo(1)
                if n == 1:
                    mod_gate(1)
                if n == 4:
                    mod_columns(5)
                    mod_gate(5)
                if kind == "ffn":
                    f = FFN_NO[n]
                    b = NF * f
                    k0 = 8 if n == 5 else 0
                    a_next = {0: 8, 2: 12, 3: 2, 5: 0}[n]

                    def gate_up(t, i):
                        dve.wait_ge(sil_ok[t], i + 1)
                        if t == 0 and not (isinstance(i, int) and i == 0):
                            dve.wait_ge(S["gt_ps"], i)
                        dve.tensor_tensor(g[:, t, :], sil[:, t, :], ps[:, 4 + t, FB:2 * FB], ALU.mult)\
                           .then_inc(g_ok[t], 1)

                    if ADA_PLAN[n][1]:
                        for a in range(2):
                            ada_one(a, a_next, k0)
                            a_next += 1
                    lo(0)
                    gate_up(0, b)
                    lo(1)
                    gate_up(1, b)
                    if n:
                        dve.wait_ge(S["zero_acc"], FFN_NO[n] + 1)
                    for first, steps, per in ada_steps(n):
                        dve.wait_ge(a_used[last[0][0]], last[0][1])
                        with dve.Fori(0, steps) as i:
                            us.enter(i, steps)
                            ua.enter(i, steps)
                            c.enter(i, per)
                            lo(2)
                            ada(0, i * per + a_next, k0, (per - 1, i + ua.n[per - 1]))
                            dve.wait_ge(S["gt_hi"], i + (b + first + 1))
                            dve.tensor_tensor(xlo[:, 8:10, :], ps[:, 6, :].rearrange("p (a b) -> p a b", b=SEQ),
                                              xhi[:, 8:10, :].bitcast(F32), ALU.subtract).then_inc(S["gt_lo"], 1)
                            lo(0)
                            gate_up(0, i + (b + first + 1))
                            gate_up(1, i + (b + first + 1))
                            lo(1)
                            if per == 2:
                                ada(1, i * per + (a_next + 1), k0, (0, i + (ua.n[0] - steps + 1)))
                            c.leave(steps)
                            ua.leave()
                            us.leave()
                        a_next += per * steps
                        last[0] = (per - 1, ua.n[per - 1])
                    dve.wait_ge(S["gt_hi"], b + NF)
                    dve.tensor_tensor(xlo[:, 8:10, :], ps[:, 6, :].rearrange("p (a b) -> p a b", b=SEQ),
                                      xhi[:, 8:10, :].bitcast(F32), ALU.subtract).then_inc(S["gt_lo"], 1)
                    lo(2)
                    if n == 0:
                        mod_gate(0)
                        mod_columns(1)
                    else:
                        mod_columns({2: 3, 3: 4, 5: 6}[n])
                        mod_gate({2: 3, 3: 4, 5: 6}[n])
                if kind == "ml":
                    G = lambda j: gt[0:4, j, :]
                    dve.wait_ge(S["ml_gate"], 1)
                    dve.wait_ge(S["mlc_in"], 64)
                    step(dve.tensor_scalar(G(1), ps[32:36, 7, 0:SEQ], mlb_sb[32:36, :], None, ALU.add))
                    mark(dve.tensor_scalar(G(0), ps[0:4, 7, 0:SEQ], mlb_sb[0:4, :], None, ALU.add))
                    dve.scalar_tensor_tensor(out=G(2), in0=G(1), scalar=-1.0, in1=G(1), op0=ALU.mult, op1=ALU.min)\
                       .then_inc(S["ml_na"], 1)
                    dve.wait_ge(S["ml_e"], 1)
                    log1p(G(3), G(4), G(5), G(6), S["ml_u"], S["ml_l"])
                    step(dve.scalar_tensor_tensor(out=G(6), in0=G(1), scalar=0.0, in1=G(5), op0=ALU.min, op1=ALU.subtract))
                    step(dve.tensor_tensor_scan(G(7), ones[0:4, :], G(6), 0.0, ALU.mult, ALU.add))
                    step(dve.tensor_tensor(G(8), G(0), G(7), ALU.subtract))
                    step(dve.tensor_tensor_scan(G(4), G(8), G(8), 0.0, ALU.max, ALU.max))
                    dve.tensor_tensor(G(2), G(4), G(7), ALU.add).then_inc(S["ml_rows"], 1)
                    dve.wait_ge(S["ml_em"], 1)
                    dve.tensor_scalar(G(2), G(4), -1.0, None, ALU.mult).then_inc(S["ml_rows"], 1)

                    def ada_ml(b, i):
                        if b == 0:
                            ada(0, i + ml_a[0], 0, (0, i + ua.n[0]), acc2, araw2)

                    ml_a = [0]
                    dve.wait_ge(S["zero_acc2"], 1)
                    dve.wait_ge(a_used[last[0][0]], last[0][1])
                    project(2, ada_ml, 1)
                    ml_a[0] = 2
                    dve.wait_ge(S["ml_ct"], 1)
                    dve.tensor_copy(colm[:, :, :], ps[:, 7, 256:272].rearrange("p (a b) -> p a b", b=8))\
                       .then_inc(S["ml_cols"], 1)
                    project(2, ada_ml, 1)
                    last[0] = (0, ua.n[0])
                    dve.wait_ge(S["ml_cols"], 1)

                    def exponent(h):
                        dve.wait_ge(S["ml_nm"], h + 1)
                        e, q = E_ml[:, h, :], ps[:, h, 0:SEQ]
                        dve.scalar_tensor_tensor(out=e[:, 0:SEQ], in0=q, scalar=colm[:, 0, h:h + 1], in1=mask[:, :],
                                                 op0=ALU.add, op1=ALU.min)
                        dve.scalar_tensor_tensor(out=e[:, SEQ:384], in0=q[:, P:SEQ], scalar=colm[:, 1, h:h + 1],
                                                 in1=mask[:, 0:P], op0=ALU.add, op1=ALU.min).then_inc(S["ml_arg"], 1)

                    dve.wait_ge(S["const"], 5)
                    for h in range(H_ML):
                        exponent(h)
                    dve.wait_ge(S["ml_E"], 1)
                    for h in range(H_ML):
                        dve.wait_ge(S["ml_sc"], h + 1)
                        dve.scalar_tensor_tensor(out=E_ml[:, h, :], in0=E_ml[:, h, :], scalar=DK ** -0.5,
                                                 in1=ps[:, 6 + h % 2, 0:384], op0=ALU.mult, op1=ALU.mult)\
                           .then_inc(S["ml_ST"], 1)
                        if h:
                            after_piece(2 * h - 1)
                        dve.wait_ge(S["ml_nd"], h + 1)
                        dve.tensor_copy(sm[:, 0, h:8:4], ps[:, 6 + h % 2, 384:386]).then_inc(S["ml_den"], 1)
                        ada_one(h % 2, 4 + h, 0, total=acc2, place=araw2)
                    after_piece(7)
                    dve.wait_ge(S["ml_den"], H_ML)
                    step(dve.scalar_tensor_tensor(out=sm[:, 1, :], in0=sm[:, 0, :], scalar=-1.0, in1=sm[:, 0, :],
                                                  op0=ALU.mult, op1=ALU.max))
                    step(dve.tensor_tensor(sm[:, 1, :].rearrange("p (a b) -> p a b", b=4),
                                           sm[:, 1, :].rearrange("p (a b) -> p a b", b=4), colm[:, :, 4:8], ALU.max))
                    dve.reciprocal(sm[:, 2, :], sm[:, 1, :]).then_inc(S["ml_r"], 1)
                    dve.wait_ge(S["ml_r"], 1)
                    dve.wait_ge(S["ml_rs"], 1)
                    step(dve.tensor_tensor(sm[:, 5, :], sm[:, 2, :], sm[:, 4, :], ALU.mult))
                    dve.wait_ge(S["ml_og"], 2)
                    step(dve.tensor_tensor(og[:, 1, :], og[:, 1, :], nwl, ALU.mult))
                    dve.wait_ge(S["ml_gw"], 1)
                    for t in range(T):
                        for h in range(H_ML):
                            v_ = slice(h * DV, (h + 1) * DV)
                            dve.scalar_tensor_tensor(out=am[:, t, v_], in0=ps[:, 2 * t + h // 2, (h % 2) * DV:(h % 2 + 1) * DV],
                                                     scalar=sm[:, 5, 4 * t + h:4 * t + h + 1], in1=og[:, t, v_],
                                                     op0=ALU.mult, op1=ALU.mult).then_inc(S["ml_am"], 1)
                    for q in range(2):
                        dve.wait_ge(S["ml_hi"], q + 1)
                        dve.tensor_tensor(xlo[:, 4 * q:4 * q + 4, :], ps[:, 4 + 2 * q:6 + 2 * q, :].rearrange(
                            "p a (c b) -> p (a c) b", b=SEQ), xhi[:, 4 * q:4 * q + 4, :].bitcast(F32), ALU.subtract)\
                           .then_inc(S["ml_lo"], 1)
                    for u in (2, 3, 4, 5):
                        lo((2, 0, 0, 1)[u - 2])
                        ada_one(u % 2, 6 + u, 0, total=acc2, place=araw2)
                if kind == "mb":
                    R = lambda j: dtt[0:H_MB, j, :]
                    dve.wait_ge(S["mb_gate"], 1)
                    dve.wait_ge(S["mbc_in"], 48)
                    step(dve.tensor_scalar(R(0), ps[0:H_MB, 7, 0:SEQ], mbv_sb[:, 0:1], None, ALU.add))
                    dve.scalar_tensor_tensor(out=R(1), in0=R(0), scalar=-1.0, in1=R(0), op0=ALU.mult, op1=ALU.min)\
                       .then_inc(S["mb_na"], 1)
                    dve.wait_ge(S["mb_e"], 1)
                    log1p(R(2), R(3), R(4), R(5), S["mb_u"], S["mb_l"])
                    step(dve.scalar_tensor_tensor(out=R(3), in0=R(0), scalar=0.0, in1=R(4), op0=ALU.max, op1=ALU.add))
                    dve.wait_ge(S["mb_eA"], 1)
                    step(dve.tensor_scalar(R(1), R(3), sg[0:H_MB, 0, 0:1], -1.0, ALU.mult, ALU.mult))
                    dve.tensor_tensor_scan(R(5), ones[0:H_MB, :], R(1), 0.0, ALU.mult, ALU.add).then_inc(S["mb_rows"], 1)
                    def convolve(b, i):
                        dve.wait_ge(pj_free[b], i + (PROJ_BEFORE[4] + 1 + ONE))
                        for j in range(3):
                            sh = 3 - j
                            for q in (2 * b, 2 * b + 1):
                                r = dve.scalar_tensor_tensor(
                                    out=cacc[:, q, sh:SEQ], in0=cin[:, q, 0:SEQ - sh],
                                    scalar=cols[:, bass.ds(i * 4 + (ROW_MBW + j * CONV_F + q), 1)],
                                    in1=cacc[:, q, sh:SEQ], op0=ALU.mult, op1=ALU.add)
                                if j < 2:
                                    if q % 2:
                                        step(r)
                                    else:
                                        mark(r)
                                elif q % 2 == 0:
                                    mark(r)
                        r.then_inc(S["mb_conv"], 1)

                    project(6, convolve, 10)
                    dve.wait_ge(S["mb_ct"], 1)
                    mark(dve.tensor_scalar(colb[:, 0:2, :], ps[:, 7, 256:320].rearrange("p (a b) -> p a b", b=H_MB),
                                           -1.0, None, ALU.mult))
                    dve.tensor_copy(colb[:, 2:4, :], ps[:, 7, 320:384].rearrange("p (a b) -> p a b", b=H_MB))\
                       .then_inc(S["mb_cols"], 1)

                    def exponent(p):
                        dve.wait_ge(S["mb_ab"], p + 1)
                        for j in range(2):
                            h = 2 * p + j
                            e, q = E_mb[:, p % 2, j * 384:(j + 1) * 384], ps[:, 6 + p % 2, j * SEQ:(j + 1) * SEQ]
                            dve.scalar_tensor_tensor(out=e[:, 0:SEQ], in0=q, scalar=colb[:, 0, h:h + 1],
                                                     in1=mask[:, :], op0=ALU.add, op1=ALU.min)
                            r = dve.scalar_tensor_tensor(out=e[:, SEQ:384], in0=q[:, P:SEQ], scalar=colb[:, 1, h:h + 1],
                                                         in1=mask[:, 0:P], op0=ALU.add, op1=ALU.min)
                        r.then_inc(S["mb_arg"], 1)

                    def weights(p):
                        dve.wait_ge(S["mb_E"], p + 1)
                        dve.wait_ge(S["mb_cb"], p // 4 + 1)
                        if p >= 2:
                            dve.wait_ge(S["mb_y"], p - 1)
                        q = ps[:, 2 + (p // 4) % 2, :]
                        for j in range(2):
                            h = 2 * p + j
                            e, w = (v[:, p % 2, j * 384:(j + 1) * 384] for v in (E_mb, W_mb))
                            dve.scalar_tensor_tensor(out=w[:, 0:SEQ], in0=e[:, 0:SEQ], scalar=colb[:, 2, h:h + 1],
                                                     in1=q[:, 0:SEQ], op0=ALU.mult, op1=ALU.mult)
                            r = dve.scalar_tensor_tensor(out=w[:, SEQ:384], in0=e[:, SEQ:384],
                                                         scalar=colb[:, 3, h:h + 1], in1=q[:, SEQ:384],
                                                         op0=ALU.mult, op1=ALU.mult)
                        r.then_inc(S["mb_W"], 1)

                    def add_dx(gr):
                        dve.wait_ge(S["mb_y"], 4 * (gr + 1))
                        for t in range(T):
                            dve.wait_ge(S["mb_xd"], 2 * gr + t + 1)
                            dve.tensor_tensor(xd[:, t, :], ps[:, t, :], xd[:, t, :], ALU.add).then_inc(S["mb_add"], 1)

                    def times_z(gr):
                        dve.wait_ge(S["mb_zs"], gr + 1)
                        dve.wait_ge(S["mb_add"], 2 * gr + 2)
                        s_ = slice(gr * 512, (gr + 1) * 512)
                        for t in range(T):
                            dve.tensor_tensor(zs[:, t, s_], xd[:, t, :], zs[:, t, s_], ALU.mult).then_inc(S["mb_z"], 1)

                    def normed(gr):
                        dve.wait_ge(S["mb_rs"], gr + 1)
                        dve.wait_ge(S["nwm_in"], 16)
                        s_ = slice(gr * 512, (gr + 1) * 512)
                        for t in range(T):
                            dve.scalar_tensor_tensor(out=zs[:, t, s_], in0=zs[:, t, s_],
                                                     scalar=sg[:, 1, 2 * gr + t:2 * gr + t + 1], in1=nwm[:, s_],
                                                     op0=ALU.mult, op1=ALU.mult).then_inc(S["mb_yn"], 1)

                    dve.wait_ge(S["mb_cols"], 1)
                    dve.wait_ge(S["mb_xs"], GROUPS)
                    exponent(0)
                    for p in range(16):
                        gr = p // 4
                        if p + 1 < 16:
                            exponent(p + 1)
                        if p % 4 == 0 and gr:
                            add_dx(gr - 1)
                        weights(p)
                        if p >= 2:
                            after_piece(p - 2)
                        if p % 4 == 1 and gr:
                            times_z(gr - 1)
                        if p % 4 == 3 and gr:
                            normed(gr - 1)
                    after_piece(15)
                    add_dx(GROUPS - 1)
                    times_z(GROUPS - 1)
                    normed(GROUPS - 1)
                    for q in range(4):
                        dve.wait_ge(S["mb_hi"], q + 1)
                        dve.tensor_tensor(xlo[:, 4 * q:4 * q + 4, :], ps[:, 2 * q:2 * q + 2, :].rearrange(
                            "p a (c b) -> p (a c) b", b=SEQ), xhi[:, 4 * q:4 * q + 4, :].bitcast(F32), ALU.subtract)\
                           .then_inc(S["mb_lo"], 1)
                    out_units(8, True)
                if kind == "hy":
                    project(8)

                    def logits(h):
                        dve.wait_ge(S["hy_sc"], h + 1)
                        if h >= 2:
                            dve.wait_ge(S["hy_o"], h - 1)
                        L, q, st = L_at[:, h % 2, :], ps[:, 6 + h % 2, :], stat[:, h, :]
                        mark(dve.scalar_tensor_tensor(out=L[:, 0:P], in0=q[:, 0:P], scalar=DH ** -0.5,
                                                      in1=bm[:, h, P:SEQ], op0=ALU.mult, op1=ALU.add))
                        step(dve.scalar_tensor_tensor(out=L[:, P:384], in0=q[:, P:384], scalar=DH ** -0.5,
                                                      in1=bm[:, h, :], op0=ALU.mult, op1=ALU.add))
                        mark(dve.tensor_reduce(st[:, 0:1], L[:, 0:P], AX, ALU.max))
                        step(dve.tensor_reduce(st[:, 1:2], L[:, P:384], AX, ALU.max))
                        dve.tensor_scalar(st[:, 2:4], st[:, 0:2], -1.0, None, ALU.mult).then_inc(S["hy_L"], 1)

                    def weigh(h):
                        dve.wait_ge(S["hy_o"], h + 1)
                        dve.tensor_tensor(hT[:, 16 + h, :], ps[:, h % 3, 0:SEQ], hT[:, 16 + h, :],
                                          ALU.mult).then_inc(S["hy_at"], 1)

                    dve.wait_ge(S["hy_bm"], 4)
                    logits(0)
                    for h in range(H_AT):
                        if h + 1 < H_AT:
                            logits(h + 1)
                        dve.wait_ge(S["hy_P"], 2 * h + 2)
                        pr, st = P_at[:, h % 2, :], stat[:, h, :]
                        step(dve.reciprocal(st[:, 6:8], st[:, 4:6]))
                        mark(dve.tensor_scalar(pr[:, 0:P], pr[:, 0:P], st[:, 6:7], None, ALU.mult))
                        dve.tensor_scalar(pr[:, P:384], pr[:, P:384], st[:, 7:8], None, ALU.mult).then_inc(S["hy_Pn"], 1)
                        if h:
                            weigh(h - 1)
                            after_piece(2 * h - 1)
                    weigh(H_AT - 1)
                    after_piece(15)
                    dve.wait_ge(S["hy_ga"], 1)
                    dve.tensor_tensor(xlo[:, 8:16, :], hT[:, 16:24, :], xhi[:, 8:16, :].bitcast(F32), ALU.subtract)\
                       .then_inc(S["hy_alo"], 1)

                    project(4)

                    def short_conv(b, i):
                        if b == 0:
                            return
                        tile = lambda o: hT[:, bass.ds(i * 2 + o, 2), :]
                        u, y = tile(32), tile(40)
                        step(dve.tensor_tensor(u, u, y, ALU.mult))
                        for j in (2, 1, 0):
                            sh = 2 - j
                            for q in range(2):
                                w_ = cols[:, bass.ds(i * 2 + (ROW_HYW + j * 8 + q), 1)]
                                yq = hT[:, bass.ds(i * 2 + (40 + q), 1), sh:SEQ].rearrange("p a b -> p (a b)")
                                uq = hT[:, bass.ds(i * 2 + (32 + q), 1), 0:SEQ - sh].rearrange("p a b -> p (a b)")
                                if j == 2:
                                    r = dve.tensor_scalar(yq, uq, w_, None, ALU.mult)
                                else:
                                    r = dve.scalar_tensor_tensor(out=yq, in0=uq, scalar=w_, in1=yq,
                                                                 op0=ALU.mult, op1=ALU.add)
                                (step if q else mark)(r)
                        step(dve.tensor_tensor(y, y, tile(24), ALU.mult))
                        dve.tensor_tensor(y, y, tile(48), ALU.mult).then_inc(S["hy_cv"], 1)

                    project(4, short_conv, 8)
                    dve.wait_ge(S["hy_chi"], 1)
                    dve.tensor_tensor(xlo[:, 0:8, :], hT[:, 40:48, :], xhi[:, 0:8, :].bitcast(F32), ALU.subtract)\
                       .then_inc(S["hy_clo"], 1)
                    for u in range(2, 4):
                        lo(u % SLOTS)
                    tot = used_before_hy
                    lo(4 % SLOTS)
                    dve.wait_ge(w_used[3 % SLOTS], tot[0] + 20 + 2)
                    for t in range(T):
                        r = dve.tensor_tensor(mg[:, t, :], ps[:, 2 * t:2 * t + 2, :].rearrange("p a b -> p (a b)"),
                                              sgm[:, t, 0:D], ALU.mult)
                        if t == 0:
                            mark(r)
                    r.then_inc(S["hy_ya"], 1)
                    dve.wait_ge(S["hy_ya"], 1)
                    for u in range(5, 8):
                        lo(u % SLOTS)
                    dve.wait_ge(w_used[7 % SLOTS], tot[1] + 20 + 3)
                    for t in range(T):
                        step(dve.tensor_tensor(sgm[:, t, D:2 * D], ps[:, 2 * t:2 * t + 2, :]
                                               .rearrange("p a b -> p (a b)"), sgm[:, t, D:2 * D], ALU.mult))
                        dve.tensor_tensor(mg[:, t, :], mg[:, t, :], sgm[:, t, D:2 * D], ALU.add).then_inc(S["hy_mg"], 1)
                    for q in range(2):
                        dve.wait_ge(S["hy_mhi"], q + 1)
                        dve.tensor_tensor(xlo[:, 8 + 4 * q:12 + 4 * q, :], ps[:, 4 + 2 * q:6 + 2 * q, :].rearrange(
                            "p a (c b) -> p (a c) b", b=SEQ), xhi[:, 8 + 4 * q:12 + 4 * q, :].bitcast(F32), ALU.subtract)\
                           .then_inc(S["hy_mlo"], 1)
                    for u in range(8, 12):
                        lo(u % SLOTS)
                    yb = vh
                    for t in range(T):
                        wait_y(dve, n, t)
                        step(dve.tensor_tensor(yb[:, t, :], ps[:, 2 * t:2 * t + 2, :].rearrange("p a b -> p (a b)"),
                                               gp[:, n % 2, :], ALU.mult))
                        dve.tensor_tensor(x[:, t, :], x[:, t, :], yb[:, t, :], ALU.add).then_inc(S["hy_fx"], 1)
                    dve.wait_ge(S["fg_in"], 16)
                    for t in range(T):
                        dve.wait_ge(S["hy_fr"], t + 1)
                        dve.scalar_tensor_tensor(out=yb[:, t, :], in0=x[:, t, :], scalar=ssx[:, n, 6 + t:7 + t],
                                                 in1=gp[:, 1, :], op0=ALU.mult, op1=ALU.mult).then_inc(S["hy_out"], 1)
                else:
                    yb = yb_of(n)
                    for t in range(T):
                        dve.wait_ge(S["post_rstd"], 2 * n + t + 1)
                        step(dve.scalar_tensor_tensor(out=yb[:, t, :], in0=ps[:, 2 * t:2 * t + 2, :]
                                                      .rearrange("p a b -> p (a b)"), scalar=ssx[:, n, 6 + t:7 + t],
                                                      in1=gp[:, n % 2, :], op0=ALU.mult, op1=ALU.mult))
                        dve.tensor_tensor(x[:, t, :], x[:, t, :], yb[:, t, :], ALU.add).then_inc(x_new[t], 1)
                    if n == 1:
                        mod_columns(2)
                        mod_gate(2)


def _halves(w):
    k, n = w.shape
    return w.reshape(2, 4, P, n // 512, 512).transpose(3, 0, 2, 1, 4).reshape(-1, P, UNIT)


def _pairs(w):
    return w.reshape(-1, 2, P, D).transpose(0, 2, 1, 3).reshape(-1, P, UNIT)


def _ffn_units(w1, w3, w2):
    up = np.concatenate([w1.reshape(D, NF, 1, FB), w3.reshape(D, NF, 1, FB)], 2).reshape(D, NF * 512)
    up, dn = _halves(up).reshape(NF, 2, P, UNIT), _pairs(w2)
    return up, dn


def _stream(stages):
    out = [stages[0][1]]
    for j, (kind, _, rest) in enumerate(stages):
        nxt = stages[j + 1][1] if j + 1 < len(stages) else None
        if kind == "ffn":
            up, dn = rest
            out.append(up[1])
            for i in range(NF - 1):
                out.append(dn[i:i + 1])
                out.append(up[i + 2] if i + 2 < NF else nxt)
            out.append(dn[NF - 1:NF])
        else:
            out.append(rest)
            if nxt is not None:
                out.append(nxt)
    return np.concatenate(out)


def kernel(**inputs):
    import concourse.bacc as _bacc
    from concourse.bass_utils import run_bass_kernel_spmd as _run

    a = {k: np.asarray(v) for k, v in inputs.items()}
    f32 = np.float32
    stages = []
    for layer in range(2):
        ffn = [_ffn_units(a["ffn_w1"][layer, s], a["ffn_w3"][layer, s], a["ffn_w2"][layer, s]) for s in range(2)]
        if layer == 0:
            w = a["ml_w_in"][0]
            mix = np.concatenate([_halves(w[:, :3072]), _pairs(a["ml_w_out"][0])])
        else:
            w = a["mb_w_in"][0]
            mix = np.concatenate([_halves(w[:, 2048:5120]), _halves(w[:, :2048]), _pairs(a["mb_w_out"][0])])
        stages += [("ffn", ffn[0][0][0], ffn[0]), ("mix", mix[:2], mix[2:]), ("ffn", ffn[1][0][0], ffn[1])]
    w = a["w_in_2"][0]
    order = [w[:, 0:2048], w[:, 2048:3072], w[:, 3072:8192], w[:, 8192:10240]]
    hy = np.concatenate([_halves(v) for v in order] + [_pairs(a[k][0]) for k in ("w_o_attn_2", "w_o_conv_2", "w_out_2")])
    stages.append(("mix", hy[:2], hy[2:]))
    units = _stream(stages)

    def ada(w, n):
        return w.reshape(4, 2, P, 3 * n, D).transpose(3, 0, 2, 1, 4).reshape(-1, P, UNIT)

    ada_units = np.concatenate([ada(a["ada_w"][0], 3), ada(a["ada_w"][1], 3), ada(a["w_ada_2"][0], 1)])
    adab = np.concatenate([a["ada_b"].reshape(6, 3, D), a["b_ada_2"].reshape(1, 3, D)])
    pre = np.concatenate([a["norm_pre"].reshape(6, 1, D), a["norm_g_2"].reshape(1, 1, D)])
    rows = np.concatenate([
        np.concatenate([adab[:, 0:2], pre], 1).reshape(-1, P),
        a["c"].reshape(-1, P), a["c_2"].reshape(-1, P),
        a["mb_conv_w"].reshape(-1, P), a["mb_conv_b"].reshape(-1, P), a["conv_w_2"].reshape(-1, P)])
    rows = np.concatenate([rows, np.zeros((ROWS - rows.shape[0], P), f32)])
    post = np.concatenate([a["norm_post"].reshape(6, D), a["final_g_2"].reshape(1, D)])
    bcast = np.stack([adab[:, 2], post], 1).reshape(1, -1)
    mlw = np.zeros((D, 36), f32)
    mlw[:, 0:4], mlw[:, 32:36] = a["ml_w_in"][0][:, 3072:3076], a["ml_w_in"][0][:, 3076:3080]
    mlw = mlw.reshape(KT, P, 36).transpose(1, 0, 2)
    mbw = a["mb_w_in"][0][:, 5120:].reshape(KT, P, H_MB).transpose(1, 0, 2)
    dist = 255 - np.arange(REL)
    big = 16 + (np.log(np.maximum(dist, 1).astype(f32) / f32(16)) / f32(np.log(8.0)) * f32(16)).astype(np.int32)
    bucket = np.where(dist < 16, np.maximum(dist, 0), np.minimum(big, 31))
    onehot = ((bucket[None, :] == np.arange(32)[:, None]) & (dist >= 0)[None, :]).astype(f32)
    negrow = np.broadcast_to(np.where(dist >= 0, 0.0, NEG).astype(f32), (H_AT, REL))
    arrays = dict(
        x_in=a["x"].reshape(SEQ, D), units=units, ada_units=ada_units, rows=rows, bcast=bcast, mlw=mlw,
        mlb=a["ml_b_gate"].reshape(8, 1), mbw=mbw, mbv=np.stack([a["mb_dt_bias"][0], a["mb_A_log"][0]], 1),
        mbd=a["mb_D"].reshape(1, H_MB), nw_ml=a["ml_norm_w"].reshape(1, D), nw_mb=a["mb_norm_w"].reshape(1, DI),
        rel=a["rel_bias_2"], onehot=onehot, negrow=negrow)
    arrays = {k: np.ascontiguousarray(v) for k, v in arrays.items()}
    nc = _bacc.Bacc("TRN2", target_bir_lowering=False, num_devices=1)
    args = [nc.dram_tensor(k, v.shape, mybir.dt.from_np(v.dtype), kind="ExternalInput").ap() for k, v in arrays.items()]
    out = nc.dram_tensor("out", (SEQ, D), F32, kind="ExternalOutput").ap()
    build(nc, *args, out)
    r = _run(nc, [arrays], core_ids=[0])
    return r.results[0]["out"].reshape(1, SEQ, D)
```

```python
import numpy as np
from contextlib import ExitStack

import concourse.bass as bass
from concourse import mybir

F32 = mybir.dt.float32
F32R = mybir.dt.float32r
BF16 = mybir.dt.bfloat16
ALU = mybir.AluOpType
ACT = mybir.ActivationFunctionType
AX = mybir.AxisListType.X

P = 128
D = 1024
SEQ = 256
T = SEQ // P
KT = D // P
F = 2816
FB = 256
NF = F // FB
UNIT = 2048
SLOTS = 3
EPS = 1e-6
NEG = -1e30

H_ML, DK, DV = 4, 128, 256
H_MB, HD, GROUPS, HPG, DI = 32, 64, 4, 8, 2048
CONV_F = 24
H_AT, DH = 8, 128
REL = 384

KIND = ["ffn", "ml", "ffn", "ffn", "mb", "ffn", "hy"]
FFN_NO = {0: 0, 2: 1, 3: 2, 5: 3}
BLOCKS_OUTS = {"ml": (6, 4), "mb": (10, 8), "hy": (20, 12)}
PROJ_BEFORE = {1: 0, 4: 6, 6: 16}

ROW_MOD = 0
ROW_C = ROW_MOD + 7 * 24
ROW_MBW = ROW_C + 16
ROW_HYW = ROW_MBW + 5 * CONV_F
ROWS = 384
assert ROW_HYW + 24 <= ROWS

ADA_STEPS = {0: ((4, 2, 10), (6, 1, 18)),
             2: ((6, 2, 12), (2, 2, 0), (2, 1, 4)),
             3: ((6, 2, 8), (4, 1, 20)),
             5: ((2, 2, 0), (8, 1, 4))}
ADA_BEFORE = {0: 8, 3: 6}


class Count:

    def __init__(self, sem):
        self.sem, self.n, self.i, self.per = sem, 0, None, 0

    def on(self, ins, k=1):
        ins.then_inc(self.sem, k)
        self.n += k
        return ins

    def value(self):
        return self.n if self.i is None else self.i * self.per + self.n

    def enter(self, i, per):
        self.i, self.per, self.first = i, per, self.n

    def leave(self, steps):
        assert self.n - self.first == self.per, (self.n - self.first, self.per)
        self.n, self.i = self.first + self.per * steps, None


class Uses:

    def __init__(self, n):
        self.n, self.i, self.steps = [0] * n, None, 0

    def next(self, s):
        n = self.n[s] if self.i is None else self.i + self.n[s]
        self.n[s] += 1 if self.i is None else self.steps
        return n

    def enter(self, i, steps):
        self.i, self.steps = i, steps

    def leave(self):
        self.i = None


def build(nc, x_in, units, ada_units, rows, bcast, mlw, mlb, mbw, mbv, mbd, nw_ml, nw_mb, rel, onehot,
          negrow, out):
    scratch = nc.dram_tensor("bias_by_distance", (H_AT, REL), F32).ap()
    ctx = ExitStack()
    with ctx:
        def sb(name, shape, dt=F32):
            return ctx.enter_context(nc.sbuf_tensor(name, shape, dt))

        def sem(name):
            return ctx.enter_context(nc.semaphore(name))

        raw = sb("raw", [P, SLOTS, UNIT])
        whi = sb("whi", [P, SLOTS, UNIT], F32R)
        wlo = sb("wlo", [P, SLOTS, UNIT], F32R)
        xhi = sb("xhi", [P, 16, SEQ], F32R)
        xlo = sb("xlo", [P, 16, SEQ], F32R)
        hf = sb("hf", [P, KT, SEQ])
        x = sb("x", [P, T, D])
        gp = sb("gp", [P, 2, D])
        cols = sb("cols", [P, ROWS])
        cT = sb("cT", [P, 16])
        shT = sb("shT", [P, 7, KT])
        g1T = sb("g1T", [P, 7, KT])
        modc = sb("modc", [P, KT])
        ident = sb("ident", [P, P])
        ones = sb("ones", [P, SEQ])
        zero = sb("zero", [1, 512], BF16)
        negh = sb("negh", [P, 8])
        ssx = sb("ssx", [P, 8, 8])
        base = sb("base", [P, 8])
        mask = sb("mask", [P, SEQ])
        WORDS = 18432
        M = sb("M", [P, WORDS])
        ps = ctx.enter_context(nc.psum_tensor("ps", [P, 8, 512], F32))

        def m(off, *shape):
            n = int(np.prod(shape))
            assert off + n <= WORDS, off + n
            ap = M[:, off:off + n]
            return ap.rearrange("p (a b) -> p a b", b=shape[1]) if len(shape) == 2 else ap

        acc = m(0, 6144)
        araw = m(6144, 2, UNIT)
        brow = m(10240, 2, D)
        sil = m(12288, T, FB)
        g = m(12800, T, FB)
        qkT = m(0, 8, SEQ)
        vv = m(2048, T, D)
        og = m(4096, T, D)
        am = m(0, T, D)
        acc2 = m(6144, 3072)
        araw2 = [m(16000, UNIT), hf[:, :, :].rearrange("p a b -> p (a b)")]

        def ml_junk(h, t):
            return E_ml[:, h, 0:DV] if t == 0 else gt[:, 5 + h, :]

        brow2 = m(4096, 2, D)
        E_ml = m(9216, H_ML, 384)
        gt = m(10752, 9, SEQ)
        colm = m(13056, T, 8)
        sm = m(13072, 8, 8)
        nwl = m(13312, D)
        mlw_sb = m(14336, KT, 36)
        mlb_sb = m(14624, 1)
        zs = m(0, T, DI)
        xcT = m(4096, CONV_F, SEQ)
        xs = m(10240, T, DI)
        cin = m(0, 4, SEQ)
        cacc = m(1024, 4, SEQ)
        dtt = m(14336, 6, SEQ)
        colb = m(15872, 4, H_MB)
        nwm = m(16000, DI)
        xd = m(4096, T, 512)
        xj = m(5120, T, 512)
        mbw_sb = sb("mbw_sb", [P, KT, H_MB])
        mbd_sb = sb("mbd_sb", [P, H_MB])
        mbv_sb = sb("mbv_sb", [H_MB, 2])
        sg = sb("sg", [P, 2, 8])
        hfl = hf[:, :, :].rearrange("p a b -> p (a b)")
        E_mb = hfl[:, 0:1536].rearrange("p (a b) -> p a b", b=768)
        W_mb = m(6144, 2, 768)
        hT = m(0, 56, SEQ)
        vh = m(14336, T, D)
        bm = m(16384, H_AT, SEQ)
        bmr = m(4096, H_AT, SEQ)
        sgm = m(0, T, 2 * D)
        mg = m(6144, T, D)
        L_at = hfl[:, 0:768].rearrange("p (a b) -> p a b", b=384)
        P_at = hfl[:, 768:1536].rearrange("p (a b) -> p a b", b=384)
        stat = sb("stat", [P, H_AT, 8])
        wdist = m(15200, REL)
        rel_sb = m(15600, H_AT)
        oneh_sb = m(17024, REL)
        negr_sb = m(17408, REL)
        vrow = m(14712, 3, P)
        jrev = m(8192, P)

        def yb_of(n):
            return m(2048, T, D) if n == 1 else m(16000, T, D)

        def xn_of(n):
            return m(6144, T, D) if n == 6 else m(16000, T, D)

        w_in = [sem(f"w_in{s}") for s in range(SLOTS)]
        w_hi = [sem(f"w_hi{s}") for s in range(SLOTS)]
        w_lo = [sem(f"w_lo{s}") for s in range(SLOTS)]
        w_used = [sem(f"w_used{s}") for s in range(SLOTS)]
        a_in = [sem(f"a_in{s}") for s in range(2)]
        a_used = [sem(f"a_used{s}") for s in range(2)]
        names = """x_in rows_in bias_in mlc_in mbc_in nwm_in scratch_out bmr_in out_in brow_in brow2_in zero_acc2
            const zero_acc cols_tr cols_ok c_ok wd_ps wd_ok  acc_act acc_dve acc_pool
            post_ss yg_ok post_rstd pre_ss pre_rstd xn_ok tr_ok pre_hf pre_hi pre_lo
            mod_cols mod_gate mods_ok gate_read gp_ok
            gt_ps gt_hi gt_lo
            ml_gate ml_na ml_e ml_u ml_l ml_rows ml_em ml_ct ml_cols ml_sc ml_nm ml_arg ml_E ml_ST ml_nd
            ml_r ml_ss ml_rs ml_am ml_tr ml_hi ml_lo ml_gw ml_den
            mb_gate mb_na mb_e mb_u mb_l mb_eA mb_rows mb_ct mb_cols mb_cv0 mb_conv mb_silu mb_xtr mb_xs
            mb_cb mb_ab mb_arg mb_E mb_W mb_y mb_xd mb_z mb_zs mb_add mb_ss mb_rs mb_yn mb_tr mb_hi mb_lo
            hy_flip hy_bm hy_sc hy_L hy_P hy_Pn hy_pt hy_ptc hy_o hy_at hy_ga hy_alo hy_yc hy_cv hy_chi hy_clo
            hy_ya  hy_mg hy_mtr hy_mhi hy_mlo hy_fx hy_fs hy_fr hy_out hy_gs fg_in""".split()
        S = {k: sem(k) for k in names}
        y_done = [sem(f"y_done{t}") for t in range(T)]
        x_new = [sem(f"x_new{t}") for t in range(T)]
        s1_ok = [sem(f"s1_ok{t}") for t in range(T)]
        sil_ok = [sem(f"sil_ok{t}") for t in range(T)]
        g_ok = [sem(f"g_ok{t}") for t in range(T)]
        pj_ok = [sem(f"pj_ok{b}") for b in range(2)]
        pj_free = [sem(f"pj_free{b}") for b in range(2)]

        TURNED = (2, 4, 0, 6)

        block = ctx.enter_context(nc.Block())

        CREDIT = [0, 0, 1]
        ONE = 1

        def out_slot(kind, u):
            return 1 if kind == "ml" and u == 3 else u % SLOTS

        LAST, used = {}, [0] * SLOTS
        for n_, kind_ in enumerate(KIND):
            if kind_ == "ffn":
                used = [u + NF for u in used]
                LAST[n_] = (2, used[2] + CREDIT[2])
            else:
                if kind_ == "hy":
                    used_before_hy = list(used)
                blocks, outs = BLOCKS_OUTS[kind_]
                used[0] += blocks
                used[1] += blocks
                for u in range(outs):
                    used[out_slot(kind_, u)] += 1
                s_ = out_slot(kind_, outs - 1)
                LAST[n_] = (s_, used[s_] + CREDIT[s_])

        def wait_y(eng, n, t):
            if t == 0:
                eng.wait_ge(y_done[0], n + 1)
            else:
                eng.wait_ge(w_used[LAST[n][0]], LAST[n][1])

        GATES_BEFORE = [0, 2, 3, 4, 6, 6, 7]

        def ada_steps(n):
            first = 0
            for steps, per, place in ADA_STEPS[n]:
                yield first, steps, per, place
                first += steps

        A_TOTAL = {"start": (4, 4)}
        at = [4, 4]
        for n_ in (0, 1, 2, 3, 5):
            if n_ == 1:
                at = [at[0] + 6, at[1] + 6]
            else:
                before_ = n_ in ADA_BEFORE
                at = [at[0] + before_ + NF - 1, at[1] + before_ + sum(k_ for k_, per_, _ in ADA_STEPS[n_] if per_ == 2)]
            A_TOTAL[n_] = tuple(at)

        @block.sync
        def _(sp):
            unit = [0]
            us = Uses(SLOTS)
            aunit = [0]
            ua = Uses(2)

            def load(s, index):
                n = us.next(s)
                if us.i is not None or n > 0:
                    sp.wait_ge(w_lo[s], n + CREDIT[s])
                sp.dma_start(raw[:, s, :], units[bass.ds(index, 1), :, :].rearrange("u p n -> p (u n)"))\
                  .then_inc(w_in[s], 16)

            def load_ada(s, index, place=(araw[:, 0, :], araw[:, 1, :])):
                n = ua.next(s)
                if ua.i is not None or n > 0:
                    sp.wait_ge(a_used[s], n)
                sp.dma_start(place[s], ada_units[bass.ds(index, 1), :, :].rearrange("u p n -> p (u n)"))\
                  .then_inc(a_in[s], 16)

            def load_brow(k):
                if k:
                    sp.wait_ge(S["gp_ok"], k)
                sp.dma_start(brow[:, :, :], bass.AP(bcast.tensor, k * 2 * D, [[0, P], [1, 2 * D]]))\
                  .then_inc(S["brow_in"], 16)

            sp.dma_start(vrow[:, :, :], rows.rearrange("(a p) n -> p a n", p=P)).then_inc(S["rows_in"], 16)
            sp.dma_start(x[:, :, :], x_in.rearrange("(t p) d -> p t d", p=P)).then_inc(S["x_in"], 16)
            for a in range(2):
                load_ada(a, a)
            sp.dma_start(oneh_sb[0:32, :], onehot[:, :]).then_inc(S["bias_in"], 16)
            sp.dma_start(negr_sb[0:H_AT, :], negrow[:, :]).then_inc(S["bias_in"], 16)
            sp.dma_start(rel_sb[0:32, :], rel[:, :]).then_inc(S["bias_in"], 16)
            load(0, 0)
            load(1, 1)
            for a in range(2, 10):
                load_ada(a % 2, a)
            unit[0], aunit[0] = 2, 10
            sp.wait_ge(S["wd_ok"], 1)
            sp.wait_ge(S["cols_ok"], 1)
            sp.dma_start(nwl, bass.AP(nw_ml.tensor, 0, [[0, P], [1, D]])).then_inc(S["mlc_in"], 16)
            sp.dma_start(mlw_sb[:, :, :], mlw).then_inc(S["mlc_in"], 16)
            sp.dma_start(mlb_sb[0:4, :], mlb[0:4, :]).then_inc(S["mlc_in"], 16)
            sp.dma_start(mlb_sb[32:36, :], mlb[4:8, :]).then_inc(S["mlc_in"], 16)
            sp.dma_start(mbw_sb[:, :, :], mbw).then_inc(S["mbc_in"], 16)
            sp.dma_start(mbv_sb[:, :], mbv).then_inc(S["mbc_in"], 16)
            sp.dma_start(mbd_sb[:, :], bass.AP(mbd.tensor, 0, [[0, P], [1, H_MB]])).then_inc(S["mbc_in"], 16)
            sp.dma_start(scratch[:, :], wdist[0:H_AT, :]).then_inc(S["scratch_out"], 16)

            for n, kind in enumerate(KIND):
                if kind == "ffn":
                    if KIND[n - 1] != "ffn" and n:
                        for t in range(T):
                            sp.wait_ge(x_new[t], n)
                    if n == 2:
                        sp.wait_ge(S["mod_gate"], 3)
                    load(0, unit[0])
                    load(1, unit[0] + 1)
                    load_brow(GATES_BEFORE[n])
                    unit[0] += 2
                    if n == 3:
                        for a in range(2):
                            load_ada(a, aunit[0])
                            aunit[0] += 1
                    for _, steps, per, _ in ada_steps(n):
                        with sp.Fori(0, steps) as i:
                            us.enter(i, steps)
                            ua.enter(i, steps)
                            load(2, i * 3 + unit[0])
                            load_ada(0, i * per + aunit[0])
                            load(0, i * 3 + (unit[0] + 1))
                            load(1, i * 3 + (unit[0] + 2))
                            if per == 2:
                                load_ada(1, i * per + (aunit[0] + 1))
                            us.leave()
                            ua.leave()
                        unit[0] += 3 * steps
                        aunit[0] += per * steps
                    load(2, unit[0])
                    unit[0] += 1
                    if n in (0, 3):
                        load_brow(GATES_BEFORE[n] + 1)
                else:
                    blocks, outs = BLOCKS_OUTS[kind]
                    if kind == "mb":
                        sp.wait_ge(S["tr_ok"], 4 * n + 4)
                        sp.dma_start(nwm, bass.AP(nw_mb.tensor, 0, [[0, P], [1, DI]])).then_inc(S["nwm_in"], 16)
                    if kind == "hy":
                        for t in range(T):
                            sp.wait_ge(x_new[t], n)
                        sp.wait_ge(S["scratch_out"], 16)
                        sp.dma_start(bmr[:, :, 0:P], bass.AP(scratch.tensor, 0, [[1, P], [REL, H_AT], [1, P]]))\
                          .then_inc(S["bmr_in"], 16)
                        sp.dma_start(bmr[:, :, P:SEQ], bass.AP(scratch.tensor, P, [[1, P], [REL, H_AT], [1, P]]))\
                          .then_inc(S["bmr_in"], 16)
                    if kind == "ml":
                        sp.wait_ge(S["tr_ok"], 4 * n + 4)
                        sp.wait_ge(S["pre_lo"], 2 * n + 2)
                        sp.wait_ge(S["ml_gate"], 1)
                    if kind == "ml":
                        for j in range(4):
                            load(0, unit[0])
                            load_ada(j % 2, aunit[0], araw2)
                            load(1, unit[0] + 1)
                            unit[0] += 2
                            aunit[0] += 1
                        blocks = 2
                    with sp.Fori(0, blocks) as i:
                        us.enter(i, blocks)
                        load(0, i * 2 + unit[0])
                        if kind == "ml":
                            ua.enter(i, blocks)
                            load_ada(0, i * 2 + aunit[0], araw2)
                            load_ada(1, i * 2 + (aunit[0] + 1), araw2)
                            ua.leave()
                        load(1, i * 2 + (unit[0] + 1))
                        us.leave()
                    unit[0] += 2 * blocks
                    if kind == "ml":
                        aunit[0] += 2 * blocks
                    for u in range(2, outs):
                        load(out_slot(kind, u), unit[0])
                        unit[0] += 1
                        if kind == "ml":
                            for s in range(2):
                                load_ada(s, aunit[0], araw2)
                                aunit[0] += 1
                    if kind == "ml":
                        sp.wait_ge(S["ml_tr"], 2)
                        sp.dma_start(brow2[:, :, :], bass.AP(bcast.tensor, 2 * 2 * D, [[0, P], [1, 2 * D]]))\
                          .then_inc(S["brow2_in"], 16)
                    if kind != "hy":
                        load(0, unit[0])
                        load(1, unit[0] + 1)
                        unit[0] += 2
                    else:
                        sp.dma_start(gp[:, 1, :], bass.AP(bcast.tensor, 13 * D, [[0, P], [1, D]])).then_inc(S["fg_in"], 16)
            for t in range(T):
                sp.wait_ge(S["hy_out"], t + 1)
                sp.dma_start(out[t * P:(t + 1) * P, :], vh[:, t, :]).then_inc(S["out_in"], 16)
            sp.wait_ge(S["out_in"], 16 * T)

        @block.gpsimd
        def _(pool):
            c = Count(S["acc_pool"])

            def step(ins):
                c.on(ins)
                pool.wait_ge(c.sem, c.n)

            pool.memset(zero[:, :], 0.0).then_inc(S["const"], 1)
            pool.memset(ones[:, :], 1.0).then_inc(S["const"], 1)
            pool.memset(negh[:, :], -0.5).then_inc(S["const"], 1)
            step(pool.memset(ident[:, :], 0.0))
            pool.affine_select(out=ident[:, :], in_=ident[:, :], compare_op=ALU.not_equal, fill=1.0, base=0,
                               pattern=[[-1, P]], channel_multiplier=1).then_inc(S["const"], 1)
            pool.memset(acc, 0.0).then_inc(S["zero_acc"], 1)
            step(pool.memset(mask[:, :], 0.0))
            pool.affine_select(out=mask[:, 0:P], in_=mask[:, 0:P], compare_op=ALU.is_ge, fill=NEG, base=0,
                               pattern=[[1, P]], channel_multiplier=-1).then_inc(S["const"], 1)

            taken = {}

            def inv_rms(src, dst, count, ready):
                w = src.shape[1]
                step(pool.tensor_scalar(base[:, 0:w], src, 1.0 / count, EPS, ALU.mult, ALU.add))
                pool.tensor_tensor(dst, base[:, 0:w], negh[:, 0:w], ALU.pow).then_inc(ready, 1)
                taken[ready.name] = taken.get(ready.name, 0) + 1
                pool.wait_ge(ready, taken[ready.name])

            for n, kind in enumerate(KIND):
                for t in range(T):
                    pool.wait_ge(S["pre_ss"], 2 * n + t + 1)
                    inv_rms(ssx[:, n, t:t + 1], ssx[:, n, 2 + t:3 + t], D, S["pre_rstd"])
                if n == 2:
                    pool.wait_ge(S["gp_ok"], 3)
                if n in (2, 3, 5):
                    pool.wait_ge(S["mod_gate"], GATES_BEFORE[n])
                    pool.memset({2: acc, 3: acc[:, 3 * D:6 * D], 5: acc[:, 0:3 * D]}[n], 0.0).then_inc(S["zero_acc"], 1)
                if n == 1:
                    for s in range(2):
                        pool.wait_ge(a_used[s], A_TOTAL[0][s])
                    pool.memset(acc2, 0.0).then_inc(S["zero_acc2"], 1)
                if kind == "ml":
                    pool.wait_ge(S["mlc_in"], 64)
                    for pair in range(2):
                        v_ = slice(pair * 2 * DV, (pair + 1) * 2 * DV)
                        for t in range(T):
                            pool.wait_ge(pj_free[t], PROJ_BEFORE[n] + 4 + pair + 1 + ONE)
                            pool.tensor_tensor(og[:, t, v_], og[:, t, v_], nwl[:, v_], ALU.mult).then_inc(S["ml_gw"], 1)
                        pool.wait_ge(S["ml_ss"], 4 * pair + 4)
                        inv_rms(sm[:, 3, 4 * pair:4 * pair + 4], sm[:, 4, 4 * pair:4 * pair + 4], DV, S["ml_rs"])
                if kind == "mb":
                    for gr in range(GROUPS):
                        pool.wait_ge(S["mb_xs"], GROUPS)
                        if gr:
                            pool.wait_ge(S["mb_z"], 2 * gr)
                        for t in range(T):
                            pool.tensor_tensor(
                                xd[:, t, :].rearrange("p (h d) -> p h d", d=HD),
                                xs[:, t, gr * 512:(gr + 1) * 512].rearrange("p (h d) -> p h d", d=HD),
                                mbd_sb[:, gr * HPG:(gr + 1) * HPG].unsqueeze(2).to_broadcast([P, HPG, HD]),
                                ALU.mult).then_inc(S["mb_xd"], 1)
                        pool.wait_ge(S["mb_ss"], 2 * gr + 2)
                        inv_rms(sg[:, 0, 2 * gr:2 * gr + 2], sg[:, 1, 2 * gr:2 * gr + 2], 512, S["mb_rs"])
                if kind == "hy":
                    pool.wait_ge(S["bmr_in"], 32)
                    step(pool.memset(jrev, 0.0))
                    pool.affine_select(out=jrev, in_=jrev, compare_op=ALU.not_equal, fill=1.0, base=1 - P,
                                       pattern=[[1, P]], channel_multiplier=1).then_inc(S["hy_gs"], 1)
                    for t in range(T):
                        pool.wait_ge(S["hy_fs"], t + 1)
                        inv_rms(ssx[:, n, 4 + t:5 + t], ssx[:, n, 6 + t:7 + t], D, S["hy_fr"])
                else:
                    for t in range(T):
                        pool.wait_ge(S["post_ss"], 2 * n + t + 1)
                        inv_rms(ssx[:, n, 4 + t:5 + t], ssx[:, n, 6 + t:7 + t], D, S["post_rstd"])

        @block.scalar
        def _(act):
            c = Count(S["acc_act"])
            us = Uses(SLOTS)

            for q in pj_free + [S["mb_silu"]]:
                act.sem_inc(q, ONE)

            def hi(s):
                n = us.next(s)
                act.wait_ge(w_in[s], 16 * n + 16)
                if us.i is not None or n > 0:
                    act.wait_ge(w_used[s], n + CREDIT[s])
                act.activation(whi[:, s, :], raw[:, s, :], ACT.Copy).then_inc(w_hi[s], 1)

            def project(blocks, evacs, pb):
                with act.Fori(0, blocks) as i:
                    us.enter(i, blocks)
                    hi(0)
                    act.wait_ge(pj_ok[0], i + (pb + 1))
                    evacs(0, i)
                    hi(1)
                    evacs(1, i)
                    us.leave()

            def first_block(evacs, pb):
                hi(0)
                act.wait_ge(pj_ok[0], pb + 1)
                evacs(0, 0)
                hi(1)
                evacs(1, 0)

            def after_piece(p, pb, evac):
                blk, part = divmod(p, 4)
                if part == 1:
                    hi(0)
                if part == 2:
                    act.wait_ge(pj_ok[0], pb + blk + 1)
                    evac(0, blk)
                if part == 3:
                    hi(1)
                    evac(1, blk)

            def out_units(kind, outs):
                for u in range(2, outs):
                    hi(out_slot(kind, u))
                hi(0)

            act.wait_ge(S["cols_ok"], 1)
            act.activation(cT[:, :], cols[:, ROW_C:ROW_C + 16], ACT.Silu).then_inc(S["c_ok"], 1)

            for n, kind in enumerate(KIND):
                for t in range(T):
                    if n == 0:
                        act.wait_ge(S["x_in"], 16)
                    else:
                        act.wait_ge(x_new[t], n)
                    act.activation(hfl[:, t * D:(t + 1) * D], x[:, t, :], ACT.Square,
                                   accum_out=ssx[:, n, t:t + 1]).then_inc(S["pre_ss"], 1)
                if n in (2, 5):
                    hi(1)
                if n == 0:
                    hi(0)
                    hi(1)
                for q in range(4):
                    act.wait_ge(S["pre_hf"], 4 * n + q + 1)
                    act.activation(xhi[:, 2 * q:2 * q + 2, :], hf[:, 2 * q:2 * q + 2, :], ACT.Copy)\
                       .then_inc(S["pre_hi"], 1)
                if kind == "ffn":
                    f = FFN_NO[n]

                    def silu(t, done):
                        if done is not None:
                            act.wait_ge(g_ok[t], done)
                        act.activation(sil[:, t, :], ps[:, 4 + t, 0:FB], ACT.Silu).then_inc(sil_ok[t], 1)

                    hi(0)
                    act.wait_ge(s1_ok[0], NF * f + 1)
                    silu(0, NF * f if f else None)
                    hi(1)
                    silu(1, NF * f if f else None)
                    with act.Fori(0, NF - 1) as i:
                        us.enter(i, NF - 1)
                        hi(2)
                        act.wait_ge(S["gt_ps"], i + (NF * f + 1))
                        act.activation(xhi[:, 8:10, :], ps[:, 6, :], ACT.Copy).then_inc(S["gt_hi"], 1)
                        hi(0)
                        act.wait_ge(s1_ok[0], i + (NF * f + 2))
                        silu(0, i + (NF * f + 1))
                        hi(1)
                        silu(1, i + (NF * f + 1))
                        us.leave()
                    act.wait_ge(w_used[2], us.n[2] + CREDIT[2])
                    act.wait_ge(S["gt_ps"], NF * f + NF)
                    act.activation(xhi[:, 8:10, :], ps[:, 6, :], ACT.Copy).then_inc(S["gt_hi"], 1)
                    hi(2)
                if kind == "ml":
                    act.wait_ge(S["gp_ok"], GATES_BEFORE[n])
                    act.wait_ge(S["ml_na"], 1)
                    act.activation(gt[0:4, 3, :], gt[0:4, 2, :], ACT.Exp).then_inc(S["ml_e"], 1)
                    act.wait_ge(S["ml_u"], 1)
                    act.activation(gt[0:4, 5, :], gt[0:4, 4, :], ACT.Ln).then_inc(S["ml_l"], 1)

                    def ev_qk(b, i):
                        act.activation(qkT[:, bass.ds(i * 4 + 2 * b, 2), :],
                                       ps[:, 4 + b, :].rearrange("p (a b) -> p a b", b=SEQ), ACT.Copy)\
                           .then_inc(pj_free[b], 1)

                    def ev_v(b, i):
                        act.activation(vv[:, b, bass.ds(i * 512, 512)], ps[:, 4 + b, :], ACT.Copy)\
                           .then_inc(pj_free[b], 1)

                    def ev_o(b, i):
                        act.activation(og[:, b, i * 512:(i + 1) * 512], ps[:, 4 + b, :], ACT.Sigmoid)\
                           .then_inc(pj_free[b], 1)

                    pb = PROJ_BEFORE[n]
                    first_block(ev_qk, pb)
                    act.wait_ge(S["ml_rows"], 1)
                    act.activation(gt[0:4, 3, :], gt[0:4, 2, :], ACT.Exp, scale=-1.0).then_inc(S["ml_em"], 1)
                    project(1, lambda b, i: ev_qk(b, i + 1), pb + 1)
                    project(2, ev_v, pb + 2)
                    act.wait_ge(S["ml_arg"], H_ML)
                    act.activation(E_ml[:, :, :], E_ml[:, :, :], ACT.Exp).then_inc(S["ml_E"], 1)

                    def squares(pair):
                        act.wait_ge(S["ml_r"], pair + 1)
                        for t in range(T):
                            for h in (2 * pair, 2 * pair + 1):
                                j = 4 * pair + 2 * (h % 2) + t
                                act.activation(ml_junk(h, t),
                                               ps[:, 2 * t + pair, (h % 2) * DV:(h % 2 + 1) * DV], ACT.Square,
                                               scale=sm[:, 2, j:j + 1], accum_out=sm[:, 3, j:j + 1])\
                                   .then_inc(S["ml_ss"], 1)

                    for p in range(4):
                        after_piece(p, pb + 4, ev_o)
                    squares(0)
                    for p in range(4, 8):
                        after_piece(p, pb + 4, ev_o)
                    squares(1)
                    for q in range(2):
                        act.wait_ge(S["ml_tr"], q + 1)
                        act.activation(xhi[:, 4 * q:4 * q + 4, :], ps[:, 4 + 2 * q:6 + 2 * q, :], ACT.Copy)\
                           .then_inc(S["ml_hi"], 1)
                    out_units("ml", 4)
                if kind == "mb":
                    act.wait_ge(S["gp_ok"], GATES_BEFORE[n])
                    act.wait_ge(S["mb_na"], 1)
                    act.activation(dtt[0:H_MB, 2, :], dtt[0:H_MB, 1, :], ACT.Exp).then_inc(S["mb_e"], 1)
                    act.wait_ge(S["mbc_in"], 48)
                    act.activation(sg[0:H_MB, 0, 0:1], mbv_sb[:, 1:2], ACT.Exp).then_inc(S["mb_eA"], 1)
                    act.wait_ge(S["mb_u"], 1)
                    act.activation(dtt[0:H_MB, 4, :], dtt[0:H_MB, 3, :], ACT.Ln).then_inc(S["mb_l"], 1)

                    def ev_z(b, i):
                        act.activation(zs[:, b, i * 512:(i + 1) * 512], ps[:, 4 + b, :], ACT.Copy)\
                           .then_inc(pj_free[b], 1)

                    def ev_x(b, i, base=0):
                        i = i + base
                        act.wait_ge(S["mb_conv"], i * 2 + ONE)
                        act.wait_ge(S["mb_silu"], i * 2 + ONE)
                        for k in range(2):
                            q = 2 * b + k
                            act.activation(cacc[:, q, :], ps[:, 4 + b, k * SEQ:(k + 1) * SEQ], ACT.Identity,
                                           scale=cols[:, bass.ds(i * 4 + (ROW_MBW + 3 * CONV_F + q), 1)],
                                           bias=cols[:, bass.ds(i * 4 + (ROW_MBW + 4 * CONV_F + q), 1)])\
                               .then_inc(S["mb_cv0"], 1)
                        act.activation(cin[:, 2 * b:2 * b + 2, :],
                                       ps[:, 4 + b, :].rearrange("p (a b) -> p a b", b=SEQ), ACT.Copy)\
                           .then_inc(pj_free[b], 1)
                        if b:
                            for bb in range(2):
                                act.wait_ge(S["mb_conv"], i * 2 + (bb + 1 + ONE))
                                act.activation(xcT[:, bass.ds(i * 4 + 2 * bb, 2), :], cacc[:, 2 * bb:2 * bb + 2, :],
                                               ACT.Silu).then_inc(S["mb_silu"], 1)

                    pb = PROJ_BEFORE[n]
                    first_block(ev_x, pb)
                    project(4, lambda b, i: ev_x(b, i, 1), pb + 1)

                    def x_by_token(k):
                        act.wait_ge(S["mb_xtr"], k + 1)
                        act.activation(xs[:, k % 2, (k // 2) * D:(k // 2 + 1) * D], ps[:, 2 * (k % 2):2 * (k % 2) + 2, :],
                                       ACT.Copy).then_inc(S["mb_xs"], 1)

                    x_by_token(0)
                    x_by_token(1)
                    project(1, lambda b, i: ev_x(b, i, 5), pb + 5)
                    x_by_token(2)
                    x_by_token(3)

                    def decays(p):
                        act.wait_ge(S["mb_arg"], p + 1)
                        act.activation(E_mb[:, p % 2, :], E_mb[:, p % 2, :], ACT.Exp).then_inc(S["mb_E"], 1)

                    def silu_z(gr):
                        s_ = slice(gr * 512, (gr + 1) * 512)
                        act.wait_ge(pj_free[1], pb + 6 + gr + 1 + ONE)
                        act.activation(zs[:, :, s_], zs[:, :, s_], ACT.Silu).then_inc(S["mb_zs"], 1)

                    def squares(gr):
                        for t in range(T):
                            act.wait_ge(S["mb_z"], 2 * gr + t + 1)
                            act.activation(xj[:, t, :], zs[:, t, gr * 512:(gr + 1) * 512], ACT.Square,
                                           accum_out=sg[:, 0, 2 * gr + t:2 * gr + t + 1]).then_inc(S["mb_ss"], 1)

                    decays(0)
                    for p in range(16):
                        gr = p // 4
                        if p + 1 < 16:
                            decays(p + 1)
                        after_piece(p, pb + 6, ev_z)
                        if p % 4 == 0 and gr:
                            silu_z(gr - 1)
                        if p % 4 == 2 and gr:
                            squares(gr - 1)
                    silu_z(GROUPS - 1)

                    def turned_hi(gr):
                        act.wait_ge(S["mb_tr"], gr + 1)
                        act.activation(xhi[:, 4 * gr:4 * gr + 4, :], ps[:, TURNED[gr]:TURNED[gr] + 2, :], ACT.Copy)\
                           .then_inc(S["mb_hi"], 1)

                    for gr in range(3):
                        turned_hi(gr)
                    squares(GROUPS - 1)
                    hi(2)
                    hi(0)
                    turned_hi(3)
                    for u in range(4, 9):
                        hi(u % SLOTS if u < 8 else 0)
                if kind == "hy":
                    for k in range(4):
                        act.wait_ge(S["hy_flip"], k + 1)
                        act.activation(bm[:, 2 * k:2 * k + 2, :], ps[:, 4 + k % 2, :]
                                       .rearrange("p (a b) -> p a b", b=SEQ), ACT.Copy).then_inc(S["hy_bm"], 1)

                    def ev_h(first, func):
                        def ev(b, i):
                            act.activation(hT[:, bass.ds(i * 4 + (first + 2 * b), 2), :],
                                           ps[:, 4 + b, :].rearrange("p (a b) -> p a b", b=SEQ), func)\
                               .then_inc(pj_free[b], 1)
                        return ev

                    def ev_vh(b, i):
                        act.activation(vh[:, b, bass.ds(i * 512, 512)], ps[:, 4 + b, :], ACT.Copy)\
                           .then_inc(pj_free[b], 1)

                    def ev_m(b, i):
                        act.activation(sgm[:, b, bass.ds(i * 512, 512)], ps[:, 4 + b, :], ACT.Sigmoid)\
                           .then_inc(pj_free[b], 1)

                    pb = PROJ_BEFORE[n]
                    project(4, ev_h(0, ACT.Copy), pb)
                    project(2, ev_vh, pb + 4)
                    project(2, ev_h(16, ACT.Silu), pb + 6)

                    def softmax(h):
                        act.wait_ge(S["hy_L"], h + 1)
                        for t in range(T):
                            sl = slice(0, P) if t == 0 else slice(P, 384)
                            act.activation(P_at[:, h % 2, sl], L_at[:, h % 2, sl], ACT.Exp,
                                           bias=stat[:, h, 2 + t:3 + t], accum_out=stat[:, h, 4 + t:5 + t])\
                               .then_inc(S["hy_P"], 1)

                    softmax(0)
                    for h in range(H_AT):
                        if h + 1 < H_AT:
                            softmax(h + 1)
                        if h:
                            after_piece(2 * h - 1, pb + 8, ev_h(24, ACT.Copy))
                        act.wait_ge(S["hy_pt"], h + 1)
                        act.activation(L_at[:, h % 2, :], ps[:, 3, 0:384], ACT.Copy).then_inc(S["hy_ptc"], 1)
                        after_piece(2 * h, pb + 8, ev_h(24, ACT.Copy))
                    after_piece(15, pb + 8, ev_h(24, ACT.Copy))
                    act.wait_ge(S["hy_at"], H_AT)
                    act.activation(xhi[:, 8:16, :], hT[:, 16:24, :], ACT.Copy).then_inc(S["hy_ga"], 1)
                    project(2, ev_h(40, ACT.Copy), pb + 12)
                    project(2, ev_h(48, ACT.Silu), pb + 14)
                    project(4, ev_m, pb + 16)
                    hi(2)
                    act.wait_ge(S["hy_cv"], 4)
                    act.activation(xhi[:, 0:8, :], hT[:, 40:48, :], ACT.Copy).then_inc(S["hy_chi"], 1)
                    for u in range(3, 8):
                        hi(u % SLOTS)
                    for q in range(2):
                        act.wait_ge(S["hy_mtr"], q + 1)
                        act.activation(xhi[:, 8 + 4 * q:12 + 4 * q, :], ps[:, 2 * q:2 * q + 2, :], ACT.Copy)\
                           .then_inc(S["hy_mhi"], 1)
                    for u in range(8, 12):
                        hi(u % SLOTS)
                    for t in range(T):
                        act.wait_ge(S["hy_fx"], t + 1)
                        act.activation(hfl[:, t * D:(t + 1) * D], x[:, t, :], ACT.Square,
                                       accum_out=ssx[:, n, 4 + t:5 + t]).then_inc(S["hy_fs"], 1)
                else:
                    if n == 1:
                        act.wait_ge(a_used[1], A_TOTAL[1][1])
                    for t in range(T):
                        wait_y(act, n, t)
                        act.activation(hfl[:, t * D:(t + 1) * D], ps[:, 2 * t:2 * t + 2, :], ACT.Square,
                                       accum_out=ssx[:, n, 4 + t:5 + t]).then_inc(S["post_ss"], 1)

        @block.tensor
        def _(pe):
            us = Uses(SLOTS)
            pe.sem_inc(w_used[2], CREDIT[2])

            def mm(out, lhsT, rhs, start=False, stop=False):
                return pe.matmul(out, lhsT, rhs, start=start, stop=stop, skip_group_check=True)

            def three(out, ahi, alo, bhi, blo, start=False, stop=False):
                mm(out, ahi, bhi, start=start)
                mm(out, ahi, blo)
                return mm(out, alo, bhi, stop=stop)

            def ready(s):
                pe.wait_ge(w_lo[s], us.next(s) + (1 + CREDIT[s]))

            def by_token(s, t):
                for kk in range(4):
                    k = 4 * s + kk
                    w = slice(kk * 512, kk * 512 + 512)
                    r = three(ps[:, 4 + t, :], xhi[:, k, t * P:(t + 1) * P], xlo[:, k, t * P:(t + 1) * P],
                              whi[:, s, w], wlo[:, s, w], start=(k == 0), stop=(k == 7))
                return r

            def by_feature(s, q):
                for kk in range(4):
                    k = 4 * s + kk
                    w = slice(kk * 512 + q * P, kk * 512 + q * P + P)
                    r = three(ps[:, 4 + q // 2, (q % 2) * SEQ:(q % 2 + 1) * SEQ], whi[:, s, w], wlo[:, s, w],
                              xhi[:, k, :], xlo[:, k, :], start=(k == 0 and q % 2 == 0), stop=(k == 7))
                return r

            def project(blocks, token, pb):
                with pe.Fori(0, blocks) as i:
                    us.enter(i, blocks)
                    ready(0)
                    if token:
                        pe.wait_ge(pj_free[0], i + (pb + ONE))
                        by_token(0, 0)
                        pe.wait_ge(pj_free[1], i + (pb + ONE))
                        by_token(0, 1).then_inc(w_used[0], 1)
                        ready(1)
                        by_token(1, 0).then_inc(pj_ok[0], 1)
                        by_token(1, 1).then_inc(w_used[1], 1)
                    else:
                        for b in range(2):
                            pe.wait_ge(pj_free[b], i + (pb + ONE))
                            by_feature(0, 2 * b)
                            r = by_feature(0, 2 * b + 1)
                        r.then_inc(w_used[0], 1)
                        ready(1)
                        by_feature(1, 0)
                        by_feature(1, 1).then_inc(pj_ok[0], 1)
                        by_feature(1, 2)
                        by_feature(1, 3).then_inc(w_used[1], 1)
                    us.leave()

            def token_piece(p, pb):
                blk, part = divmod(p, 4)
                s, t = divmod(part, 2)
                if t == 0:
                    ready(s)
                if s == 0:
                    pe.wait_ge(pj_free[t], pb + blk + ONE)
                r = by_token(s, t)
                if part:
                    r.then_inc((None, w_used[0], pj_ok[0], w_used[1])[part], 1)

            def feature_piece(p, pb):
                blk, part = divmod(p, 4)
                s, b = divmod(part, 2)
                if b == 0:
                    ready(s)
                if s == 0:
                    pe.wait_ge(pj_free[b], pb + blk + ONE)
                by_feature(s, 2 * b)
                r = by_feature(s, 2 * b + 1)
                if part:
                    r.then_inc((None, w_used[0], pj_ok[0], w_used[1])[part], 1)

            def down(s, k, start=False, stop=False, done0=None, bank=0):
                ready(s)
                for t in range(T):
                    for kk in range(2):
                        for n in range(2):
                            w = slice(kk * D + n * 512, kk * D + n * 512 + 512)
                            r = three(ps[:, bank + 2 * t + n, :], xhi[:, k + kk, t * P:(t + 1) * P],
                                      xlo[:, k + kk, t * P:(t + 1) * P], whi[:, s, w], wlo[:, s, w],
                                      start=start and kk == 0, stop=stop and kk == 1)
                    if t == 0 and done0 is not None:
                        r.then_inc(done0, 1)
                r.then_inc(w_used[s], 1)

            def mod_sums(k):
                return acc2 if k == 2 else acc[:, 3 * D * (k % 2):3 * D * (k % 2) + 3 * D]

            def shift_scale(k, when):
                if k:
                    pe.wait_ge(S["mods_ok"], k)
                for q in range(16):
                    if q in (0, 8):
                        for s in range(2):
                            pe.wait_ge(a_used[s], 2 if when == "start" and q == 0 else A_TOTAL[when][s])
                    r = mm(ps[:, 7, q:q + 1], mod_sums(k)[:, q * P:(q + 1) * P], ones[:, 0:1], start=True, stop=True)
                r.then_inc(S["mod_cols"], 1)

            def gate(k, when):
                for s in range(2):
                    pe.wait_ge(a_used[s], A_TOTAL[when][s])
                if k:
                    pe.wait_ge(S["gate_read"], k)
                for q in range(2):
                    r = mm(ps[:, 4 + q, :], ones[:, 0:P], mod_sums(k)[:, 2 * D + q * 512:2 * D + (q + 1) * 512],
                           start=True, stop=True)
                r.then_inc(S["mod_gate"], 1)

            pe.wait_ge(S["const"], 5)
            pe.wait_ge(S["rows_in"], 16)
            for a in range(3):
                r = pe.transpose(ps[:, 6, a * P:(a + 1) * P], vrow[:, a, :], ident[:, :])
            r.then_inc(S["cols_tr"], 1)
            pe.wait_ge(S["bias_in"], 48)
            mm(ps[0:H_AT, 5, 0:REL], rel_sb[0:32, :], oneh_sb[0:32, :], start=True, stop=True).then_inc(S["wd_ps"], 1)
            pe.wait_ge(S["wd_ok"], 1)

            for n, kind in enumerate(KIND):
                xn = xn_of(n)
                for t in range(T):
                    pe.wait_ge(S["xn_ok"], 2 * n + t + 1)
                    for k in range(KT):
                        r = pe.transpose(ps[:, k // 2, (k % 2) * SEQ + t * P:(k % 2) * SEQ + (t + 1) * P],
                                         xn[:, t, k * P:(k + 1) * P], ident[:, :])
                        if t == 1 and k % 2:
                            r.then_inc(S["tr_ok"], 1)
                if n == 0:
                    shift_scale(0, "start")
                if n == 4:
                    gate(5, 3)
                if kind == "hy":
                    pe.wait_ge(S["gate_read"], GATES_BEFORE[n])
                    pe.wait_ge(S["hy_gs"], 1)
                    for k in range(4):
                        if k >= 2:
                            pe.wait_ge(S["hy_bm"], k - 1)
                        mm(ps[:, 4 + k % 2, :], jrev, bmr[:, 2 * k:2 * k + 2, :], start=True, stop=True)\
                            .then_inc(S["hy_flip"], 1)
                    pe.wait_ge(S["hy_bm"], 4)
                if n:
                    pe.wait_ge(S["gate_read"], GATES_BEFORE[n])
                pe.wait_ge(S["pre_lo"], 2 * n + 1)
                if kind == "ffn":
                    f = FFN_NO[n]
                    b = NF * f

                    def turn(i):
                        for t in range(T):
                            pe.wait_ge(g_ok[t], i + (b + 1))
                        pe.wait_ge(S["gt_lo"], i + (b + ONE))
                        for kk in range(2):
                            for t in range(T):
                                r = pe.transpose(ps[:, 6, kk * SEQ + t * P:kk * SEQ + (t + 1) * P],
                                                 g[:, t, kk * P:(kk + 1) * P], ident[:, :])
                        r.then_inc(S["gt_ps"], 1)

                    ready(0)
                    by_token(0, 0)
                    by_token(0, 1).then_inc(w_used[0], 1)
                    ready(1)
                    pe.wait_ge(S["pre_lo"], 2 * n + 2)
                    by_token(1, 0).then_inc(s1_ok[0], 1)
                    by_token(1, 1).then_inc(w_used[1], 1)
                    for q in range(4):
                        mm(ps[:, q, :], zero[0:1, 0:P], zero[0:1, :], start=True)
                    for first, steps, _, _ in ada_steps(n):
                        with pe.Fori(0, steps) as i:
                            us.enter(i, steps)
                            ready(0)
                            for t in range(T):
                                pe.wait_ge(g_ok[t], i + (b + first + 1))
                                r = by_token(0, t)
                            r.then_inc(w_used[0], 1)
                            turn(i + first)
                            ready(1)
                            by_token(1, 0).then_inc(s1_ok[0], 1)
                            by_token(1, 1).then_inc(w_used[1], 1)
                            pe.wait_ge(S["gt_lo"], i + (b + first + 1 + ONE))
                            down(2, 8)
                            us.leave()
                    turn(NF - 1)
                    if n == 0:
                        gate(0, 0)
                        shift_scale(1, 0)
                    else:
                        k = {2: 3, 3: 4, 5: 6}[n]
                        shift_scale(k, n)
                        gate(k, n)
                    pe.wait_ge(S["gt_lo"], b + NF + ONE)
                    down(2, 8, stop=True, done0=y_done[0])
                    if n == 0:
                        gate(1, 0)
                    if n == 3:
                        shift_scale(5, n)
                if kind == "ml":
                    pe.wait_ge(S["mlc_in"], 64)
                    pe.wait_ge(S["pre_lo"], 2 * n + 2)
                    pe.wait_ge(S["mods_ok"], GATES_BEFORE[n])
                    for k in range(KT):
                        r = mm(ps[0:36, 7, 0:SEQ], mlw_sb[:, k, :], hf[:, k, :], start=(k == 0), stop=(k == 7))
                    r.then_inc(S["ml_gate"], 1)
                    pb = PROJ_BEFORE[n]
                    project(2, False, pb)
                    pe.wait_ge(S["ml_rows"], 2)
                    pe.wait_ge(S["ml_em"], 1)
                    for j, row in enumerate((8, 3)):
                        for t in range(T):
                            r = pe.transpose(ps[:, 7, 256 + (t * 2 + j) * 4:256 + (t * 2 + j) * 4 + 4],
                                             gt[0:4, row, t * P:(t + 1) * P], ident[0:4, 0:4])
                    r.then_inc(S["ml_ct"], 1)
                    project(2, True, pb + 2)
                    pe.wait_ge(S["ml_cols"], 1)
                    for h in range(H_ML):
                        mm(ps[:, h, 0:SEQ], ident[0:4, h:h + 1].to_broadcast([4, P]), gt[0:4, 1, :],
                           start=True, stop=True).then_inc(S["ml_nm"], 1)

                    def scores(h):
                        if h >= 2:
                            pe.wait_ge(S["ml_den"], h - 1)
                        b = 6 + h % 2
                        mm(ps[:, b, 0:SEQ], qkT[:, 4 + h, 0:P], qkT[:, h, :], start=True, stop=True)
                        mm(ps[:, b, SEQ:384], qkT[:, 4 + h, P:SEQ], qkT[:, h, P:SEQ], start=True, stop=True)\
                            .then_inc(S["ml_sc"], 1)

                    scores(0)
                    scores(1)
                    token_piece(0, pb + 4)
                    for h in range(H_ML):
                        token_piece(2 * h + 1, pb + 4)
                        pe.wait_ge(S["ml_ST"], h + 1)
                        e0, e1, e2 = (E_ml[:, h, k * P:(k + 1) * P] for k in range(3))
                        v0, v1 = (vv[:, t, h * DV:(h + 1) * DV] for t in range(2))
                        o0, o1 = (ps[:, 2 * t + h // 2, (h % 2) * DV:(h % 2 + 1) * DV] for t in range(2))
                        d0, d1 = (ps[:, 6 + h % 2, 384 + t:385 + t] for t in range(2))
                        mm(o0, e0, v0, start=True, stop=True)
                        mm(o1, e1, v0, start=True)
                        mm(o1, e2, v1, stop=True)
                        mm(d0, e0, ones[:, 0:1], start=True, stop=True)
                        mm(d1, e1, ones[:, 0:1], start=True)
                        mm(d1, e2, ones[:, 0:1], stop=True).then_inc(S["ml_nd"], 1)
                        if h < 3:
                            token_piece(2 * h + 2, pb + 4)
                        if h + 2 < H_ML:
                            scores(h + 2)
                    pe.wait_ge(S["ml_am"], 8)
                    for k in range(KT):
                        for t in range(T):
                            r = pe.transpose(ps[:, 4 + k // 2, (k % 2) * SEQ + t * P:(k % 2) * SEQ + (t + 1) * P],
                                             am[:, t, k * P:(k + 1) * P], ident[:, :])
                        if k % 4 == 3:
                            r.then_inc(S["ml_tr"], 1)
                    for u in range(4):
                        pe.wait_ge(S["ml_lo"], u // 2 + 1)
                        down(out_slot(kind, u), 2 * u, start=(u == 0), stop=(u == 3),
                             done0=y_done[0] if u == 3 else None)
                    shift_scale(2, 1)
                    gate(2, 1)
                if kind == "mb":
                    pe.wait_ge(S["mbc_in"], 48)
                    pe.wait_ge(S["pre_lo"], 2 * n + 2)
                    pe.wait_ge(S["mods_ok"], GATES_BEFORE[n])
                    for k in range(KT):
                        r = mm(ps[0:H_MB, 7, 0:SEQ], mbw_sb[:, k, :], hf[:, k, :], start=(k == 0), stop=(k == 7))
                    r.then_inc(S["mb_gate"], 1)
                    pb = PROJ_BEFORE[n]
                    project(5, False, pb)
                    pe.wait_ge(S["mb_rows"], 1)
                    for j, row in enumerate((5, 3)):
                        for t in range(T):
                            r = pe.transpose(ps[:, 7, 256 + (2 * j + t) * 32:256 + (2 * j + t + 1) * 32],
                                             dtt[0:H_MB, row, t * P:(t + 1) * P], ident[0:H_MB, 0:H_MB])
                    r.then_inc(S["mb_ct"], 1)
                    pe.wait_ge(S["mb_silu"], 8 + ONE)

                    def x_by_token(k):
                        if k >= 2:
                            pe.wait_ge(S["mb_xs"], k - 1)
                        for q in range(8):
                            r = pe.transpose(ps[:, 2 * (k % 2) + q // 4, (q % 4) * P:(q % 4 + 1) * P],
                                             xcT[:, 8 * (k // 2) + q, (k % 2) * P:(k % 2 + 1) * P], ident[:, :])
                        r.then_inc(S["mb_xtr"], 1)

                    x_by_token(0)
                    x_by_token(1)
                    project(1, False, pb + 5)
                    x_by_token(2)
                    x_by_token(3)
                    token_piece(0, pb + 6)

                    def cb(gr):
                        if gr == 0:
                            pe.wait_ge(S["mb_silu"], 12 + ONE)
                        if gr >= 2:
                            pe.wait_ge(S["mb_W"], 4 * (gr - 1))
                        bT, cT_ = xcT[:, 16 + gr, :], xcT[:, 20 + gr, :]
                        mm(ps[:, 2 + gr % 2, 0:SEQ], bT[:, 0:P], cT_, start=True, stop=True)
                        mm(ps[:, 2 + gr % 2, SEQ:384], bT[:, P:SEQ], cT_[:, P:SEQ], start=True, stop=True)\
                            .then_inc(S["mb_cb"], 1)

                    def decay(p):
                        if p >= 2:
                            pe.wait_ge(S["mb_arg"], p - 1)
                        for j in range(2):
                            h = 2 * p + j
                            r = mm(ps[:, 6 + p % 2, j * SEQ:(j + 1) * SEQ],
                                   ident[0:H_MB, h:h + 1].to_broadcast([H_MB, P]), dtt[0:H_MB, 5, :],
                                   start=True, stop=True)
                        r.then_inc(S["mb_ab"], 1)

                    pe.wait_ge(S["mb_cols"], 1)
                    decay(0)
                    decay(1)
                    pe.wait_ge(S["mb_xs"], GROUPS)
                    token_piece(1, pb + 6)
                    cb(0)
                    for p in range(16):
                        gr = p // 4
                        if p % 4 == 2 and gr + 1 < GROUPS:
                            cb(gr + 1)
                        pe.wait_ge(S["mb_W"], p + 1)
                        if p % 4 == 0 and gr:
                            pe.wait_ge(S["mb_add"], 2 * gr)
                        for j in range(2):
                            h = 2 * p + j
                            hh = h % HPG
                            w0, w1, w2_ = (W_mb[:, p % 2, j * 384 + k * P:j * 384 + (k + 1) * P] for k in range(3))
                            o0, o1 = (ps[:, t, hh * HD:(hh + 1) * HD] for t in range(2))
                            x0, x1 = (xs[:, t, h * HD:(h + 1) * HD] for t in range(2))
                            mm(o0, w0, x0, start=True, stop=True)
                            mm(o1, w1, x0, start=True)
                            r = mm(o1, w2_, x1, stop=True)
                        r.then_inc(S["mb_y"], 1)
                        if p + 2 < 16:
                            decay(p + 2)
                        if p + 2 < 16:
                            token_piece(p + 2, pb + 6)

                    def turn_y(gr):
                        pe.wait_ge(S["mb_yn"], 2 * gr + 2)
                        for k in range(4):
                            for t in range(T):
                                r = pe.transpose(ps[:, TURNED[gr] + k // 2, (k % 2) * SEQ + t * P:(k % 2) * SEQ + (t + 1) * P],
                                                 zs[:, t, (4 * gr + k) * P:(4 * gr + k + 1) * P], ident[:, :])
                        r.then_inc(S["mb_tr"], 1)

                    pe.wait_ge(S["mb_W"], 16)
                    turn_y(0)
                    for t in range(T):
                        pe.wait_ge(pj_free[t], pb + 10 + ONE)
                    turn_y(1)
                    pe.wait_ge(S["mb_add"], 2 * GROUPS)
                    turn_y(2)
                    for u in range(8):
                        if u == 2:
                            turn_y(3)
                        pe.wait_ge(S["mb_lo"], max(u // 2 + 1, 3))
                        down(u % SLOTS, 2 * u, start=(u == 0), stop=(u == 7), done0=y_done[0] if u == 7 else None)
                if kind == "hy":
                    pe.wait_ge(S["pre_lo"], 2 * n + 2)
                    pb = PROJ_BEFORE[n]
                    project(4, False, pb)
                    project(2, True, pb + 4)
                    project(2, False, pb + 6)

                    def logits(h):
                        if h >= 2:
                            pe.wait_ge(S["hy_L"], h - 1)
                        q, k, b = hT[:, h, :], hT[:, 8 + h, :], 6 + h % 2
                        mm(ps[:, b, 0:P], q[:, 0:P], k[:, 0:P], start=True, stop=True)
                        mm(ps[:, b, P:384], q[:, P:SEQ], k, start=True, stop=True).then_inc(S["hy_sc"], 1)

                    logits(0)
                    logits(1)
                    feature_piece(0, pb + 8)
                    for h in range(H_AT):
                        pe.wait_ge(S["hy_Pn"], h + 1)
                        if h:
                            pe.wait_ge(S["hy_ptc"], h)
                        for dst, src in ((0, 0), (1, 1), (2, 2)):
                            r = pe.transpose(ps[:, 3, dst * P:(dst + 1) * P], P_at[:, h % 2, src * P:(src + 1) * P],
                                             ident[:, :])
                        r.then_inc(S["hy_pt"], 1)
                        if h + 2 < H_AT:
                            logits(h + 2)
                        feature_piece(2 * h + 1, pb + 8)
                        pe.wait_ge(S["hy_ptc"], h + 1)
                        if h >= 3:
                            pe.wait_ge(S["hy_at"], h - 2)
                        o = ps[:, h % 3, 0:SEQ]
                        mm(o, vh[:, 0, h * DH:(h + 1) * DH], L_at[:, h % 2, 0:SEQ], start=True)
                        mm(o[:, P:SEQ], vh[:, 1, h * DH:(h + 1) * DH], L_at[:, h % 2, SEQ:384], stop=True)\
                            .then_inc(S["hy_o"], 1)
                        if h + 1 < H_AT:
                            feature_piece(2 * h + 2, pb + 8)
                    project(4, False, pb + 12)
                    project(4, True, pb + 16)
                    pe.wait_ge(S["hy_alo"], 1)
                    for u in range(4):
                        down(u % SLOTS, 8 + 2 * u, start=(u == 0), stop=(u == 3))
                    pe.wait_ge(S["hy_clo"], 1)
                    for t in range(T):
                        pe.wait_ge(pj_free[t], pb + 20 + ONE)
                    for u in range(4, 8):
                        down(u % SLOTS, 2 * (u - 4), start=(u == 4), stop=(u == 7),
                             done0=S["hy_yc"] if u == 7 else None, bank=4)
                    pe.wait_ge(S["hy_ya"], 1)
                    for t in range(T):
                        pe.wait_ge(S["hy_mg"], t + 1)
                        for k in range(KT):
                            r = pe.transpose(ps[:, k // 2, (k % 2) * SEQ + t * P:(k % 2) * SEQ + (t + 1) * P],
                                             mg[:, t, k * P:(k + 1) * P], ident[:, :])
                            if t == 1 and k % 4 == 3:
                                r.then_inc(S["hy_mtr"], 1)
                    for u in range(8, 12):
                        pe.wait_ge(S["hy_mlo"], (u - 8) // 2 + 1)
                        down(u % SLOTS, 8 + 2 * (u - 8), start=(u == 8), stop=(u == 11),
                             done0=y_done[0] if u == 11 else None, bank=4)

        @block.vector
        def _(dve):
            c = Count(S["acc_dve"])
            us = Uses(SLOTS)
            ua = Uses(2)
            for q in (w_lo[2], S["gt_lo"], S["mb_conv"]):
                dve.sem_inc(q, ONE)

            def step(ins):
                c.on(ins)
                dve.wait_ge(c.sem, c.value())

            def mark(ins):
                c.on(ins)

            def lo(s):
                n = us.next(s)
                dve.wait_ge(w_hi[s], n + 1)
                dve.tensor_tensor(wlo[:, s, :], raw[:, s, :], whi[:, s, :].bitcast(F32), ALU.subtract)\
                   .then_inc(w_lo[s], 1)

            def ada(s, a, k0, after, total=acc, place=(araw[:, 0, :], araw[:, 1, :])):
                n = ua.next(s)
                dve.wait_ge(a_in[s], 16 * n + 16)
                if after is not None:
                    dve.wait_ge(a_used[after[0]], after[1])
                sums = total[:, bass.ds((a // 4) * D, D)]
                for kk in range(2):
                    r = dve.scalar_tensor_tensor(out=sums, in0=place[s][:, kk * D:(kk + 1) * D],
                                                 scalar=cT[:, bass.ds((a % 4) * 2 + (k0 + kk), 1)], in1=sums,
                                                 op0=ALU.mult, op1=ALU.add)
                    if kk == 0:
                        step(r)
                r.then_inc(a_used[s], 1)

            def project(blocks, body=None, per=0):
                with dve.Fori(0, blocks) as i:
                    us.enter(i, blocks)
                    ua.enter(i, blocks)
                    c.enter(i, per)
                    lo(0)
                    if body:
                        body(0, i)
                    lo(1)
                    if body:
                        body(1, i)
                    c.leave(blocks)
                    us.leave()
                    ua.leave()

            def after_piece(p):
                if p % 4 in (1, 3):
                    lo((0, 1)[p % 4 == 3])

            def out_units(kind, outs):
                for u in range(2, outs):
                    lo(out_slot(kind, u))
                lo(0)

            def mod_columns(k):
                r = ROW_MOD + 24 * k
                dve.wait_ge(S["mod_cols"], k + 1)
                mark(dve.tensor_tensor(shT[:, k, :], ps[:, 7, 0:8], cols[:, r:r + 8], ALU.add))
                step(dve.tensor_tensor(modc[:, :], ps[:, 7, 8:16], cols[:, r + 8:r + 16], ALU.add))
                dve.scalar_tensor_tensor(out=g1T[:, k, :], in0=modc[:, :], scalar=1.0, in1=cols[:, r + 16:r + 24],
                                         op0=ALU.add, op1=ALU.mult).then_inc(S["mods_ok"], 1)

            def gate_bias(k):
                dve.wait_ge(S["mod_gate"], k + 1)
                bw = brow2 if k == 2 else brow
                if k == 2:
                    dve.wait_ge(S["brow2_in"], 16)
                else:
                    dve.wait_ge(S["brow_in"], 16 * (k + 1 - (k > 2)))
                dve.tensor_tensor(gp[:, k % 2, :], ps[:, 4:6, :].rearrange("p a b -> p (a b)"), bw[:, 0, :], ALU.add)\
                   .then_inc(S["gate_read"], 1)

            def gate_post(k):
                bw = brow2 if k == 2 else brow
                dve.wait_ge(S["gate_read"], k + 1)
                if k < 6:
                    dve.scalar_tensor_tensor(out=gp[:, k % 2, :], in0=gp[:, k % 2, :],
                                             scalar=1.0 if k in (1, 4) else 0.5, in1=bw[:, 1, :],
                                             op0=ALU.mult, op1=ALU.mult).then_inc(S["gp_ok"], 1)
                else:
                    dve.tensor_copy(gp[:, k % 2, 0:1], gp[:, k % 2, 0:1]).then_inc(S["gp_ok"], 1)

            def mod_gate(k):
                gate_bias(k)
                gate_post(k)

            def log1p(e, u, ln, z, u_ok, ln_ok, meanwhile):
                dve.tensor_scalar(u, e, 1.0, None, ALU.add).then_inc(u_ok, 1)
                dve.wait_ge(u_ok, 1)
                step(dve.tensor_scalar(z, u, -1.0, 0.0, ALU.add, ALU.is_equal))
                dve.wait_ge(ln_ok, 1)
                step(dve.scalar_tensor_tensor(out=u, in0=u, scalar=-1.0, in1=z, op0=ALU.add, op1=ALU.add))
                step(dve.reciprocal(u, u))
                meanwhile()
                step(dve.tensor_tensor(u, u, e, ALU.mult))
                mark(dve.tensor_tensor(ln, ln, u, ALU.mult))
                step(dve.tensor_tensor(z, z, e, ALU.mult))
                step(dve.tensor_tensor(ln, ln, z, ALU.add))

            dve.wait_ge(S["cols_tr"], 1)
            dve.tensor_copy(cols[:, :], ps[:, 6, 0:ROWS]).then_inc(S["cols_ok"], 1)
            dve.wait_ge(S["wd_ps"], 1)
            dve.tensor_tensor(wdist[0:H_AT, :], ps[0:H_AT, 5, 0:REL], negr_sb[0:H_AT, :], ALU.add).then_inc(S["wd_ok"], 1)
            dve.wait_ge(S["c_ok"], 1)
            dve.wait_ge(S["zero_acc"], 1)
            last = [None]

            def ada_one(s, a, k0, **where):
                ada(s, a, k0, last[0], **where)
                last[0] = (s, ua.n[s])

            LATE = {1: 1, 2: 2, 4: 5}

            def normed_x(n):
                if n == 0:
                    dve.wait_ge(S["x_in"], 16)
                for t in range(T):
                    if t == 1 and n in (1, 2):
                        if n == 2:
                            mod_columns(2)
                        gate_bias(LATE[n])
                    dve.wait_ge(S["pre_rstd"], 2 * n + t + 1)
                    dve.tensor_scalar(xn_of(n)[:, t, :], x[:, t, :], ssx[:, n, 2 + t:3 + t], None, ALU.mult)\
                       .then_inc(S["xn_ok"], 1)

            ada_one(0, 0, 0)
            normed_x(0)
            for a in range(1, 8):
                ada_one(a % 2, a, 0)
            lo(0)
            lo(1)
            mod_columns(0)

            for n, kind in enumerate(KIND):
                if n:
                    normed_x(n)
                dve.wait_ge(S["mods_ok"], n + 1)
                for q in range(4):
                    dve.wait_ge(S["tr_ok"], 4 * n + q + 1)
                    for k in range(2 * q, 2 * q + 2):
                        r = dve.tensor_scalar(hf[:, k, :], ps[:, k // 2, (k % 2) * SEQ:(k % 2 + 1) * SEQ],
                                              g1T[:, n, k:k + 1], shT[:, n, k:k + 1], ALU.mult, ALU.add)
                    r.then_inc(S["pre_hf"], 1)
                    if q >= 2:
                        half = q - 2
                        dve.wait_ge(S["pre_hi"], 4 * n + 2 * half + 2)
                        s_ = slice(4 * half, 4 * half + 4)
                        dve.tensor_tensor(xlo[:, s_, :], hf[:, s_, :], xhi[:, s_, :].bitcast(F32), ALU.subtract)\
                           .then_inc(S["pre_lo"], 1)
                if n in (2, 5):
                    lo(1)
                if n == 4:
                    mod_columns(5)
                    gate_bias(5)
                if n in LATE:
                    gate_post(LATE[n])
                if kind == "ffn":
                    f = FFN_NO[n]
                    b = NF * f
                    k0 = 8 if n == 5 else 0
                    def gate_up(t, i, turned=True):
                        dve.wait_ge(sil_ok[t], i + 1)
                        if t == 0 and turned:
                            dve.wait_ge(S["gt_ps"], i)
                        dve.tensor_tensor(g[:, t, :], sil[:, t, :], ps[:, 4 + t, FB:2 * FB], ALU.mult)\
                           .then_inc(g_ok[t], 1)

                    if n in ADA_BEFORE:
                        for a in range(2):
                            ada_one(a, ADA_BEFORE[n] + a, k0)
                    lo(0)
                    gate_up(0, b, turned=f > 0)
                    lo(1)
                    gate_up(1, b)
                    if n:
                        dve.wait_ge(S["zero_acc"], FFN_NO[n] + 1)
                    for first, steps, per, place in ada_steps(n):
                        dve.wait_ge(a_used[last[0][0]], last[0][1])
                        with dve.Fori(0, steps) as i:
                            us.enter(i, steps)
                            ua.enter(i, steps)
                            c.enter(i, per)
                            lo(2)
                            ada(0, i * per + place, k0, (per - 1, i + ua.n[per - 1]))
                            dve.wait_ge(S["gt_hi"], i + (b + first + 1))
                            dve.tensor_tensor(xlo[:, 8:10, :], ps[:, 6, :].rearrange("p (a b) -> p a b", b=SEQ),
                                              xhi[:, 8:10, :].bitcast(F32), ALU.subtract).then_inc(S["gt_lo"], 1)
                            lo(0)
                            gate_up(0, i + (b + first + 1))
                            gate_up(1, i + (b + first + 1))
                            lo(1)
                            if per == 2:
                                ada(1, i * per + (place + 1), k0, (0, i + (ua.n[0] - steps + 1)))
                            c.leave(steps)
                            ua.leave()
                            us.leave()
                        last[0] = (per - 1, ua.n[per - 1])
                    dve.wait_ge(S["gt_hi"], b + NF)
                    dve.tensor_tensor(xlo[:, 8:10, :], ps[:, 6, :].rearrange("p (a b) -> p a b", b=SEQ),
                                      xhi[:, 8:10, :].bitcast(F32), ALU.subtract).then_inc(S["gt_lo"], 1)
                    lo(2)
                    if n == 0:
                        mod_gate(0)
                        mod_columns(1)
                    else:
                        mod_columns({2: 3, 3: 4, 5: 6}[n])
                        mod_gate({2: 3, 3: 4, 5: 6}[n])
                if kind == "ml":
                    G = lambda j: gt[0:4, j, :]
                    dve.wait_ge(S["ml_gate"], 1)
                    dve.wait_ge(S["mlc_in"], 64)
                    step(dve.tensor_scalar(G(1), ps[32:36, 7, 0:SEQ], mlb_sb[32:36, :], None, ALU.add))
                    mark(dve.tensor_scalar(G(0), ps[0:4, 7, 0:SEQ], mlb_sb[0:4, :], None, ALU.add))
                    dve.scalar_tensor_tensor(out=G(2), in0=G(1), scalar=-1.0, in1=G(1), op0=ALU.mult, op1=ALU.min)\
                       .then_inc(S["ml_na"], 1)
                    dve.wait_ge(S["ml_e"], 1)
                    log1p(G(3), G(4), G(5), G(6), S["ml_u"], S["ml_l"], lambda: lo(0))
                    step(dve.scalar_tensor_tensor(out=G(6), in0=G(1), scalar=0.0, in1=G(5), op0=ALU.min, op1=ALU.subtract))
                    step(dve.tensor_tensor_scan(G(7), ones[0:4, :], G(6), 0.0, ALU.mult, ALU.add))
                    step(dve.tensor_tensor(G(8), G(0), G(7), ALU.subtract))
                    step(dve.tensor_tensor_scan(G(4), G(8), G(8), 0.0, ALU.max, ALU.max))
                    dve.tensor_tensor(G(2), G(4), G(7), ALU.add).then_inc(S["ml_rows"], 1)
                    dve.tensor_scalar(G(1), G(4), -1.0, None, ALU.mult).then_inc(S["ml_rows"], 1)
                    lo(1)

                    dve.wait_ge(S["zero_acc2"], 1)
                    ada_one(0, 0, 0, total=acc2, place=araw2)
                    lo(0)
                    ada_one(1, 1, 0, total=acc2, place=araw2)
                    lo(1)
                    dve.wait_ge(S["ml_ct"], 1)
                    dve.tensor_copy(colm[:, :, :], ps[:, 7, 256:272].rearrange("p (a b) -> p a b", b=8))\
                       .then_inc(S["ml_cols"], 1)
                    for a in (2, 3):
                        lo(0)
                        ada_one(a % 2, a, 0, total=acc2, place=araw2)
                        lo(1)
                    dve.wait_ge(S["ml_cols"], 1)

                    def exponent(h):
                        dve.wait_ge(S["ml_nm"], h + 1)
                        e, q = E_ml[:, h, :], ps[:, h, 0:SEQ]
                        dve.scalar_tensor_tensor(out=e[:, 0:SEQ], in0=q, scalar=colm[:, 0, h:h + 1], in1=mask[:, :],
                                                 op0=ALU.add, op1=ALU.min)
                        dve.scalar_tensor_tensor(out=e[:, SEQ:384], in0=q[:, P:SEQ], scalar=colm[:, 1, h:h + 1],
                                                 in1=mask[:, 0:P], op0=ALU.add, op1=ALU.min).then_inc(S["ml_arg"], 1)

                    dve.wait_ge(S["const"], 5)
                    for h in range(H_ML):
                        exponent(h)
                    dve.wait_ge(S["ml_E"], 1)

                    def heads_out(pair):
                        dve.wait_ge(S["ml_rs"], pair + 1)
                        dve.wait_ge(S["ml_gw"], 2 * pair + 2)
                        j4 = slice(4 * pair, 4 * pair + 4)
                        step(dve.tensor_tensor(sm[:, 5, j4], sm[:, 2, j4], sm[:, 4, j4], ALU.mult))
                        for h in (2 * pair, 2 * pair + 1):
                            for t in range(T):
                                v_ = slice(h * DV, (h + 1) * DV)
                                j = 4 * pair + 2 * (h % 2) + t
                                dve.scalar_tensor_tensor(out=am[:, t, v_], in0=ps[:, 2 * t + pair, (h % 2) * DV:(h % 2 + 1) * DV],
                                                         scalar=sm[:, 5, j:j + 1], in1=og[:, t, v_],
                                                         op0=ALU.mult, op1=ALU.mult).then_inc(S["ml_am"], 1)

                    for h in range(H_ML):
                        dve.wait_ge(S["ml_sc"], h + 1)
                        dve.scalar_tensor_tensor(out=E_ml[:, h, :], in0=E_ml[:, h, :], scalar=DK ** -0.5,
                                                 in1=ps[:, 6 + h % 2, 0:384], op0=ALU.mult, op1=ALU.mult)\
                           .then_inc(S["ml_ST"], 1)
                        if h:
                            after_piece(2 * h - 1)
                        if h == 3:
                            heads_out(0)
                        dve.wait_ge(S["ml_nd"], h + 1)
                        j = slice(2 * h, 2 * h + 2)
                        dve.tensor_copy(sm[:, 0, j], ps[:, 6 + h % 2, 384:386]).then_inc(S["ml_den"], 1)
                        dve.wait_ge(S["ml_den"], h + 1)
                        step(dve.scalar_tensor_tensor(out=sm[:, 1, j], in0=sm[:, 0, j], scalar=-1.0, in1=sm[:, 0, j],
                                                      op0=ALU.mult, op1=ALU.max))
                        step(dve.tensor_tensor(sm[:, 1, j].unsqueeze(2), sm[:, 1, j].unsqueeze(2),
                                               colm[:, :, 4 + h:5 + h], ALU.max))
                        r = dve.reciprocal(sm[:, 2, j], sm[:, 1, j])
                        if h % 2:
                            r.then_inc(S["ml_r"], 1)
                        else:
                            mark(r)
                        if h < H_ML - 1:
                            ada_one(h % 2, 4 + h, 0, total=acc2, place=araw2)
                    after_piece(7)
                    heads_out(1)
                    ada_one(1, 7, 0, total=acc2, place=araw2)
                    for q in range(2):
                        dve.wait_ge(S["ml_hi"], q + 1)
                        dve.tensor_tensor(xlo[:, 4 * q:4 * q + 4, :], ps[:, 4 + 2 * q:6 + 2 * q, :].rearrange(
                            "p a (c b) -> p (a c) b", b=SEQ), xhi[:, 4 * q:4 * q + 4, :].bitcast(F32), ALU.subtract)\
                           .then_inc(S["ml_lo"], 1)
                    ada_one(0, 8, 0, total=acc2, place=araw2)
                    for u in (2, 3):
                        lo(out_slot(kind, u))
                        ada_one((u + 1) % 2, 7 + u, 0, total=acc2, place=araw2)
                    lo(0)
                    ada_one(1, 11, 0, total=acc2, place=araw2)
                if kind == "mb":
                    R = lambda j: dtt[0:H_MB, j, :]
                    dve.wait_ge(S["mb_gate"], 1)
                    dve.wait_ge(S["mbc_in"], 48)
                    step(dve.tensor_scalar(R(0), ps[0:H_MB, 7, 0:SEQ], mbv_sb[:, 0:1], None, ALU.add))
                    dve.scalar_tensor_tensor(out=R(1), in0=R(0), scalar=-1.0, in1=R(0), op0=ALU.mult, op1=ALU.min)\
                       .then_inc(S["mb_na"], 1)
                    dve.wait_ge(S["mb_e"], 1)
                    log1p(R(2), R(3), R(4), R(5), S["mb_u"], S["mb_l"], lambda: lo(0))
                    step(dve.scalar_tensor_tensor(out=R(3), in0=R(0), scalar=0.0, in1=R(4), op0=ALU.max, op1=ALU.add))
                    dve.wait_ge(S["mb_eA"], 1)
                    step(dve.tensor_scalar(R(1), R(3), sg[0:H_MB, 0, 0:1], -1.0, ALU.mult, ALU.mult))
                    dve.tensor_tensor_scan(R(5), ones[0:H_MB, :], R(1), 0.0, ALU.mult, ALU.add).then_inc(S["mb_rows"], 1)
                    lo(1)

                    def convolve(b, i, base=0):
                        i = i + base
                        """Taps 0..2 of feature tiles 2b, 2b + 1: a token's sum takes the three before it."""
                        dve.wait_ge(pj_free[b], i + (PROJ_BEFORE[4] + 1 + ONE))
                        for j in range(3):
                            sh = 3 - j
                            for q in (2 * b, 2 * b + 1):
                                r = dve.scalar_tensor_tensor(
                                    out=cacc[:, q, sh:SEQ], in0=cin[:, q, 0:SEQ - sh],
                                    scalar=cols[:, bass.ds(i * 4 + (ROW_MBW + j * CONV_F + q), 1)],
                                    in1=cacc[:, q, sh:SEQ], op0=ALU.mult, op1=ALU.add)
                                if j < 2:
                                    if q % 2:
                                        step(r)
                                    else:
                                        mark(r)
                                elif q % 2 == 0:
                                    mark(r)
                        r.then_inc(S["mb_conv"], 1)

                    convolve(0, 0)
                    convolve(1, 0)
                    project(4, lambda b, i: convolve(b, i, 1), 10)
                    dve.wait_ge(S["mb_ct"], 1)
                    mark(dve.tensor_scalar(colb[:, 0:2, :], ps[:, 7, 256:320].rearrange("p (a b) -> p a b", b=H_MB),
                                           -1.0, None, ALU.mult))
                    dve.tensor_copy(colb[:, 2:4, :], ps[:, 7, 320:384].rearrange("p (a b) -> p a b", b=H_MB))\
                       .then_inc(S["mb_cols"], 1)
                    project(1, lambda b, i: convolve(b, i, 5), 10)

                    def exponent(p):
                        dve.wait_ge(S["mb_ab"], p + 1)
                        for j in range(2):
                            h = 2 * p + j
                            e, q = E_mb[:, p % 2, j * 384:(j + 1) * 384], ps[:, 6 + p % 2, j * SEQ:(j + 1) * SEQ]
                            dve.scalar_tensor_tensor(out=e[:, 0:SEQ], in0=q, scalar=colb[:, 0, h:h + 1],
                                                     in1=mask[:, :], op0=ALU.add, op1=ALU.min)
                            r = dve.scalar_tensor_tensor(out=e[:, SEQ:384], in0=q[:, P:SEQ], scalar=colb[:, 1, h:h + 1],
                                                         in1=mask[:, 0:P], op0=ALU.add, op1=ALU.min)
                        r.then_inc(S["mb_arg"], 1)

                    def weights(p):
                        dve.wait_ge(S["mb_E"], p + 1)
                        dve.wait_ge(S["mb_cb"], p // 4 + 1)
                        if p >= 2:
                            dve.wait_ge(S["mb_y"], p - 1)
                        q = ps[:, 2 + (p // 4) % 2, :]
                        for j in range(2):
                            h = 2 * p + j
                            e, w = (v[:, p % 2, j * 384:(j + 1) * 384] for v in (E_mb, W_mb))
                            dve.scalar_tensor_tensor(out=w[:, 0:SEQ], in0=e[:, 0:SEQ], scalar=colb[:, 2, h:h + 1],
                                                     in1=q[:, 0:SEQ], op0=ALU.mult, op1=ALU.mult)
                            r = dve.scalar_tensor_tensor(out=w[:, SEQ:384], in0=e[:, SEQ:384],
                                                         scalar=colb[:, 3, h:h + 1], in1=q[:, SEQ:384],
                                                         op0=ALU.mult, op1=ALU.mult)
                        r.then_inc(S["mb_W"], 1)

                    def add_dx(gr):
                        dve.wait_ge(S["mb_y"], 4 * (gr + 1))
                        for t in range(T):
                            dve.wait_ge(S["mb_xd"], 2 * gr + t + 1)
                            dve.tensor_tensor(xd[:, t, :], ps[:, t, :], xd[:, t, :], ALU.add).then_inc(S["mb_add"], 1)

                    def times_z(gr):
                        dve.wait_ge(S["mb_zs"], gr + 1)
                        dve.wait_ge(S["mb_add"], 2 * gr + 2)
                        s_ = slice(gr * 512, (gr + 1) * 512)
                        for t in range(T):
                            dve.tensor_tensor(zs[:, t, s_], xd[:, t, :], zs[:, t, s_], ALU.mult).then_inc(S["mb_z"], 1)

                    def normed(gr):
                        dve.wait_ge(S["mb_rs"], gr + 1)
                        dve.wait_ge(S["nwm_in"], 16)
                        s_ = slice(gr * 512, (gr + 1) * 512)
                        for t in range(T):
                            dve.scalar_tensor_tensor(out=zs[:, t, s_], in0=zs[:, t, s_],
                                                     scalar=sg[:, 1, 2 * gr + t:2 * gr + t + 1], in1=nwm[:, s_],
                                                     op0=ALU.mult, op1=ALU.mult).then_inc(S["mb_yn"], 1)

                    dve.wait_ge(S["mb_cols"], 1)
                    dve.wait_ge(S["mb_xs"], GROUPS)
                    exponent(0)
                    for p in range(16):
                        gr = p // 4
                        if p + 1 < 16:
                            exponent(p + 1)
                        if p % 4 == 0 and gr:
                            add_dx(gr - 1)
                        weights(p)
                        if p:
                            after_piece(p - 1)
                        if p % 4 == 1 and gr:
                            times_z(gr - 1)
                        if p % 4 == 3 and gr:
                            normed(gr - 1)
                    add_dx(GROUPS - 1)
                    times_z(GROUPS - 1)

                    def turned_lo(gr):
                        dve.wait_ge(S["mb_hi"], gr + 1)
                        dve.tensor_tensor(xlo[:, 4 * gr:4 * gr + 4, :], ps[:, TURNED[gr]:TURNED[gr] + 2, :].rearrange(
                            "p a (c b) -> p (a c) b", b=SEQ), xhi[:, 4 * gr:4 * gr + 4, :].bitcast(F32), ALU.subtract)\
                           .then_inc(S["mb_lo"], 1)

                    turned_lo(0)
                    turned_lo(1)
                    turned_lo(2)
                    after_piece(15)
                    normed(GROUPS - 1)
                    lo(2)
                    lo(0)
                    turned_lo(3)
                    for u in range(4, 9):
                        lo(u % SLOTS if u < 8 else 0)
                if kind == "hy":
                    project(8)

                    def logits(h):
                        dve.wait_ge(S["hy_sc"], h + 1)
                        if h >= 2:
                            dve.wait_ge(S["hy_o"], h - 1)
                        L, q, st = L_at[:, h % 2, :], ps[:, 6 + h % 2, :], stat[:, h, :]
                        mark(dve.scalar_tensor_tensor(out=L[:, 0:P], in0=q[:, 0:P], scalar=DH ** -0.5,
                                                      in1=bm[:, h, P:SEQ], op0=ALU.mult, op1=ALU.add))
                        step(dve.scalar_tensor_tensor(out=L[:, P:384], in0=q[:, P:384], scalar=DH ** -0.5,
                                                      in1=bm[:, h, :], op0=ALU.mult, op1=ALU.add))
                        mark(dve.tensor_reduce(st[:, 0:1], L[:, 0:P], AX, ALU.max))
                        step(dve.tensor_reduce(st[:, 1:2], L[:, P:384], AX, ALU.max))
                        dve.tensor_scalar(st[:, 2:4], st[:, 0:2], -1.0, None, ALU.mult).then_inc(S["hy_L"], 1)

                    def weigh(h):
                        dve.wait_ge(S["hy_o"], h + 1)
                        dve.tensor_tensor(hT[:, 16 + h, :], ps[:, h % 3, 0:SEQ], hT[:, 16 + h, :],
                                          ALU.mult).then_inc(S["hy_at"], 1)

                    dve.wait_ge(S["hy_bm"], 4)
                    logits(0)
                    for h in range(H_AT):
                        if h + 1 < H_AT:
                            logits(h + 1)
                        dve.wait_ge(S["hy_P"], 2 * h + 2)
                        pr, st = P_at[:, h % 2, :], stat[:, h, :]
                        step(dve.reciprocal(st[:, 6:8], st[:, 4:6]))
                        mark(dve.tensor_scalar(pr[:, 0:P], pr[:, 0:P], st[:, 6:7], None, ALU.mult))
                        dve.tensor_scalar(pr[:, P:384], pr[:, P:384], st[:, 7:8], None, ALU.mult).then_inc(S["hy_Pn"], 1)
                        if h:
                            weigh(h - 1)
                            after_piece(2 * h - 1)
                    weigh(H_AT - 1)
                    after_piece(15)
                    dve.wait_ge(S["hy_ga"], 1)
                    dve.tensor_tensor(xlo[:, 8:16, :], hT[:, 16:24, :], xhi[:, 8:16, :].bitcast(F32), ALU.subtract)\
                       .then_inc(S["hy_alo"], 1)

                    project(4)

                    def short_conv(b, i):
                        if b == 0:
                            return
                        tile = lambda o: hT[:, bass.ds(i * 2 + o, 2), :]
                        u, y = tile(32), tile(40)
                        step(dve.tensor_tensor(u, u, y, ALU.mult))
                        for j in (2, 1, 0):
                            sh = 2 - j
                            for q in range(2):
                                w_ = cols[:, bass.ds(i * 2 + (ROW_HYW + j * 8 + q), 1)]
                                yq = hT[:, bass.ds(i * 2 + (40 + q), 1), sh:SEQ].rearrange("p a b -> p (a b)")
                                uq = hT[:, bass.ds(i * 2 + (32 + q), 1), 0:SEQ - sh].rearrange("p a b -> p (a b)")
                                if j == 2:
                                    r = dve.tensor_scalar(yq, uq, w_, None, ALU.mult)
                                else:
                                    r = dve.scalar_tensor_tensor(out=yq, in0=uq, scalar=w_, in1=yq,
                                                                 op0=ALU.mult, op1=ALU.add)
                                (step if q else mark)(r)
                        step(dve.tensor_tensor(y, y, tile(24), ALU.mult))
                        dve.tensor_tensor(y, y, tile(48), ALU.mult).then_inc(S["hy_cv"], 1)

                    project(4, short_conv, 8)
                    lo(2)
                    dve.wait_ge(S["hy_chi"], 1)
                    dve.tensor_tensor(xlo[:, 0:8, :], hT[:, 40:48, :], xhi[:, 0:8, :].bitcast(F32), ALU.subtract)\
                       .then_inc(S["hy_clo"], 1)
                    lo(3 % SLOTS)
                    lo(4 % SLOTS)
                    dve.wait_ge(w_used[3 % SLOTS], used_before_hy[0] + 20 + 2)
                    for t in range(T):
                        r = dve.tensor_tensor(mg[:, t, :], ps[:, 2 * t:2 * t + 2, :].rearrange("p a b -> p (a b)"),
                                              sgm[:, t, 0:D], ALU.mult)
                        if t == 0:
                            mark(r)
                    r.then_inc(S["hy_ya"], 1)
                    dve.wait_ge(S["hy_ya"], 1)
                    for u in range(5, 8):
                        lo(u % SLOTS)
                    for t in range(T):
                        if t == 0:
                            dve.wait_ge(S["hy_yc"], 1)
                        else:
                            dve.wait_ge(w_used[7 % SLOTS], used_before_hy[1] + 20 + 3)
                        step(dve.tensor_tensor(sgm[:, t, D:2 * D], ps[:, 4 + 2 * t:6 + 2 * t, :]
                                               .rearrange("p a b -> p (a b)"), sgm[:, t, D:2 * D], ALU.mult))
                        dve.tensor_tensor(mg[:, t, :], mg[:, t, :], sgm[:, t, D:2 * D], ALU.add).then_inc(S["hy_mg"], 1)
                    for q in range(2):
                        dve.wait_ge(S["hy_mhi"], q + 1)
                        dve.tensor_tensor(xlo[:, 8 + 4 * q:12 + 4 * q, :], ps[:, 2 * q:2 * q + 2, :].rearrange(
                            "p a (c b) -> p (a c) b", b=SEQ), xhi[:, 8 + 4 * q:12 + 4 * q, :].bitcast(F32), ALU.subtract)\
                           .then_inc(S["hy_mlo"], 1)
                    for u in range(8, 12):
                        lo(u % SLOTS)
                    yb = vh
                    for t in range(T):
                        wait_y(dve, n, t)
                        step(dve.tensor_tensor(yb[:, t, :], ps[:, 4 + 2 * t:6 + 2 * t, :].rearrange("p a b -> p (a b)"),
                                               gp[:, n % 2, :], ALU.mult))
                        dve.tensor_tensor(x[:, t, :], x[:, t, :], yb[:, t, :], ALU.add).then_inc(S["hy_fx"], 1)
                    dve.wait_ge(S["fg_in"], 16)
                    for t in range(T):
                        dve.wait_ge(S["hy_fr"], t + 1)
                        dve.scalar_tensor_tensor(out=yb[:, t, :], in0=x[:, t, :], scalar=ssx[:, n, 6 + t:7 + t],
                                                 in1=gp[:, 1, :], op0=ALU.mult, op1=ALU.mult).then_inc(S["hy_out"], 1)
                else:
                    yb = yb_of(n)
                    for t in range(T):
                        dve.wait_ge(S["post_ss"], 2 * n + t + 1)
                        dve.tensor_tensor(yb[:, t, :], ps[:, 2 * t:2 * t + 2, :].rearrange("p a b -> p (a b)"),
                                          gp[:, n % 2, :], ALU.mult).then_inc(S["yg_ok"], 1)
                        dve.wait_ge(S["yg_ok"], 2 * n + t + 1)
                        dve.wait_ge(S["post_rstd"], 2 * n + t + 1)
                        dve.scalar_tensor_tensor(out=x[:, t, :], in0=yb[:, t, :], scalar=ssx[:, n, 6 + t:7 + t],
                                                 in1=x[:, t, :], op0=ALU.mult, op1=ALU.add).then_inc(x_new[t], 1)


def _halves(w):
    k, n = w.shape
    return w.reshape(2, 4, P, n // 512, 512).transpose(3, 0, 2, 1, 4).reshape(-1, P, UNIT)


def _pairs(w):
    return w.reshape(-1, 2, P, D).transpose(0, 2, 1, 3).reshape(-1, P, UNIT)


def _ffn_units(w1, w3, w2):
    up = np.concatenate([w1.reshape(D, NF, 1, FB), w3.reshape(D, NF, 1, FB)], 2).reshape(D, NF * 512)
    up, dn = _halves(up).reshape(NF, 2, P, UNIT), _pairs(w2)
    return up, dn


def _stream(stages):
    out = [stages[0][1]]
    for j, (kind, _, rest) in enumerate(stages):
        nxt = stages[j + 1][1] if j + 1 < len(stages) else None
        if kind == "ffn":
            up, dn = rest
            out.append(up[1])
            for i in range(NF - 1):
                out.append(dn[i:i + 1])
                out.append(up[i + 2] if i + 2 < NF else nxt)
            out.append(dn[NF - 1:NF])
        else:
            out.append(rest)
            if nxt is not None:
                out.append(nxt)
    return np.concatenate(out)


def kernel(**inputs):
    import concourse.bacc as _bacc
    from concourse.bass_utils import run_bass_kernel_spmd as _run

    a = {k: np.asarray(v) for k, v in inputs.items()}
    f32 = np.float32
    stages = []
    for layer in range(2):
        ffn = [_ffn_units(a["ffn_w1"][layer, s], a["ffn_w3"][layer, s], a["ffn_w2"][layer, s]) for s in range(2)]
        if layer == 0:
            w = a["ml_w_in"][0]
            mix = np.concatenate([_halves(w[:, :3072]), _pairs(a["ml_w_out"][0])])
        else:
            w = a["mb_w_in"][0]
            mix = np.concatenate([_halves(w[:, 2048:5120]), _halves(w[:, :2048]), _pairs(a["mb_w_out"][0])])
        stages += [("ffn", ffn[0][0][0], ffn[0]), ("mix", mix[:2], mix[2:]), ("ffn", ffn[1][0][0], ffn[1])]
    w = a["w_in_2"][0]
    order = [w[:, 0:2048], w[:, 2048:3072], w[:, 3072:8192], w[:, 8192:10240]]
    hy = np.concatenate([_halves(v) for v in order] + [_pairs(a[k][0]) for k in ("w_o_attn_2", "w_o_conv_2", "w_out_2")])
    stages.append(("mix", hy[:2], hy[2:]))
    units = _stream(stages)

    def ada(w, n):
        return w.reshape(4, 2, P, 3 * n, D).transpose(3, 0, 2, 1, 4).reshape(-1, P, UNIT)

    ada_units = np.concatenate([ada(a["ada_w"][0], 3), ada(a["ada_w"][1], 3), ada(a["w_ada_2"][0], 1)])
    adab = np.concatenate([a["ada_b"].reshape(6, 3, D), a["b_ada_2"].reshape(1, 3, D)])
    pre = np.concatenate([a["norm_pre"].reshape(6, 1, D), a["norm_g_2"].reshape(1, 1, D)])
    rows = np.concatenate([
        np.concatenate([adab[:, 0:2], pre], 1).reshape(-1, P),
        a["c"].reshape(-1, P), a["c_2"].reshape(-1, P),
        a["mb_conv_w"].reshape(-1, P), a["mb_conv_b"].reshape(-1, P), a["conv_w_2"].reshape(-1, P)])
    rows = np.concatenate([rows, np.zeros((ROWS - rows.shape[0], P), f32)])
    post = np.concatenate([a["norm_post"].reshape(6, D), a["final_g_2"].reshape(1, D)])
    bcast = np.stack([adab[:, 2], post], 1).reshape(1, -1)
    mlw = np.zeros((D, 36), f32)
    mlw[:, 0:4], mlw[:, 32:36] = a["ml_w_in"][0][:, 3072:3076], a["ml_w_in"][0][:, 3076:3080]
    mlw = mlw.reshape(KT, P, 36).transpose(1, 0, 2)
    mbw = a["mb_w_in"][0][:, 5120:].reshape(KT, P, H_MB).transpose(1, 0, 2)
    dist = 255 - np.arange(REL)
    big = 16 + (np.log(np.maximum(dist, 1).astype(f32) / f32(16)) / f32(np.log(8.0)) * f32(16)).astype(np.int32)
    bucket = np.where(dist < 16, np.maximum(dist, 0), np.minimum(big, 31))
    onehot = ((bucket[None, :] == np.arange(32)[:, None]) & (dist >= 0)[None, :]).astype(f32)
    negrow = np.broadcast_to(np.where(dist >= 0, 0.0, NEG).astype(f32), (H_AT, REL))
    arrays = dict(
        x_in=a["x"].reshape(SEQ, D), units=units, ada_units=ada_units, rows=rows, bcast=bcast, mlw=mlw,
        mlb=a["ml_b_gate"].reshape(8, 1), mbw=mbw, mbv=np.stack([a["mb_dt_bias"][0], a["mb_A_log"][0]], 1),
        mbd=a["mb_D"].reshape(1, H_MB), nw_ml=a["ml_norm_w"].reshape(1, D), nw_mb=a["mb_norm_w"].reshape(1, DI),
        rel=a["rel_bias_2"], onehot=onehot, negrow=negrow)
    arrays = {k: np.ascontiguousarray(v) for k, v in arrays.items()}
    nc = _bacc.Bacc("TRN2", target_bir_lowering=False, num_devices=1)
    args = [nc.dram_tensor(k, v.shape, mybir.dt.from_np(v.dtype), kind="ExternalInput").ap() for k, v in arrays.items()]
    out = nc.dram_tensor("out", (SEQ, D), F32, kind="ExternalOutput").ap()
    build(nc, *args, out)
    r = _run(nc, [arrays], core_ids=[0])
    return r.results[0]["out"].reshape(1, SEQ, D)
```
